# Optimizing a Trainium2 kernel written in Bass

```python
import jax, jax.numpy as jnp
from jax import lax
import numpy as np

D_MODEL = 2048
BATCH = 1
SEQ = 256
DEPTH = 1

GRID_W = 64
CTX_LEN = 256
HEAD_DIM = 128
NA_HEADS = 8
RET_HEADS = 8
NA_WIDTH = NA_HEADS * HEAD_DIM
RET_WIDTH = RET_HEADS * HEAD_DIM
MIX_WIDTH = NA_WIDTH + RET_WIDTH
WIN_ROWS = 8
WIN_COLS = 16
RET_CHUNK = 128
ROPE_BASE = 10000.0
N_EXPERTS = 16
EXPERT_FF = 1024
CAPACITY_FACTOR = 2
N_MOD = 6
EPS = 1e-6
NEG_INF = -1e30
KV_COLS = 2 * NA_WIDTH + 2 * RET_WIDTH
IN_COLS = KV_COLS + NA_WIDTH + 2 * RET_WIDTH
LAT_SPLITS = (NA_WIDTH, 2 * NA_WIDTH, 2 * NA_WIDTH + RET_WIDTH, KV_COLS, KV_COLS + NA_WIDTH, KV_COLS + NA_WIDTH + RET_WIDTH)
CTX_KV_SPLITS = (NA_WIDTH, 2 * NA_WIDTH, 2 * NA_WIDTH + RET_WIDTH)
CTX_Q_SPLITS = (NA_WIDTH, NA_WIDTH + RET_WIDTH)

kernel_name = 'hybrid_natten_retention_ecmoe_dit_block'

def rms_norm(x, w):
    xf = x.astype(jnp.float32)
    y = xf * lax.rsqrt(jnp.mean(xf * xf, axis=-1, keepdims=True) + EPS)
    return (y * w.astype(jnp.float32)).astype(x.dtype)

def modulate(h, shift, scale):
    return h * (1.0 + scale) + shift

def to_heads(x):
    b, l, w = x.shape
    return x.reshape(b, l, w // HEAD_DIM, HEAD_DIM).transpose(0, 2, 1, 3)

def from_heads(x):
    b, h, l, d = x.shape
    return x.transpose(0, 2, 1, 3).reshape(b, l, h * d)

def _rotate_pairs(x, ang):
    cos, sin = jnp.cos(ang), jnp.sin(ang)
    x1, x2 = jnp.split(x, 2, axis=-1)
    return jnp.concatenate([x1 * cos - x2 * sin, x2 * cos + x1 * sin], axis=-1)

def axial_rope(x, row_pos, col_pos):
    axis_dim = HEAD_DIM // 2
    inv_freq = ROPE_BASE ** (-jnp.arange(0, axis_dim, 2, dtype=jnp.float32) / axis_dim)
    ang_r = row_pos.astype(jnp.float32)[:, None] * inv_freq
    ang_c = col_pos.astype(jnp.float32)[:, None] * inv_freq
    xf = x.astype(jnp.float32)
    out = jnp.concatenate([_rotate_pairs(xf[..., :axis_dim], ang_r), _rotate_pairs(xf[..., axis_dim:], ang_c)], axis=-1)
    return out.astype(x.dtype)

def neighbourhood_attention(q, k, v, k_ctx, v_ctx, rpb, rows):
    b, h, l, dh = q.shape
    kh = min(WIN_ROWS, rows)
    kw = WIN_COLS
    scale = dh ** -0.5
    qg = q.reshape(b, h, rows, GRID_W, dh)
    kg = k.reshape(b, h, rows, GRID_W, dh)
    vg = v.reshape(b, h, rows, GRID_W, dh)
    r = jnp.arange(rows)
    row_start = jnp.clip(r - kh // 2, 0, rows - kh)
    key_rows = row_start[:, None] + jnp.arange(kh)[None, :]
    k_blk = kg[:, :, key_rows]
    v_blk = vg[:, :, key_rows]
    cq = jnp.arange(GRID_W)
    col_start = jnp.clip(cq - kw // 2, 0, GRID_W - kw)
    col_ok = (cq[None, :] >= col_start[:, None]) & (cq[None, :] < col_start[:, None] + kw)
    row_off = key_rows - r[:, None] + (WIN_ROWS - 1)
    col_off = jnp.clip(cq[None, :] - cq[:, None], -(kw - 1), kw - 1) + (WIN_COLS - 1)
    bias = rpb[:, row_off[:, None, :, None], col_off[None, :, None, :]]
    s_win = jnp.einsum('bhrcd,bhrikd->bhrcik', qg, k_blk).astype(jnp.float32) * scale + bias[None].astype(jnp.float32)
    s_win = jnp.where(col_ok[:, None, :], s_win, NEG_INF).reshape(b, h, rows, GRID_W, kh * GRID_W)
    s_ctx = jnp.einsum('bhrcd,bhnd->bhrcn', qg, k_ctx).astype(jnp.float32) * scale
    p = jax.nn.softmax(jnp.concatenate([s_win, s_ctx], axis=-1), axis=-1)
    p_win = p[..., :kh * GRID_W].reshape(b, h, rows, GRID_W, kh, GRID_W).astype(v.dtype)
    p_ctx = p[..., kh * GRID_W:].astype(v.dtype)
    out = jnp.einsum('bhrcik,bhrikd->bhrcd', p_win, v_blk) + jnp.einsum('bhrcn,bhnd->bhrcd', p_ctx, v_ctx)
    return out.reshape(b, h, l, dh)

def context_self_attention(q, k, v):
    s = jnp.einsum('bhnd,bhmd->bhnm', q, k).astype(jnp.float32) * HEAD_DIM ** -0.5
    p = jax.nn.softmax(s, axis=-1).astype(v.dtype)
    return jnp.einsum('bhnm,bhmd->bhnd', p, v)

def retention_chunkwise(q, k, v, log_gamma, state0):
    b, h, l, d = q.shape
    n = l // RET_CHUNK
    pos = jnp.arange(RET_CHUNK, dtype=jnp.float32)
    diff = pos[:, None] - pos[None, :]
    intra = jnp.where(diff >= 0, jnp.exp(log_gamma[:, None, None] * jnp.maximum(diff, 0.0)), 0.0)
    q_decay = jnp.exp(log_gamma[:, None] * (pos + 1.0))
    k_decay = jnp.exp(log_gamma[:, None] * (RET_CHUNK - 1.0 - pos))
    chunk_decay = jnp.exp(log_gamma * RET_CHUNK)[None, :, None, None]
    qc = q.astype(jnp.float32).reshape(b, h, n, RET_CHUNK, d)
    kc = k.astype(jnp.float32).reshape(b, h, n, RET_CHUNK, d)
    vc = v.astype(jnp.float32).reshape(b, h, n, RET_CHUNK, d)
    scores = jnp.einsum('bhnid,bhnjd->bhnij', qc, kc) * intra[None, :, None]
    inner = jnp.einsum('bhnij,bhnje->bhnie', scores, vc)
    chunk_kv = jnp.einsum('bhnjd,bhnje->nbhde', kc * k_decay[None, :, None, :, None], vc)

    def step(state, kv_n):
        return state * chunk_decay + kv_n, state

    _, prev_states = lax.scan(step, state0.astype(jnp.float32), chunk_kv)
    cross = jnp.einsum('bhnid,nbhde->bhnie', qc * q_decay[None, :, None, :, None], prev_states)
    return (inner + cross).reshape(b, h, l, d)

def context_state(k, v, log_gamma, reverse):
    l = k.shape[2]
    m = jnp.arange(l, dtype=jnp.float32)
    dist = m if reverse else (l - 1.0 - m)
    w = jnp.exp(log_gamma[:, None] * dist)
    return jnp.einsum('bhmd,bhme->bhde', k.astype(jnp.float32) * w[None, :, :, None], v.astype(jnp.float32))

def bidirectional_retention(q, k, v, lg_f, lg_b, s_f, s_b):
    fwd = retention_chunkwise(q, k, v, lg_f, s_f)
    bwd = jnp.flip(retention_chunkwise(jnp.flip(q, 2), jnp.flip(k, 2), jnp.flip(v, 2), lg_b, s_b), 2)
    return fwd + bwd

def retention_output(o, g, gn_w):
    mu = jnp.mean(o, axis=-1, keepdims=True)
    var = jnp.mean(jnp.square(o - mu), axis=-1, keepdims=True)
    o = from_heads((o - mu) * lax.rsqrt(var + EPS)) * gn_w.astype(jnp.float32)
    return o.astype(g.dtype) * jax.nn.silu(g)

def expert_choice_ffn(h, w_router, w_gate, w_up, w_down):
    b, n, d = h.shape
    cap = CAPACITY_FACTOR * n // N_EXPERTS
    logits = jnp.einsum('bnd,de->ben', h, w_router).astype(jnp.float32)
    affinity = jax.nn.softmax(logits, axis=1)
    gates, idx = lax.top_k(affinity, cap)
    xe = jax.vmap(lambda hb, ib: hb[ib])(h, idx)
    hid = jax.nn.silu(jnp.einsum('becd,edf->becf', xe, w_gate)) * jnp.einsum('becd,edf->becf', xe, w_up)
    ye = jnp.einsum('becf,efd->becd', hid, w_down) * gates[..., None].astype(h.dtype)

    def combine(idx_b, y_b):
        return jnp.zeros((n, d), y_b.dtype).at[idx_b.reshape(-1)].add(y_b.reshape(-1, d))

    return jax.vmap(combine)(idx, ye)

def setup_inputs(seed: int = 0) -> dict:
    key = jax.random.key(seed)
    ks = jax.random.split(key, 24)
    f32 = jnp.float32

    def nrm(k, shape, scale):
        return jax.random.normal(k, shape, f32) * scale

    gamma0 = 1.0 - 2.0 ** (-5.0 - jnp.arange(RET_HEADS, dtype=f32))
    decay_logit = jnp.log(gamma0) - jnp.log1p(-gamma0)
    return {
        'x': nrm(ks[0], (BATCH, SEQ, D_MODEL), 1.0),
        'c': nrm(ks[1], (BATCH, D_MODEL), 1.0),
        'ctx': nrm(ks[2], (BATCH, CTX_LEN, D_MODEL), 1.0),
        'c_ctx': nrm(ks[3], (D_MODEL,), 1.0),
        'w_mod': nrm(ks[4], (DEPTH, D_MODEL, N_MOD * D_MODEL), 0.5 * D_MODEL ** -0.5),
        'b_mod': nrm(ks[5], (DEPTH, N_MOD * D_MODEL), 0.02),
        'norm_mix_w': 1.0 + nrm(ks[6], (DEPTH, D_MODEL), 0.02),
        'norm_ffn_w': 1.0 + nrm(ks[7], (DEPTH, D_MODEL), 0.02),
        'w_in': nrm(ks[8], (DEPTH, D_MODEL, IN_COLS), D_MODEL ** -0.5),
        'na_rpb': nrm(ks[9], (DEPTH, NA_HEADS, 2 * WIN_ROWS - 1, 2 * WIN_COLS - 1), 0.1),
        'ret_decay_fwd': decay_logit[None] + nrm(ks[10], (DEPTH, RET_HEADS), 0.1),
        'ret_decay_bwd': decay_logit[None] + nrm(ks[11], (DEPTH, RET_HEADS), 0.1),
        'ret_gn_w': 1.0 + nrm(ks[12], (DEPTH, RET_WIDTH), 0.02),
        'w_out': nrm(ks[13], (DEPTH, MIX_WIDTH, D_MODEL), MIX_WIDTH ** -0.5),
        'w_router': nrm(ks[14], (DEPTH, D_MODEL, N_EXPERTS), D_MODEL ** -0.5),
        'w_gate': nrm(ks[15], (DEPTH, N_EXPERTS, D_MODEL, EXPERT_FF), D_MODEL ** -0.5),
        'w_up': nrm(ks[16], (DEPTH, N_EXPERTS, D_MODEL, EXPERT_FF), D_MODEL ** -0.5),
        'w_down': nrm(ks[17], (DEPTH, N_EXPERTS, EXPERT_FF, D_MODEL), EXPERT_FF ** -0.5),
        'final_norm_w': 1.0 + nrm(ks[18], (D_MODEL,), 0.02),
    }

def reference(x, c, ctx, c_ctx, w_mod, b_mod, norm_mix_w, norm_ffn_w, w_in, na_rpb, ret_decay_fwd, ret_decay_bwd, ret_gn_w, w_out, w_router, w_gate, w_up, w_down, final_norm_w):
    seq = x.shape[1]
    rows = seq // GRID_W
    t = jnp.arange(seq)
    row_pos, col_pos = t // GRID_W, t % GRID_W
    h_lat, h_ctx = x, ctx
    for layer in range(DEPTH):
        ctx_out = layer < DEPTH - 1
        mod_lat = jnp.split((jax.nn.silu(c) @ w_mod[layer] + b_mod[layer])[:, None, :], N_MOD, axis=-1)
        mod_ctx = jnp.split(jax.nn.silu(c_ctx) @ w_mod[layer] + b_mod[layer], N_MOD, axis=-1)
        lg_f = jax.nn.log_sigmoid(ret_decay_fwd[layer].astype(jnp.float32))
        lg_b = jax.nn.log_sigmoid(ret_decay_bwd[layer].astype(jnp.float32))

        u_lat = modulate(rms_norm(h_lat, norm_mix_w[layer]), mod_lat[0], mod_lat[1])
        u_ctx = modulate(rms_norm(h_ctx, norm_mix_w[layer]), mod_ctx[0], mod_ctx[1])
        k_na, v_na, k_ret, v_ret, q_na, q_ret, g_ret = jnp.split(u_lat @ w_in[layer], LAT_SPLITS, axis=-1)
        ck_na, cv_na, ck_ret, cv_ret = [to_heads(a) for a in jnp.split(u_ctx @ w_in[layer][:, :KV_COLS], CTX_KV_SPLITS, axis=-1)]
        ck_ret = ck_ret * HEAD_DIM ** -0.5
        s_f = context_state(ck_ret, cv_ret, lg_f, reverse=False)
        s_b = context_state(ck_ret, cv_ret, lg_b, reverse=True)

        na = neighbourhood_attention(to_heads(q_na), to_heads(k_na), to_heads(v_na), ck_na, cv_na, na_rpb[layer], rows)
        q_r = axial_rope(to_heads(q_ret), row_pos, col_pos)
        k_r = axial_rope(to_heads(k_ret), row_pos, col_pos) * HEAD_DIM ** -0.5
        ret = bidirectional_retention(q_r, k_r, to_heads(v_ret), lg_f, lg_b, s_f, s_b)
        mix_lat = jnp.concatenate([from_heads(na), retention_output(ret, g_ret, ret_gn_w[layer])], axis=-1) @ w_out[layer]
        if ctx_out:
            cq_na, cq_ret, cg_ret = jnp.split(u_ctx @ w_in[layer][:, KV_COLS:], CTX_Q_SPLITS, axis=-1)
            zero_state = jnp.zeros_like(s_f)
            na_c = context_self_attention(to_heads(cq_na), ck_na, cv_na)
            ret_c = bidirectional_retention(to_heads(cq_ret), ck_ret, cv_ret, lg_f, lg_b, zero_state, zero_state)
            mix_ctx = jnp.concatenate([from_heads(na_c), retention_output(ret_c, cg_ret, ret_gn_w[layer])], axis=-1) @ w_out[layer]
            h_ctx = h_ctx + mod_ctx[2] * mix_ctx
        h_lat = h_lat + mod_lat[2] * mix_lat

        u2_lat = modulate(rms_norm(h_lat, norm_ffn_w[layer]), mod_lat[3], mod_lat[4])
        h_lat = h_lat + mod_lat[5] * expert_choice_ffn(u2_lat, w_router[layer], w_gate[layer], w_up[layer], w_down[layer])
        if ctx_out:
            u2_ctx = modulate(rms_norm(h_ctx, norm_ffn_w[layer]), mod_ctx[3], mod_ctx[4])
            h_ctx = h_ctx + mod_ctx[5] * expert_choice_ffn(u2_ctx, w_router[layer], w_gate[layer], w_up[layer], w_down[layer])
    return rms_norm(h_lat, final_norm_w)


_drawn_inputs = setup_inputs


def setup_inputs(seed=0):
    import zlib

    import numpy as np

    out = dict(_drawn_inputs(seed))
    spreads = {}
    factors = {'b_mod': 3.121,
     'norm_mix_w': 8.0,
     'norm_ffn_w': 8.0,
     'na_rpb': 25.631,
     'ret_gn_w': 8.0,
     'final_norm_w': 8.061}
    for name, (base, spread) in spreads.items():
        noise = np.random.default_rng([zlib.crc32(name.encode()), seed]).standard_normal(out[name].shape)
        drawn = base * np.exp(spread * noise) if base else spread * noise
        out[name] = __import__('jax').numpy.asarray(drawn.astype(out[name].dtype))
    for name, factor in factors.items():
        out[name] = (out[name] * factor).astype(out[name].dtype)
    return out
```

```python
from contextlib import ExitStack

import concourse.bass as bass
import numpy as np
from concourse import mybir

F32 = mybir.dt.float32
F32R = mybir.dt.float32r
BF16 = mybir.dt.bfloat16
ALU = mybir.AluOpType
ACT = mybir.ActivationFunctionType
AX_X = mybir.AxisListType.X

P = 128
D = 2048
KC = D // P
SEQ = 256
GRID_W = 64
HD = 128
NEG = -1e30
EPS = 1e-6
SCALE = HD ** -0.5
E = 16
FF = 1024
CAP = 32
FC = FF // P

COL = {"kn": 0, "vn": 1024, "kr": 2048, "vr": 3072, "qn": 4096, "qr": 5120, "gr": 6144}
BLOCKS = [(kind, g) for fam in (("kn", "qn", "vn"), ("kr", "qr", "vr", "gr")) for g in range(2) for kind in fam]
NB = len(BLOCKS)
NO = D // 512
MOD_BEFORE = 4
MOD_IN = {0: 4, 2: 5, 3: 6, 5: 7, 6: 8, 8: 9, 10: 10, 12: 11}
AHEAD = 2
CHUNKS = KC
NA_BLOCKS = {3: 0, 6: 1}
RET_BLOCKS = {9: 0, 13: 1}


def tiles_of(b):
    return 4 if b < NB and BLOCKS[b][0][0] in "kv" else 2


def bank_of(b, t):
    return t + (2 if b >= NB and (b - NB) % 2 == 0 else 0)


def stream_items():
    items = [("mod", gi, q) for gi in range(MOD_BEFORE) for q in range(8)]
    for b in range(NB + NO):
        for q in range(4):
            items.append(("w", b, q))
            if b in MOD_IN:
                items += [("mod", MOD_IN[b], 2 * q), ("mod", MOD_IN[b], 2 * q + 1)]
    return items


def host_constants():
    p = np.arange(P)[:, None].astype(np.float64)
    t = np.arange(-128, 512)[None, :]
    tb = np.arange(-384, 256)[None, :]
    tm = np.arange(-128, 256)[None, :]
    decay = np.concatenate([np.maximum(t - p, 0), np.maximum(p - tb, 0), t[:, :384] >= p, p >= tm], 1)
    ident = np.eye(P)
    freq = 10000.0 ** (-np.arange(0, 64, 2, dtype=np.float32) / np.float32(64))
    cos, sin = [], []
    for tile in range(2):
        tok = np.arange(P) + P * tile
        ar = (tok // GRID_W).astype(np.float32)[:, None] * freq.astype(np.float32)
        ac = (tok % GRID_W).astype(np.float32)[:, None] * freq.astype(np.float32)
        cos.append(np.concatenate([np.cos(ar), np.cos(ar), np.cos(ac), np.cos(ac)], 1))
        sin.append(np.concatenate([-np.sin(ar), np.sin(ar), -np.sin(ac), np.sin(ac)], 1))
    slots = np.tile(np.arange(1, CAP + 1), (P, 1))
    stack = np.tile(np.eye(CAP), (4, 1))
    sel = np.zeros((P, 2))
    sel[0::32, 0] = 1
    sel[1::32, 1] = 1
    small = np.concatenate([ident] + cos + sin + [slots, stack, sel], 1)
    cq = (np.arange(P) % GRID_W)[:, None]
    ck = np.arange(GRID_W)[None, :]
    start = np.clip(cq - 8, 0, GRID_W - 16)
    flip = np.zeros((P, P))
    flip[np.arange(P), (np.arange(P) // GRID_W) * GRID_W + GRID_W - 1 - np.arange(P) % GRID_W] = 1
    window = np.where((ck >= start) & (ck < start + 16), 0.0, NEG)
    spread = np.concatenate([np.tile(ident[:, 32 * e:32 * e + 32], (1, 4)) for e in range(4)], 1)
    late = np.concatenate([spread, np.triu(np.ones((P, P)))], 1)
    f = lambda a: np.ascontiguousarray(a.astype(np.float32))
    return {"decay": f(decay), "small": f(small), "window": f(np.concatenate([window, flip], 1)), "late": f(late)}


def build(nc, x, c, ctx, c_ctx, w_mod, b_col, b_row, nm, nf, w_in, rpb, dec_f, dec_b, gn, w_out, w_router,
          w_gate, w_up, w_down, fw, k_decay, k_small, k_window, k_late, out):
    es = ExitStack()
    base = [16512]

    def at(name, kib, shape, dt=F32):
        return nc.alloc_sbuf_tensor_at(name, [P, *shape], dt, offset=16512 + int(kib * 1024))

    ring = at("ring", 0, [8, 2048])
    xin = at("xin", 32, [4, D])
    kT = at("kT", 32, [4, 512])
    qT = at("qT", 40, [4, SEQ])
    vv = at("vv", 44, [4, 512])
    gg = at("gg", 52, [2, 512])
    pT = at("pT", 56, [2, 4, SEQ])
    junk = at("junk", 64, [D])
    uh = at("uh", 64, [KC, 512], F32R)
    mh = at("mh", 64, [KC, SEQ], F32R)
    ml = at("ml", 80, [KC, SEQ], F32R)
    xg = at("xg", 64, [KC, P])
    m5 = at("m5", 72, [D])
    xnT = at("xnT", 96, [KC, 512])
    ul = at("ul", 96, [KC, 512], F32R)
    h = at("h", 96, [2, D])
    h2n = at("h2n", 112, [2, D])
    mixT = at("mixT", 128, [KC, SEQ])
    u2T = at("u2T", 128, [KC, SEQ])
    whl = at("whl", 144, [3, 2, 512], F32R)
    gup = at("gup", 144, [4, 512])
    sgate = at("sgate", 152, [FC, CAP])
    hT = at("hT", 153, [FC, CAP])
    part = at("part", 156, [2, 512])
    affT = at("affT", 156, [4, SEQ])
    bias = at("bias", 160, [8, 6, GRID_W])
    wmask = at("wmask", 160, [2, 2, 384])
    gfb = at("gfb", 166, [2, 640])
    yy = at("yy", 160, [4, 512])
    oh = at("oh", 168, [2, 512])
    tmp = at("tmp", 172, [4, 512])
    oha = at("oha", 172, [2, 512])
    tg = at("tg", 176, [4, SEQ])
    pb = at("pb", 180, [2, 512])
    gcur = at("gcur", 180, [SEQ])
    spread = at("spread", 181, [4, P])
    tri = at("tri", 183, [P])
    ropet = at("ropet", 184, [512])
    window = at("window", 184, [GRID_W + P])
    pad = at("pad", 185, [P])
    bias_r = at("bias_r", 128, [8 * 6 * GRID_W])
    rt = at("rt", 184, [512])
    mrow = at("mrow", 186, [2, 512])
    decay = at("decay", 190, [2048])
    fwb = at("fwb", 190, [D])
    small = at("small", 198, [834])
    pos = [198 + 834 * 4 / 1024]

    def more(name, shape, dt=F32):
        n = int(np.prod(shape)) * (2 if dt == BF16 else 4)
        t_ = at(name, pos[0], shape, dt)
        pos[0] += -(-n // 32) * 32 / 1024
        return t_

    pos[0] = -(-int(pos[0] * 1024) // 32) * 32 / 1024
    csT = more("csT", [KC, 32])
    wr = more("wr", [KC, E])
    ones = more("ones", [P])
    tri_b = more("tri_b", [P], BF16)
    ones_b = more("ones_b", [P], BF16)
    modc = more("modc", [4, KC, 2])
    nmc = more("nmc", [KC])
    nfc = more("nfc", [KC])
    gnc = more("gnc", [8])
    bcol = more("bcol", [4, KC])
    cin = more("cin", [2, KC])
    dec = more("dec", [2, 8])
    lg = more("lg", [4, 16])
    acol = more("acol", [2, KC])
    a2 = more("a2", [KC])
    ss = more("ss", [8])
    rs = more("rs", [8])
    mhalf = more("mhalf", [8])
    nmax = more("nmax", [4])
    psumm = more("psumm", [4])
    prec = more("prec", [4])
    bst = more("bst", [8, 6])
    mv = more("mv", [8, 2])
    rg = more("rg", [8])
    assert pos[0] * 1024 + 16512 <= 229368
    ident = small[:, 0:128]
    cosT = small[:, 128:384].rearrange("p (t d) -> p t d", t=2)
    sinT = small[:, 384:640].rearrange("p (t d) -> p t d", t=2)
    slots = small[:, 640:672]
    stack = small[:, 672:704]
    sel = small[:, 704:706]
    aff = rt[:, 0:32].rearrange("p (t e) -> p t e", t=2)
    rmax, rsum = rt[:, 32:34], rt[:, 34:36]
    gts = rt[:, 36:68].rearrange("p (t e) -> p t e", t=2)
    sels = rt[:, 68:100].rearrange("p (t e) -> p t e", t=2)
    slotm = rt[:, 100:132].rearrange("p (t e) -> p t e", t=2)
    top8 = rt[:, 132:164]
    eq_b = rt[:, 164:180].bitcast(BF16).rearrange("p (t e) -> p t e", t=2)
    gt_b = rt[:, 180:196].bitcast(BF16).rearrange("p (t e) -> p t e", t=2)
    sel_b = rt[:, 196:212].bitcast(BF16).rearrange("p (t e) -> p t e", t=2)
    lrow = rt[0:16, 256:512]

    bank = [es.enter_context(nc.psum_tensor(f"bank{i}", [P, 512], F32)) for i in range(8)]
    pad_dram = nc.dram_tensor("rpb_padded", (120, 128), F32, kind="Internal").ap()

    def sem(name):
        return es.enter_context(nc.semaphore(name))

    small_in = sem("small_in")
    late_in = sem("late_in")
    fw_in = sem("fw_in")
    pad_in = sem("pad_in")
    pad_out = sem("pad_out")
    bias_in = sem("bias_in")
    tok_in = [sem(f"tok_in{t}") for t in range(4)]
    ring_full = [sem(f"ring_full{i}") for i in range(8)]
    h_in = sem("h_in")
    out_done = sem("out_done")
    act_link, dve_link, pool_link = sem("act_link"), sem("dve_link"), sem("pool_link")
    squares, mean_sq, rstd_ok, normed = sem("squares"), sem("mean_sq"), sem("rstd_ok"), sem("normed")
    x_turned, xt_act, xt_dve = sem("x_turned"), sem("xt_act"), sem("xt_dve")
    pool_init, c_act = sem("pool_init"), sem("c_act")
    mod_item_used, part_act, part_dve = sem("mod_item_used"), sem("part_act"), sem("part_dve")
    mod_mac = sem("mod_mac")
    mod_small, mod_add, a_ready = sem("mod_small"), sem("mod_add"), sem("a_ready")
    lg_act, lg_dve = sem("lg_act"), sem("lg_dve")
    bias_pe, bias_ok = sem("bias_pe"), sem("bias_ok")
    u_aff, uh_ok, ul_ok = sem("u_aff"), sem("uh_ok"), sem("ul_ok")
    hi_split, lo_split, chunk_used, tile_done = sem("hi_split"), sem("lo_split"), sem("chunk_used"), sem("tile_done")
    ev_act, ev_dve, roped = sem("ev_act"), sem("ev_dve"), sem("roped")
    kq_turned, kq_act, kq_dve = sem("kq_turned"), sem("kq_act"), sem("kq_dve")
    na_score, na_biased, na_exp, na_norm = sem("na_score"), sem("na_biased"), sem("na_exp"), sem("na_norm")
    na_turned, na_pt, na_out, na_mix = sem("na_turned"), sem("na_pt"), sem("na_out"), sem("na_mix")
    powers, masks = sem("powers"), sem("masks")
    ret_score, ret_masked, ret_out, ret_kept = sem("ret_score"), sem("ret_masked"), sem("ret_out"), sem("ret_kept")
    gate_act, ret_var, ret_rstd, ret_gated = sem("gate_act"), sem("ret_var"), sem("ret_rstd"), sem("ret_gated")
    ret_turned, ret_mix_a, ret_mix_d = sem("ret_turned"), sem("ret_mix_a"), sem("ret_mix_d")
    mh_ok, ml_ok = sem("mh_ok"), sem("ml_ok")
    row_bc, row_act, h_ready, h_sq = sem("row_bc"), sem("row_act"), sem("h_ready"), sem("h_sq")
    h2_act, h2_dve, h2_turned, u2_act, u2_dve = sem("h2_act"), sem("h2_dve"), sem("h2_turned"), sem("u2_act"), sem("u2_dve")
    r_pe, r_dve, r_act = sem("r_pe"), sem("r_dve"), sem("r_act")
    moe_used, gathered, xg_act, xg_dve = sem("moe_used"), sem("gathered"), sem("xg_act"), sem("xg_dve")
    gu_act, gu_dve, summed, silu_ok, hid_ok = sem("gu_act"), sem("gu_dve"), sem("summed"), sem("silu_ok"), sem("hid_ok")
    g_pe, g_ok, y_ok, comb, comb_add = sem("g_pe"), sem("g_ok"), sem("y_ok"), sem("comb"), sem("comb_add")
    f_sq_a, f_sq_d, f_mean, f_rstd, f_out = sem("f_sq_a"), sem("f_sq_d"), sem("f_mean"), sem("f_rstd"), sem("f_out")

    items = stream_items()
    n_items = len(items)
    item_at = {it: n for n, it in enumerate(items)}
    fills = [16 * sum(1 for n in range(n_items) if n % 4 == s) for s in range(4)] + [0] * 4
    mod_order = list(range(MOD_BEFORE)) + [MOD_IN[b] for b in sorted(MOD_IN)]

    def wait_item(eng, item):
        n = item_at[item]
        eng.wait_ge(ring_full[n % 4], 16 * (n // 4 + 1))

    n_even = [sum((tiles_of(i) + 1) // 2 for i in range(b)) for b in range(NB + 1)]

    def wait_evacuated(eng, b, t):
        if b >= NB:
            eng.wait_ge(h_ready, 2 * (b - NB) + t + 1)
        else:
            eng.wait_ge(ev_dve if t % 2 else ev_act, n_even[b] + t // 2 + 1)

    last_user = {}
    before = {}
    for b in range(NB + NO):
        for t in range(tiles_of(b)):
            before[b, t] = last_user.get(bank_of(b, t))
            last_user[bank_of(b, t)] = (b, t)
    n_tile = [sum(tiles_of(i) - 1 for i in range(b)) for b in range(NB + NO + 1)]

    def wait_projected(eng, b, t):
        if t == tiles_of(b) - 1:
            eng.wait_ge(chunk_used, CHUNKS * (b + 1))
        else:
            eng.wait_ge(tile_done, n_tile[b] + t + 1)

    kq_blocks = [b for b in range(NB) if BLOCKS[b][0][0] in "kq"]
    n_kq = {b: sum(tiles_of(i) for i in kq_blocks if i < b) for b in kq_blocks}
    n_kk = {b: sum(tiles_of(i) for i in kq_blocks if i < b and BLOCKS[i][0][0] == "k") for b in kq_blocks}
    n_qq = {b: n_kq[b] - n_kk[b] for b in kq_blocks}
    n_rope = {b: 2 * sum(1 for i in kq_blocks if i < b and BLOCKS[i][0][1] == "r") for b in kq_blocks}

    def wait_turned_read(eng, m):
        for b in kq_blocks:
            if n_kq[b] <= m < n_kq[b] + tiles_of(b):
                if BLOCKS[b][0][0] == "k":
                    eng.wait_ge(kq_dve, n_kk[b] + m - n_kq[b] + 1)
                else:
                    eng.wait_ge(kq_act, n_qq[b] + m - n_kq[b] + 1)

    def moe_slot(m8):
        return (m8 + 4) % 8

    wg_v = w_gate[0].rearrange("e (j k p) f -> e j p k f", p=P, k=2)
    wu_v = w_up[0].rearrange("e (j k p) f -> e j p k f", p=P, k=2)
    wd_v = w_down[0].rearrange("e (j p) d -> e j p d", p=P)
    win_v = w_in[0].rearrange("(k p) n -> p k n", p=P)
    wout_v = w_out[0].rearrange("(k p) n -> p k n", p=P)
    wmod_v = w_mod[0].rearrange("(k p) n -> p k n", p=P)
    x_v = x[0].rearrange("(t p) d -> t p d", p=P)
    ctx_v = ctx[0].rearrange("(t p) d -> t p d", p=P)
    out_v = out[0].rearrange("(t p) d -> t p d", p=P)

    block = es.enter_context(nc.Block())

    @block.sync
    def _(sp):
        for n, (kind, b, q) in enumerate(items):
            if n >= 4:
                k0, b0, q0 = items[n - 4]
                if k0 == "mod" and b0 < MOD_BEFORE:
                    sp.wait_ge(mod_item_used, 8 * b0 + q0 + 1)
                elif k0 == "mod":
                    sp.wait_ge(mod_mac, KC * (b0 - MOD_BEFORE) + 2 * q0 + 2)
                else:
                    sp.wait_ge(lo_split, CHUNKS * b0 + 4 * q0 + 4)
            if kind == "mod":
                dst = ring[:, n % 4, :].rearrange("p (k c) -> p k c", k=2)
                src = wmod_v[:, 2 * q:2 * q + 2, 1024 * b:1024 * b + 1024]
            else:
                dst = ring[:, n % 4, :].rearrange("p (k c) -> p k c", k=4)
                if b < NB:
                    c0 = COL[BLOCKS[b][0]] + 512 * BLOCKS[b][1]
                    src = win_v[:, 4 * q:4 * q + 4, c0:c0 + 512]
                else:
                    src = wout_v[:, 4 * q:4 * q + 4, 512 * (b - NB):512 * (b - NB) + 512]
            sp.dma_start(dst, src).then_inc(ring_full[n % 4], 16)

        def expert_item(e, what, j, s):
            if what == "down":
                sp.dma_start(ring[:, s, :], wd_v[e, j]).then_inc(ring_full[s], 16)
            else:
                src = (wg_v if what == "gate" else wu_v)[e, j]
                sp.dma_start(ring[:, s, :].rearrange("p (k c) -> p k c", k=2), src).then_inc(ring_full[s], 16)

        for j in range(8):
            if j == 0:
                sp.wait_ge(ret_out, 8)
                sp.wait_ge(ret_gated, 2)
            if j >= 4:
                n = max(i for i in range(n_items) if i % 4 == moe_slot(j))
                _, b0, q0 = items[n]
                sp.wait_ge(lo_split, CHUNKS * b0 + 4 * q0 + 4)
            expert_item(0, "gate", j, moe_slot(j))
        with sp.Fori(0, E - 1) as e:
            for m, (what, de) in enumerate((("up", 0), ("down", 0), ("gate", 1))):
                for j in range(8):
                    sp.wait_ge(moe_used, e * 24 + (8 * m + j + 1))
                    ee = e + de
                    s = moe_slot(j)
                    if what == "down":
                        src = wd_v[bass.ds(ee, 1), j].rearrange("a p d -> (a p) d")
                        sp.dma_start(ring[:, s, :], src).then_inc(ring_full[s], 16)
                    else:
                        src = (wg_v if what == "gate" else wu_v)[bass.ds(ee, 1), j].rearrange("a p k f -> (a p) k f")
                        dst = ring[:, s, :].rearrange("p (k c) -> p k c", k=2)
                        sp.dma_start(dst, src).then_inc(ring_full[s], 16)
        for m, what in enumerate(("up", "down")):
            for j in range(8):
                sp.wait_ge(moe_used, 24 * (E - 1) + 8 * m + j + 1)
                expert_item(E - 1, what, j, moe_slot(j))
        for t in range(2):
            sp.wait_ge(f_out, 2 * t + 2)
            sp.dma_start(out_v[t], h[:, t, :]).then_inc(out_done, 16)
        sp.wait_ge(out_done, 32)
        sp.wait_ge(pad_out, 16)

    @block.tensor
    def _(pe):
        mm = nc.tensor.matmul

        def mod_group(i):
            gi = mod_order[i]
            if i:
                pe.wait_ge(part_act, i)
                pe.wait_ge(part_dve, i)
            for q in range(8):
                wait_item(pe, ("mod", gi, q))
                n = item_at["mod", gi, q]
                w = ring[:, n % 4, :].rearrange("p (k c) -> p k c", k=2)
                for half in range(2):
                    for kk in range(2):
                        k = 2 * q + kk
                        quad = 2 * ((q + half) % 2) + kk
                        last = mm(bank[4 + half][32 * quad:32 * quad + 32, :], csT[:, k, :],
                                  w[:, kk, 512 * half:512 * half + 512], start=q < 2, stop=q >= 6)
                last.then_inc(mod_item_used, 1)

        def mod_sums(i):
            gi = mod_order[i]
            if i < MOD_BEFORE:
                pe.wait_ge(part_act, i + 1)
                pe.wait_ge(part_dve, i + 1)
                col = sel
            else:
                pe.wait_ge(mod_mac, KC * (i - MOD_BEFORE + 1))
                col = ones[:, 0:2]
            if i:
                pe.wait_ge(mod_add, i)
            for half in range(2):
                if gi // 2 in (2, 5):
                    quad = 2 * (gi % 2) + half
                    last = mm(bank[7][32 * quad:32 * quad + 1, :], col[:, 0:1], part[:, half, :], start=True, stop=True)
                else:
                    for j in range(4):
                        i2 = 4 * half + j
                        last = mm(bank[7][:, 2 * i2:2 * i2 + 2], part[:, half, P * j:P * j + P], col,
                                  start=True, stop=True)
            last.then_inc(mod_small, 1)

        def project(b, k):
            cidx = CHUNKS * b + k
            if b == 0:
                pe.wait_ge(ul_ok, k + 1)
            if b == NB:
                pe.wait_ge(ml_ok, k + 1)
            pe.wait_ge(lo_split, cidx + 1)
            wh, wl = whl[:, cidx % (AHEAD + 1), 0, :], whl[:, cidx % (AHEAD + 1), 1, :]
            hi, lo = (uh, ul) if b < NB else (mh, ml)
            for t in range(tiles_of(b)):
                if k == 0 and before[b, t]:
                    wait_evacuated(pe, *before[b, t])
                ps = bank[bank_of(b, t)][:, :]
                cols = slice(P * t, P * t + P)
                mm(ps, hi[:, k, cols], wh, start=k == 0, stop=False)
                mm(ps, hi[:, k, cols], wl, start=False, stop=False)
                last = mm(ps, lo[:, k, cols], wh, start=False, stop=k == KC - 1)
                if t == tiles_of(b) - 1:
                    last.then_inc(chunk_used, 1)
                elif k == KC - 1:
                    last.then_inc(tile_done, 1)

        def turn_tile(b, t):
            m = n_kq[b] + t
            wait_evacuated(pe, b, t)
            if BLOCKS[b][0][1] == "r" and t < 2:
                pe.wait_ge(roped, n_rope[b] + t + 1)
            if m >= 2:
                wait_turned_read(pe, m - 2)
            if b in MOD_IN:
                pe.wait_ge(mod_add, mod_order.index(MOD_IN[b]) + 1)
            for hh in range(4):
                last = nc.tensor.transpose(bank[6 + m % 2][:, P * hh:P * hh + P], tmp[:, t, P * hh:P * hh + P], ident)
            last.then_inc(kq_turned, 1)

        def na_scores(g, u):
            n = 8 * g + u
            if u == 0:
                pe.wait_ge(kq_dve, n_kk[3 * g] + 4)
                pe.wait_ge(kq_act, n_qq[3 * g + 1] + 2)
            if n >= 2:
                pe.wait_ge(na_biased, n - 1)
            hh, qt = u // 2, u % 2
            mm(bank[4 + u % 2][:, :], qT[:, hh, P * qt:P * qt + P], kT[:, hh, :], start=True, stop=True).then_inc(na_score, 1)

        def na_turn(g, u):
            n = 8 * g + u
            pe.wait_ge(na_norm, n + 1)
            if n >= 1:
                pe.wait_ge(na_pt, n)
            for kt in range(4):
                last = nc.tensor.transpose(bank[6][:, P * kt:P * kt + P], pb[:, u % 2, P * kt:P * kt + P], ident)
            last.then_inc(na_turned, 1)

        def na_values(g, u):
            hn = 4 * g + u // 2
            pe.wait_ge(na_pt, 8 * g + u + 1)
            if u == 1:
                wait_evacuated(pe, 3 * g + 2, 2)
                wait_evacuated(pe, 3 * g + 2, 3)
            if hn:
                pe.wait_ge(na_mix, hn)
            for kt in range(4):
                last = mm(bank[7][:, 0:SEQ], vv[:, kt, P * (u // 2):P * (u // 2) + P], pT[:, (u // 2) % 2, kt, :],
                          start=kt == 0, stop=kt == 3)
            last.then_inc(na_out, 1)

        def ret_scores(g, hh):
            n = 4 * g + hh
            if hh == 0:
                pe.wait_ge(kq_dve, n_kk[6 + 4 * g] + 4)
                pe.wait_ge(kq_act, n_qq[7 + 4 * g] + 2)
            if n:
                pe.wait_ge(ret_masked, n)
            for kt in range(4):
                last = mm(bank[4 + kt // 2][:, SEQ * (kt % 2):SEQ * (kt % 2) + SEQ], kT[:, hh, P * kt:P * kt + P],
                          qT[:, hh, :], start=True, stop=True)
            last.then_inc(ret_score, 1)

        def ret_values(g, hh):
            n = 4 * g + hh
            pe.wait_ge(ret_masked, n + 1)
            if hh == 0:
                wait_evacuated(pe, 8 + 4 * g, 2)
                wait_evacuated(pe, 8 + 4 * g, 3)
            if n >= 2:
                pe.wait_ge(ret_kept, n - 1)
            for it in range(2):
                for kt in range(4):
                    last = mm(bank[6 + hh % 2][:, P * it:P * it + P], pT[:, hh % 2, kt, P * it:P * it + P],
                              vv[:, kt, P * hh:P * hh + P], start=kt == 0, stop=kt == 3)
            last.then_inc(ret_out, 1)

        def ret_turn(g):
            pe.wait_ge(ret_gated, g + 1)
            for hh in range(4):
                for it in range(2):
                    last = nc.tensor.transpose(bank[6 + hh // 2][:, SEQ * (hh % 2) + P * it:SEQ * (hh % 2) + P * it + P],
                                               pb[:, it, P * hh:P * hh + P], ident)
            last.then_inc(ret_turned, 1)

        def row_on_all(m, quad, dst):
            return mm(dst, ones[32 * quad:32 * quad + 1, :], mrow[32 * quad:32 * quad + 1, m, :], start=True, stop=True)

        pe.wait_ge(small_in, 16 * 14)
        for t in range(4):
            pe.wait_ge(normed, t + 1)
        for k in range(KC):
            if k >= 4:
                pe.wait_ge(xt_dve if k % 2 else xt_act, k // 2 - 1)
            for t in range(4):
                last = nc.tensor.transpose(bank[k % 4][:, P * t:P * t + P], xin[:, t, P * k:P * k + P], ident)
            last.then_inc(x_turned, 1)
        pe.wait_ge(bias_in, 16 * 16)
        for j in range(6):
            if j >= 2:
                pe.wait_ge(bias_ok, j - 1)
            mm(bank[6 + j % 2][:, :], window[:, GRID_W:], bias_r[:, 512 * j:512 * j + 512], start=True, stop=True).then_inc(bias_pe, 1)
        pe.wait_ge(bias_ok, 6)
        pe.wait_ge(c_act, 2)
        pe.wait_ge(pool_init, 3)
        for i in range(MOD_BEFORE):
            mod_group(i)
            mod_sums(i)
        pe.wait_ge(xt_act, 8)
        pe.wait_ge(xt_dve, 8)

        for b in range(NB + NO):
            for k in range(KC):
                project(b, k)
                prev = b - 1
                if prev in MOD_IN and k == 0:
                    if prev in NA_BLOCKS:
                        pe.wait_ge(na_mix, 4 * NA_BLOCKS[prev] + 4)
                    mod_sums(mod_order.index(MOD_IN[prev]))
                if prev in kq_blocks and 4 <= k < 4 + tiles_of(prev):
                    turn_tile(prev, k - 4)
                if b in NA_BLOCKS:
                    g = NA_BLOCKS[b]
                    if 4 <= k < 12:
                        na_scores(g, k - 4)
                    if 6 <= k < 14:
                        na_turn(g, k - 6)
                    if 7 <= k < 15 and k % 2 == 0:
                        na_values(g, k - 7)
                if b in RET_BLOCKS:
                    g = RET_BLOCKS[b]
                    if k in (4, 7, 10, 13):
                        ret_scores(g, (k - 4) // 3)
                    if k in (6, 9, 12, 15):
                        ret_values(g, (k - 6) // 3)
                if prev in RET_BLOCKS and k == 4:
                    ret_turn(RET_BLOCKS[prev])
                if b >= NB and k == 8:
                    cb = b - NB
                    if cb >= 2:
                        pe.wait_ge(row_act, cb - 1)
                    row_on_all(0, cb, bank[4 + cb % 2][:, :]).then_inc(row_bc, 1)

        pe.wait_ge(row_act, 4)
        for cb in range(4):
            last = row_on_all(1, cb, bank[4 + cb][:, :])
        last.then_inc(row_bc, 1)
        pe.wait_ge(h2_act, 1)
        pe.wait_ge(h2_dve, 1)
        pe.wait_ge(h_ready, 8)
        for j in range(8):
            if j >= 4:
                pe.wait_ge(u2_act, j - 3)
                pe.wait_ge(u2_dve, j - 3)
            for kk in range(2):
                for t in range(2):
                    k = 2 * j + kk
                    last = nc.tensor.transpose(bank[j % 4][:, SEQ * kk + P * t:SEQ * kk + P * t + P], h2n[:, t, P * k:P * k + P], ident)
            last.then_inc(h2_turned, 1)
        pe.wait_ge(row_act, 5)
        for k in range(KC):
            pe.wait_ge(u2_dve if k % 2 else u2_act, k // 2 + 1)
            last = mm(bank[4][0:E, 0:SEQ], wr[:, k, :], u2T[:, k, :], start=k == 0, stop=k == KC - 1)
        last.then_inc(r_pe, 1)
        pe.wait_ge(r_dve, 1)
        for t in range(2):
            last = nc.tensor.transpose(bank[5][:, E * t:E * t + E], lrow[:, P * t:P * t + P], ident[0:16, 0:16])
        last.then_inc(r_pe, 1)
        pe.wait_ge(r_dve, 3)
        for t in range(2):
            last = nc.tensor.transpose(bank[6][0:E, P * t:P * t + P], aff[:, t, :], ident)
        last.then_inc(r_pe, 1)
        pe.wait_ge(r_dve, 4)
        for i in range(2):
            for t in range(2):
                last = nc.tensor.transpose(bank[7][:, E * (2 * i + t):E * (2 * i + t) + E],
                                           affT[0:16, 1 + i, P * t:P * t + P], ident[0:16, 0:16])
        last.then_inc(r_pe, 1)
        pe.wait_ge(r_dve, 5)
        pe.wait_ge(late_in, 32)
        for t in range(2):
            srcs = [(ones_b, eq_b[:, 0, :])] * (t == 1) + [(tri_b, eq_b[:, t, :]), (ones_b, gt_b[:, 0, :]), (ones_b, gt_b[:, 1, :])]
            for i, (l, r) in enumerate(srcs):
                last = mm(bank[4][:, E * t:E * t + E], l[:, :], r, start=i == 0, stop=i == len(srcs) - 1)
        last.then_inc(r_pe, 1)
        pe.wait_ge(r_dve, 6)
        for t in range(2):
            srcs = [(ones_b, sel_b[:, 0, :])] * (t == 1) + [(tri_b, sel_b[:, t, :])]
            for i, (l, r) in enumerate(srcs):
                last = mm(bank[5][:, E * t:E * t + E], l[:, :], r, start=i == 0, stop=i == len(srcs) - 1)
        last.then_inc(r_pe, 1)
        pe.wait_ge(r_dve, 7)
        for g in range(4):
            for t in range(2):
                last = nc.tensor.transpose(bank[6 + g // 2][:, SEQ * (g % 2) + P * t:SEQ * (g % 2) + P * t + P],
                                           oha[:, t, P * g:P * g + P], ident)
        last.then_inc(r_pe, 1)
        pe.wait_ge(r_act, 2)
        pe.wait_ge(r_dve, 8)

        pe.sem_inc(summed, 1)
        pe.sem_inc(comb, 1)
        with pe.Fori(0, 4) as g:
            for j in range(4):
                if j == 0:
                    pe.wait_ge(y_ok, g * 16 + 1)
                for k in range(4 * j, 4 * j + 4):
                    for t in range(2):
                        last = mm(bank[j][:, P * (k % 4):P * (k % 4) + P], h2n[:, t, P * k:P * k + P],
                                  oh[:, t, bass.ds(g * P, P)], start=t == 0, stop=t == 1)
                last.then_inc(gathered, 1)
            pe.wait_ge(xg_act, g * 8 + 8)
            pe.wait_ge(xg_dve, g * 8 + 8)
            for ei in range(4):
                pe.wait_ge(y_ok, g * 16 + (4 * ei + 1))
                for m in range(2):
                    for j in range(8):
                        s = moe_slot(j)
                        pe.wait_ge(ring_full[s], g * (16 * 12) + (fills[s] + 16 * (3 * ei + m + 1)))
                        w = ring[:, s, :].rearrange("p (k c) -> p k c", k=2)
                        for half in range(2):
                            for kk in range(2):
                                quad = 2 * ((j + half) % 2) + kk
                                last = mm(bank[2 * m + half][32 * quad:32 * quad + 32, :],
                                          xg[:, 2 * j + kk, CAP * ei:CAP * ei + CAP],
                                          w[:, kk, 512 * half:512 * half + 512], start=j < 2, stop=j >= 6)
                        last.then_inc(moe_used, 1)
                pe.wait_ge(g_ok, g * 4 + (ei + 1))
                mm(bank[5][:, 0:SEQ], spread[:, ei, :], tg[:, bass.ds(g, 1), :].rearrange("p a n -> p (a n)"),
                   start=True, stop=True).then_inc(g_pe, 1)
                pe.wait_ge(gu_act, g * 8 + (2 * ei + 2))
                pe.wait_ge(gu_dve, g * 8 + (2 * ei + 2))
                pe.wait_ge(hid_ok, g * 4 + (ei + 1))
                for i in range(16):
                    last = mm(bank[4][:, CAP * i:CAP * i + CAP], gup[:, i // 4, P * (i % 4):P * (i % 4) + P], stack,
                              start=True, stop=True)
                last.then_inc(summed, 1)
                pe.wait_ge(hid_ok, g * 4 + (ei + 2))
                for j in range(8):
                    s = moe_slot(j)
                    pe.wait_ge(ring_full[s], g * (16 * 12) + (fills[s] + 16 * (3 * ei + 3)))
                    for cb in range(4):
                        quad = (j + cb) % 4
                        last = mm(bank[cb][32 * quad:32 * quad + 32, :], hT[:, j, :], ring[:, s, 512 * cb:512 * cb + 512],
                                  start=j < 4, stop=j >= 4)
                    last.then_inc(moe_used, 1)
                pe.wait_ge(g_ok, g * 4 + (ei + 2))
                for cb in range(4):
                    pe.wait_ge(y_ok, g * 16 + (4 * ei + cb + 2))
                    for t in range(2):
                        i = 2 * cb + t
                        if i >= 2:
                            pe.wait_ge(comb_add, g * 32 + (8 * ei + i))
                        else:
                            pe.wait_ge(comb_add, g * 32 + (8 * ei + 1))
                        mm(bank[6 + i % 2][:, :], gcur[:, P * t:P * t + P], yy[:, cb, :], start=True, stop=True).then_inc(comb, 1)

    @block.scalar
    def _(act):
        a = nc.scalar.activation
        links = [0]

        def link(ins):
            links[0] += 1
            ins.then_inc(act_link, 1)
            act.wait_ge(act_link, links[0])

        loads = [(small[:, 0:706], k_small), (cin[:, 0, :], c), (cin[:, 1, :], c_ctx), (nmc[:, :], nm), (nfc[:, :], nf),
                 (gnc[:, :], gn), (bcol[:, :, :], b_col), (dec[:, 0, :], dec_f.partition_broadcast(P)),
                 (dec[:, 1, :], dec_b.partition_broadcast(P)), (decay[:, :], k_decay), (window[:, :], k_window),
                 (wr[:, :, :], w_router[0].rearrange("(k p) e -> p k e", p=P))]
        for t in range(4):
            act.dma_start(xin[:, t, :], (x_v if t < 2 else ctx_v)[t % 2]).then_inc(tok_in[t], 16)
        for dst, src in loads:
            act.dma_start(dst, src).then_inc(small_in, 16)
        for m in range(2):
            act.dma_start(mrow[0:P:32, m, :], b_row[m]).then_inc(small_in, 16)
        act.wait_ge(pool_init, 1)
        act.dma_start(pad[0:120, 48:79], rpb[0].rearrange("h r c -> (h r) c")).then_inc(pad_in, 16)
        for t in range(4):
            act.wait_ge(tok_in[t], 16)
            a(junk[:, :], xin[:, t, :], ACT.Square, accum_out=ss[:, t:t + 1]).then_inc(squares, 1)
            act.wait_ge(squares, t + 1)
        act.wait_ge(pad_in, 16)
        act.dma_start(pad_dram, pad[0:120, :]).then_inc(pad_out, 16)
        act.wait_ge(pool_init, 2)
        act.wait_ge(small_in, 16 * 14)
        for i in range(2):
            a(csT[:, :, i], cin[:, i, :], ACT.Silu).then_inc(c_act, 1)
        act.wait_ge(pad_out, 16)
        for half in range(2):
            for hh in range(8):
                src = bass.AP(pad_dram.tensor, pad_dram.offset + (15 * hh + 5 - half) * P,
                              [[1, GRID_W], [P, 6], [1, GRID_W]])
                dst = bias_r[64 * half:64 * half + 64, 384 * hh:384 * hh + 384].rearrange("p (s c) -> p s c", s=6)
                act.dma_start(dst, src).then_inc(bias_in, 16)
        act.wait_ge(lg_dve, 1)
        link(a(lg[:, 1, :], lg[:, 0, :], ACT.Exp, scale=-1.0))
        a(lg[:, 2, :], lg[:, 1, :], ACT.Ln, bias=1.0).then_inc(lg_act, 1)
        for k in range(0, KC, 2):
            act.wait_ge(x_turned, k + 1)
            a(xnT[:, k, :], bank[k % 4][:, :], ACT.Copy).then_inc(xt_act, 1)

        def mod_part(i):
            act.wait_ge(mod_item_used, 8 * i + 8)
            if i:
                act.wait_ge(mod_small, i)
            a(part[:, 0, :], bank[4][:, :], ACT.Copy).then_inc(part_act, 1)

        for i in range(MOD_BEFORE):
            mod_part(i)

        def split(b, k):
            cidx = CHUNKS * b + k
            if k % 4 == 0:
                wait_item(act, ("w", b, k // 4))
            if cidx > AHEAD:
                act.wait_ge(chunk_used, cidx - AHEAD)
            n = item_at["w", b, k // 4]
            a(whl[:, cidx % (AHEAD + 1), 0, :], ring[:, n % 4, 512 * (k % 4):512 * (k % 4) + 512], ACT.Copy).then_inc(hi_split, 1)

        def evacuate(b):
            kind = BLOCKS[b][0][0]
            for t in range(0, tiles_of(b), 2):
                wait_projected(act, b, t)
                if kind in "kq":
                    dst = tmp[:, t, :]
                    i = kq_blocks.index(b)
                    if i:
                        act.wait_ge(kq_turned, n_kq[b])
                else:
                    dst = (vv if kind == "v" else gg)[:, t, :]
                    if kind == "g" and BLOCKS[b][1]:
                        act.wait_ge(ret_gated, 1)
                    if kind == "v" and b == 5:
                        act.wait_ge(na_out, 4)
                    if kind == "v" and b == 8:
                        act.wait_ge(na_out, 8)
                    if kind == "v" and b == 12:
                        act.wait_ge(ret_out, 4)
                a(dst, bank[bank_of(b, t)][:, :], ACT.Copy).then_inc(ev_act, 1)

        def query_tile(b, t):
            act.wait_ge(kq_turned, n_kq[b] + t + 1)
            src = bank[6 + (n_kq[b] + t) % 2][:, :].rearrange("p (h n) -> p h n", h=4)
            a(qT[:, :, P * t:P * t + P], src, ACT.Copy, scale=SCALE).then_inc(kq_act, 1)

        def na_exponent(g, u):
            n = 8 * g + u
            act.wait_ge(na_biased, n + 1)
            a(pb[:, u % 2, :], pb[:, u % 2, :], ACT.Exp, bias=nmax[:, n % 4:n % 4 + 1],
              accum_out=psumm[:, n % 4:n % 4 + 1]).then_inc(na_exp, 1)

        def na_keep(g, u):
            act.wait_ge(na_turned, 8 * g + u + 1)
            src = bank[6][:, :].rearrange("p (k n) -> p k n", k=4)
            a(pT[:, (u // 2) % 2, :, P * (u % 2):P * (u % 2) + P], src, ACT.Copy).then_inc(na_pt, 1)

        def na_mixed(g, u):
            hn = 4 * g + u // 2
            act.wait_ge(na_out, hn + 1)
            a(mixT[:, hn, :], bank[7][:, 0:SEQ], ACT.Copy).then_inc(na_mix, 1)

        def gamma_powers(n):
            if n:
                act.wait_ge(masks, n)
            else:
                act.wait_ge(lg_dve, 2)
            for i in range(2):
                a(gfb[:, i, :], decay[:, 640 * i:640 * i + 640], ACT.Exp,
                  scale=lg[:, 3, 8 * i + n:8 * i + n + 1]).then_inc(powers, 1)

        def ret_keep(g, hh):
            n = 4 * g + hh
            act.wait_ge(ret_out, n + 1)
            if hh == 0 and g:
                act.wait_ge(ret_turned, 1)
            src = bank[6 + hh % 2][:, 0:SEQ].rearrange("p (t e) -> p t e", t=2)
            a(pb[:, :, P * hh:P * hh + P], src, ACT.Copy).then_inc(ret_kept, 1)

        def ret_mixed(g, half):
            act.wait_ge(ret_turned, g + 1)
            hn = 8 + 4 * g + 2 * half
            a(mixT[:, hn, :], bank[6 + half][:, 0:SEQ], ACT.Copy, scale=gnc[:, hn - 8:hn - 7]).then_inc(ret_mix_a, 1)

        def ahead(cidx):
            b, k = divmod(cidx, KC)
            split(b, k)
            if b == 0:
                act.wait_ge(u_aff, k + 1)
                a(uh[:, k, :], xnT[:, k, :], ACT.Copy).then_inc(uh_ok, 1)
            if b == NB:
                if k == 0:
                    act.wait_ge(chunk_used, CHUNKS * NB)
                    for t in range(2):
                        act.dma_start(h[:, t, :], x_v[t]).then_inc(h_in, 16)
                    act.wait_ge(na_mix, 8)
                if k == 8:
                    act.wait_ge(ret_mix_a, 2)
                    act.wait_ge(ret_mix_d, 2)
                if k == 12:
                    act.wait_ge(ret_mix_a, 4)
                    act.wait_ge(ret_mix_d, 4)
                a(mh[:, k, :], mixT[:, k, :], ACT.Copy).then_inc(mh_ok, 1)

        for cidx in range(AHEAD):
            ahead(cidx)
        for b in range(NB + NO):
            prev = b - 1
            for k in range(KC):
                if k == 0 and 0 <= prev < NB:
                    evacuate(prev)
                if CHUNKS * b + k + AHEAD < CHUNKS * (NB + NO):
                    ahead(CHUNKS * b + k + AHEAD)
                if prev in kq_blocks and BLOCKS[prev][0][0] == "q" and 4 <= k < 6:
                    query_tile(prev, k - 4)
                if b in NA_BLOCKS:
                    g = NA_BLOCKS[b]
                    if 4 <= k < 12:
                        na_exponent(g, k - 4)
                    if 6 <= k < 14:
                        na_keep(g, k - 6)
                    if 7 <= k < 15 and k % 2 == 0:
                        na_mixed(g, k - 7)
                if b in RET_BLOCKS:
                    g = RET_BLOCKS[b]
                    if k in (2, 5, 8, 11):
                        gamma_powers(4 * g + (k - 2) // 3)
                    if k in (6, 9, 12, 15):
                        ret_keep(g, (k - 6) // 3)
                if prev in RET_BLOCKS and k == 2:
                    act.wait_ge(ev_dve, n_even[prev] + 1)
                    act.wait_ge(ev_act, n_even[prev] + 1)
                    a(gg[:, :, :], gg[:, :, :], ACT.Silu).then_inc(gate_act, 1)
                if prev in RET_BLOCKS and k == 5:
                    ret_mixed(RET_BLOCKS[prev], 0)
                    ret_mixed(RET_BLOCKS[prev], 1)
                if b >= NB and k == 9:
                    cb = b - NB
                    act.wait_ge(row_bc, cb + 1)
                    if cb >= 2:
                        act.wait_ge(h_ready, 2 * (cb - 1))
                    a(part[:, cb % 2, :], bank[4 + cb % 2][:, :], ACT.Copy).then_inc(row_act, 1)
                if b > NB and k in (3, 4):
                    cb, t = b - 1 - NB, k - 3
                    act.wait_ge(h_ready, 2 * cb + t + 1)
                    a(tmp[:, t, :], h[:, t, 512 * cb:512 * cb + 512], ACT.Square,
                      accum_out=ss[:, 4 * t + cb:4 * t + cb + 1]).then_inc(h_sq, 1)
        for t in range(2):
            act.wait_ge(h_ready, 2 * NO - 1 + t)
            a(tmp[:, t, :], h[:, t, 1536:2048], ACT.Square, accum_out=ss[:, 4 * t + 3:4 * t + 4]).then_inc(h_sq, 1)
        act.wait_ge(row_bc, 5)
        act.wait_ge(chunk_used, CHUNKS * (NB + NO))
        for cb in range(4):
            last = a(m5[:, 512 * cb:512 * cb + 512], bank[4 + cb][:, :], ACT.Copy)
        last.then_inc(row_act, 1)
        act.wait_ge(rstd_ok, 2)
        a(h2n[:, 0, :], h[:, 0, :], ACT.Copy, scale=rs[:, 0:1]).then_inc(h2_act, 1)
        act.dma_start(spread[:, :, :], k_late[:, 0:512].rearrange("p (e m) -> p e m", e=4)).then_inc(late_in, 16)
        act.dma_start(tri[:, :], k_late[:, 512:640]).then_inc(late_in, 16)
        act.dma_start(fwb[:, :], fw.partition_broadcast(P)).then_inc(fw_in, 16)
        act.wait_ge(a_ready, 2)
        for j in range(8):
            act.wait_ge(h2_turned, j + 1)
            k = 2 * j
            a(u2T[:, k, :], bank[j % 4][:, 0:SEQ], ACT.Identity, scale=a2[:, k:k + 1],
              bias=modc[:, 2, k, 0:1]).then_inc(u2_act, 1)
        act.wait_ge(r_dve, 2)
        a(aff[:, :, :], aff[:, :, :], ACT.Exp).then_inc(r_act, 1)
        act.wait_ge(r_pe, 7)
        a(tg[:, 0:2, :], bank[6][:, :].rearrange("p (g n) -> p g n", g=2), ACT.Copy).then_inc(r_act, 1)

        with act.Fori(0, 4) as g:
            for j in range(4):
                act.wait_ge(gathered, g * 4 + (j + 1))
                for k in (4 * j, 4 * j + 2):
                    a(xg[:, k, :], bank[j][:, P * (k % 4):P * (k % 4) + P], ACT.Identity, scale=a2[:, k:k + 1],
                      bias=modc[:, 2, k, 0:1]).then_inc(xg_act, 1)
            for ei in range(4):
                for m in range(2):
                    act.wait_ge(moe_used, g * 96 + (24 * ei + 8 * m + 8))
                    if m == 0:
                        act.wait_ge(summed, g * 4 + (ei + 1))
                    a(gup[:, 2 * m, :], bank[2 * m][:, :], ACT.Copy).then_inc(gu_act, 1)
                act.wait_ge(summed, g * 4 + (ei + 2))
                act.wait_ge(hid_ok, g * 4 + (ei + 1))
                a(sgate[:, :, :], bank[4][:, 0:SEQ].rearrange("p (f n) -> p f n", f=FC), ACT.Silu).then_inc(silu_ok, 1)
        act.wait_ge(comb_add, E * 8 + 1)
        a(ring[:, 0, :], h[:, 0, :], ACT.Square, accum_out=ss[:, 0:1]).then_inc(f_sq_a, 1)

    @block.vector
    def _(dve):
        v = nc.vector
        links = [0]

        def link(ins):
            links[0] += 1
            ins.then_inc(dve_link, 1)
            dve.wait_ge(dve_link, links[0])

        for t in range(4):
            dve.wait_ge(squares, t + 1)
        v.tensor_scalar(rs[:, 4:8], ss[:, 0:4], 1.0 / D, EPS, ALU.mult, ALU.add).then_inc(mean_sq, 1)
        dve.wait_ge(rstd_ok, 1)
        for t in range(4):
            v.tensor_scalar(xin[:, t, :], xin[:, t, :], rs[:, t:t + 1], None, ALU.mult).then_inc(normed, 1)
        dve.wait_ge(small_in, 16 * 14)
        decs = dec[:, :, :].rearrange("p a b -> p (a b)")
        link(v.tensor_scalar(lg[:, 3, :], decs, -1.0, None, ALU.mult))
        v.tensor_tensor(lg[:, 0, :], lg[:, 3, :], decs, ALU.max).then_inc(lg_dve, 1)
        dve.wait_ge(lg_act, 1)
        link(v.tensor_scalar(lg[:, 0, :], decs, 0.0, None, ALU.min))
        v.tensor_tensor(lg[:, 3, :], lg[:, 0, :], lg[:, 2, :], ALU.subtract).then_inc(lg_dve, 1)
        for k in range(1, KC, 2):
            dve.wait_ge(x_turned, k + 1)
            v.tensor_copy(xnT[:, k, :], bank[k % 4][:, :]).then_inc(xt_dve, 1)

        bv = bias[:, :, :, :].rearrange("p h s c -> p (h s) c")
        for j in range(6):
            dve.wait_ge(bias_pe, j + 1)
            v.tensor_tensor(bv[:, 8 * j:8 * j + 8, :], bank[6 + j % 2][:, :].rearrange("p (s c) -> p s c", s=8),
                            window[:, 0:GRID_W].unsqueeze(1).broadcast_to([P, 8, GRID_W]), ALU.add).then_inc(bias_ok, 1)

        def mod_part(i):
            dve.wait_ge(mod_item_used, 8 * i + 8)
            if i:
                dve.wait_ge(mod_small, i)
            v.tensor_copy(part[:, 1, :], bank[5][:, :]).then_inc(part_dve, 1)

        def mod_finish(i):
            gi = mod_order[i]
            dve.wait_ge(mod_small, i + 1)
            m = gi // 2
            if m in (2, 5):
                for half in range(2):
                    r = 32 * (2 * (gi % 2) + half)
                    last = v.tensor_tensor(mrow[r:r + 1, m // 3, :], mrow[r:r + 1, m // 3, :], bank[7][r:r + 1, :], ALU.add)
                last.then_inc(mod_add, 1)
            else:
                mi = {0: 0, 1: 1, 3: 2, 4: 3}[m]
                k0 = 8 * (gi % 2)
                v.tensor_tensor(modc[:, mi, k0:k0 + 8, :], bank[7][:, 0:16].rearrange("p (k c) -> p k c", c=2),
                                bcol[:, mi, k0:k0 + 8].unsqueeze(2).broadcast_to([P, 8, 2]), ALU.add).then_inc(mod_add, 1)

        def mod_multiply(i, k):
            gi = mod_order[i]
            if k == 0:
                dve.wait_ge(mod_small, i)
            if k % 2 == 0:
                wait_item(dve, ("mod", gi, k // 2))
            n = item_at["mod", gi, k // 2]
            w = ring[:, n % 4, 1024 * (k % 2):1024 * (k % 2) + 1024]
            acc = part[:, :, :].rearrange("p a n -> p (a n)")
            if k == 0:
                ins = v.tensor_scalar(acc, w, csT[:, k, 0:1], None, ALU.mult)
            else:
                dve.wait_ge(mod_mac, KC * (i - MOD_BEFORE) + k)
                ins = v.scalar_tensor_tensor(out=acc, in0=w, scalar=csT[:, k, 0:1], in1=acc, op0=ALU.mult, op1=ALU.add)
            ins.then_inc(mod_mac, 1)

        for i in range(MOD_BEFORE):
            mod_part(i)
            mod_finish(i)
        dve.wait_ge(mod_add, MOD_BEFORE)
        for i in range(2):
            last = v.scalar_tensor_tensor(out=acol[:, i, :], in0=modc[:, 1, :, i], scalar=1.0, in1=nmc[:, :],
                                          op0=ALU.add, op1=ALU.mult)
        last.then_inc(a_ready, 1)
        dve.wait_ge(a_ready, 1)
        dve.wait_ge(xt_act, 8)
        dve.wait_ge(xt_dve, 8)

        def split(b, k):
            cidx = CHUNKS * b + k
            n = item_at["w", b, k // 4]
            dve.wait_ge(hi_split, cidx + 1)
            v.tensor_tensor(whl[:, cidx % (AHEAD + 1), 1, :], ring[:, n % 4, 512 * (k % 4):512 * (k % 4) + 512],
                            whl[:, cidx % (AHEAD + 1), 0, :].bitcast(F32), ALU.subtract).then_inc(lo_split, 1)

        def evacuate(b):
            kind = BLOCKS[b][0][0]
            for t in range(1, tiles_of(b), 2):
                wait_projected(dve, b, t)
                if kind in "kq":
                    dst = tmp[:, t, :]
                    if kq_blocks.index(b):
                        dve.wait_ge(kq_turned, n_kq[b])
                else:
                    dst = (vv if kind == "v" else gg)[:, t, :]
                    if kind == "v" and b == 5:
                        dve.wait_ge(na_out, 4)
                    if kind == "v" and b == 8:
                        dve.wait_ge(na_out, 8)
                    if kind == "v" and b == 12:
                        dve.wait_ge(ret_out, 4)
                v.tensor_copy(dst, bank[bank_of(b, t)][:, :]).then_inc(ev_dve, 1)

        def key_tile(b, t):
            dve.wait_ge(kq_turned, n_kq[b] + t + 1)
            src = bank[6 + (n_kq[b] + t) % 2][:, :].rearrange("p (h n) -> p h n", h=4)
            v.tensor_copy(kT[:, :, P * t:P * t + P], src).then_inc(kq_dve, 1)

        def na_bias(g, u):
            n = 8 * g + u
            hn, qt = 4 * g + u // 2, u % 2
            if n == 0:
                dve.wait_ge(bias_ok, 6)
            dve.wait_ge(na_score, n + 1)
            if n >= 2:
                dve.wait_ge(na_turned, n - 1)
            s = 2 * (1 - qt)
            v.tensor_tensor(pb[:, u % 2, 0:SEQ], bank[4 + u % 2][:, 0:SEQ],
                            bias[:, hn, s:s + 4, :].rearrange("p a b -> p (a b)"), ALU.add)
            link(v.tensor_copy(pb[:, u % 2, SEQ:512], bank[4 + u % 2][:, SEQ:512]))
            link(v.tensor_reduce(prec[:, n % 4:n % 4 + 1], pb[:, u % 2, :], AX_X, ALU.max))
            v.tensor_scalar(nmax[:, n % 4:n % 4 + 1], prec[:, n % 4:n % 4 + 1], -1.0, None, ALU.mult).then_inc(na_biased, 1)

        def na_normal(g, u):
            n = 8 * g + u
            dve.wait_ge(na_exp, n + 1)
            link(v.reciprocal(prec[:, n % 4:n % 4 + 1], psumm[:, n % 4:n % 4 + 1]))
            v.tensor_scalar(pb[:, u % 2, :], pb[:, u % 2, :], prec[:, n % 4:n % 4 + 1], None, ALU.mult).then_inc(na_norm, 1)

        def ret_mask(g, hh):
            n = 4 * g + hh
            dve.wait_ge(ret_score, n + 1)
            dve.wait_ge(masks, n + 1)
            if n >= 2:
                dve.wait_ge(ret_out, n - 1)
            for kt in range(4):
                o = P * (1 - kt % 2)
                last = v.tensor_tensor(pT[:, hh % 2, kt, :], bank[4 + kt // 2][:, SEQ * (kt % 2):SEQ * (kt % 2) + SEQ],
                                       wmask[:, hh % 2, kt // 2, o:o + SEQ], ALU.mult)
            last.then_inc(ret_masked, 1)

        def ret_normal(g):
            for hh in range(4):
                for it in range(2):
                    last = v.bn_stats(bst[:, 2 * hh + it, :], pb[:, it, P * hh:P * hh + P])
            link(last)
            for i in range(8):
                last = v.bn_aggr(mv[:, i, :], bst[:, i, :])
            link(last)
            v.tensor_scalar(rg[:, :], mv[:, :, 1], EPS, None, ALU.add).then_inc(ret_var, 1)
            dve.wait_ge(ret_rstd, g + 1)
            for hh in range(4):
                for it in range(2):
                    i = 2 * hh + it
                    last = v.tensor_scalar(pb[:, it, P * hh:P * hh + P], pb[:, it, P * hh:P * hh + P], mv[:, i, 0:1],
                                           rg[:, i:i + 1], ALU.subtract, ALU.mult)
            link(last)
            dve.wait_ge(gate_act, g + 1)
            v.tensor_tensor(pb[:, :, :], pb[:, :, :], gg[:, :, :], ALU.mult).then_inc(ret_gated, 1)

        def ret_mixed(g, half):
            dve.wait_ge(ret_turned, g + 1)
            dve.wait_ge(ret_mix_a, 2 * g + half + 1)
            hn = 9 + 4 * g + 2 * half
            v.tensor_scalar(mixT[:, hn, :], bank[6 + half][:, SEQ:512], gnc[:, hn - 8:hn - 7], None, ALU.mult).then_inc(ret_mix_d, 1)

        def residual(cb):
            b = NB + cb
            dve.wait_ge(row_act, cb + 1)
            if cb == 0:
                dve.wait_ge(h_in, 32)
            for t in range(2):
                wait_projected(dve, b, t)
                link(v.tensor_tensor(tmp[:, 2 + t, :], bank[bank_of(b, t)][:, :], part[:, cb % 2, :], ALU.mult))
                v.tensor_tensor(h[:, t, 512 * cb:512 * cb + 512], h[:, t, 512 * cb:512 * cb + 512], tmp[:, 2 + t, :],
                                ALU.add).then_inc(h_ready, 1)

        def ahead(cidx):
            b, k = divmod(cidx, KC)
            if b == 0:
                for i in range(2):
                    last = v.tensor_scalar(xnT[:, k, SEQ * i:SEQ * i + SEQ], xnT[:, k, SEQ * i:SEQ * i + SEQ],
                                           acol[:, i, k:k + 1], modc[:, 0, k, i:i + 1], ALU.mult, ALU.add)
                last.then_inc(u_aff, 1)
            split(b, k)
            if b == 0:
                dve.wait_ge(uh_ok, k + 1)
                v.tensor_tensor(ul[:, k, :], xnT[:, k, :], uh[:, k, :].bitcast(F32), ALU.subtract).then_inc(ul_ok, 1)
            if b == NB:
                dve.wait_ge(mh_ok, k + 1)
                v.tensor_tensor(ml[:, k, :], mixT[:, k, :], mh[:, k, :].bitcast(F32), ALU.subtract).then_inc(ml_ok, 1)

        for cidx in range(AHEAD):
            ahead(cidx)
        for b in range(NB + NO):
            prev = b - 1
            for k in range(KC):
                if k == 0 and 0 <= prev < NB:
                    evacuate(prev)
                if CHUNKS * b + k + AHEAD < CHUNKS * (NB + NO):
                    ahead(CHUNKS * b + k + AHEAD)
                if k == 2 and prev >= NB:
                    residual(prev - NB)
                if k == 1 and prev in MOD_IN:
                    mod_finish(mod_order.index(MOD_IN[prev]))
                if b in MOD_IN:
                    mod_multiply(mod_order.index(MOD_IN[b]), k)
                if prev in kq_blocks and BLOCKS[prev][0][0] == "k" and 4 <= k < 8:
                    key_tile(prev, k - 4)
                if b in NA_BLOCKS:
                    g = NA_BLOCKS[b]
                    if 4 <= k < 12:
                        na_bias(g, k - 4)
                    if 5 <= k < 13:
                        na_normal(g, k - 5)
                if b in RET_BLOCKS:
                    g = RET_BLOCKS[b]
                    if k in (5, 8, 11, 14):
                        ret_mask(g, (k - 5) // 3)
                if prev in RET_BLOCKS and k == 3:
                    dve.wait_ge(ret_kept, 4 * RET_BLOCKS[prev] + 4)
                    ret_normal(RET_BLOCKS[prev])
                if prev in RET_BLOCKS and k == 5:
                    ret_mixed(RET_BLOCKS[prev], 0)
                    ret_mixed(RET_BLOCKS[prev], 1)
        residual(NO - 1)
        link(v.scalar_tensor_tensor(out=a2[:, :], in0=modc[:, 3, :, 0], scalar=1.0, in1=nfc[:, :], op0=ALU.add, op1=ALU.mult))
        dve.wait_ge(h_sq, 2 * NO)
        link(v.tensor_reduce(rs[:, 2:4], ss[:, :].rearrange("p (t c) -> p t c", t=2), AX_X, ALU.add))
        v.tensor_scalar(rs[:, 4:6], rs[:, 2:4], 1.0 / D, EPS, ALU.mult, ALU.add).then_inc(mean_sq, 1)
        dve.wait_ge(rstd_ok, 2)
        v.tensor_scalar(h2n[:, 1, :], h[:, 1, :], rs[:, 1:2], None, ALU.mult).then_inc(h2_dve, 1)
        v.memset(ones_b[:, :], 1.0).then_inc(a_ready, 1)
        for j in range(8):
            dve.wait_ge(h2_turned, j + 1)
            dve.wait_ge(u2_act, j + 1)
            k = 2 * j + 1
            v.tensor_scalar(u2T[:, k, :], bank[j % 4][:, SEQ:512], a2[:, k:k + 1], modc[:, 2, k, 0:1],
                            ALU.mult, ALU.add).then_inc(u2_dve, 1)
        dve.wait_ge(late_in, 32)
        v.tensor_copy(tri_b[:, :], tri[:, :])
        dve.wait_ge(r_pe, 1)
        v.tensor_copy(lrow, bank[4][0:E, 0:SEQ]).then_inc(r_dve, 1)
        dve.wait_ge(r_pe, 2)
        lt = bank[5][:, 0:2 * E].rearrange("p (t e) -> p t e", t=2)
        link(v.tensor_reduce(rmax, lt, AX_X, ALU.max))
        v.tensor_tensor(aff[:, :, :], lt, rmax.unsqueeze(2).broadcast_to([P, 2, E]), ALU.subtract).then_inc(r_dve, 1)
        dve.wait_ge(r_act, 1)
        link(v.tensor_reduce(rsum, aff[:, :, :], AX_X, ALU.add))
        link(v.reciprocal(rmax, rsum))
        v.tensor_tensor(aff[:, :, :], aff[:, :, :], rmax.unsqueeze(2).broadcast_to([P, 2, E]), ALU.mult).then_inc(r_dve, 1)
        dve.wait_ge(r_pe, 3)
        v.tensor_copy(affT[0:E, 0, :], bank[6][0:E, 0:SEQ])
        link(v.tensor_copy(affT[0:E, 3, :], bank[6][0:E, 0:SEQ]))
        for i in range(4):
            link(v.max(top8[0:E, 8 * i:8 * i + 8], affT[0:E, 3, :]))
            if i < 3:
                link(v.match_replace(affT[0:E, 3, :], top8[0:E, 8 * i:8 * i + 8], affT[0:E, 3, :], -1.0))
        v.tensor_scalar(affT[0:E, 1, :], affT[0:E, 0, :], top8[0:E, 31:32], None, ALU.is_gt)
        v.tensor_scalar(affT[0:E, 2, :], affT[0:E, 0, :], top8[0:E, 31:32], None, ALU.is_equal).then_inc(r_dve, 1)
        dve.wait_ge(r_pe, 4)
        gts_ps = bank[7][:, 0:4 * E].rearrange("p (i t e) -> p i t e", i=2, t=2)
        v.tensor_copy(gt_b, gts_ps[:, 0])
        v.tensor_copy(gts, gts_ps[:, 0])
        v.tensor_copy(slotm, gts_ps[:, 1])
        v.tensor_copy(eq_b, gts_ps[:, 1]).then_inc(r_dve, 1)
        dve.wait_ge(r_dve, 5)
        dve.wait_ge(r_pe, 5)
        ps_t = bank[4][:, 0:2 * E].rearrange("p (t e) -> p t e", t=2)
        link(v.tensor_scalar(sels, ps_t, float(CAP), None, ALU.is_le))
        link(v.tensor_tensor(sels, sels, slotm, ALU.mult))
        link(v.tensor_tensor(sels, sels, gts, ALU.add))
        v.tensor_copy(sel_b, sels).then_inc(r_dve, 1)
        dve.wait_ge(r_pe, 6)
        ps_s = bank[5][:, 0:2 * E].rearrange("p (t e) -> p t e", t=2)
        link(v.tensor_tensor(slotm, ps_s, sels, ALU.mult))
        for t in range(2):
            last = v.tensor_tensor(oh[:, t, :].rearrange("p (e s) -> p e s", e=E),
                                   slotm[:, t, :].unsqueeze(2).broadcast_to([P, E, CAP]),
                                   slots.unsqueeze(1).broadcast_to([P, E, CAP]), ALU.is_equal)
        link(last)
        for t in range(2):
            last = v.tensor_tensor(oha[:, t, :].rearrange("p (e s) -> p e s", e=E),
                                   oh[:, t, :].rearrange("p (e s) -> p e s", e=E),
                                   aff[:, t, :].unsqueeze(2).broadcast_to([P, E, CAP]), ALU.mult)
        last.then_inc(r_dve, 1)
        dve.wait_ge(r_pe, 7)
        v.tensor_copy(tg[:, 2:4, :], bank[7][:, :].rearrange("p (g n) -> p g n", g=2)).then_inc(r_dve, 1)

        for credit in (y_ok, g_ok, hid_ok, comb_add):
            dve.sem_inc(credit, 1)
        with dve.Fori(0, 4) as g:
            for j in range(4):
                dve.wait_ge(gathered, g * 4 + (j + 1))
                dve.wait_ge(xg_act, g * 8 + (2 * j + 2))
                for k in (4 * j + 1, 4 * j + 3):
                    v.tensor_scalar(xg[:, k, :], bank[j][:, P * (k % 4):P * (k % 4) + P], a2[:, k:k + 1],
                                    modc[:, 2, k, 0:1], ALU.mult, ALU.add).then_inc(xg_dve, 1)
            for ei in range(4):
                for m in range(2):
                    dve.wait_ge(moe_used, g * 96 + (24 * ei + 8 * m + 8))
                    if m == 0:
                        dve.wait_ge(summed, g * 4 + (ei + 1))
                    v.tensor_copy(gup[:, 2 * m + 1, :], bank[2 * m + 1][:, :]).then_inc(gu_dve, 1)
                dve.wait_ge(g_pe, g * 4 + (ei + 1))
                dve.wait_ge(comb, g * 32 + (8 * ei + 1))
                v.tensor_copy(gcur[:, :], bank[5][:, 0:SEQ]).then_inc(g_ok, 1)
                dve.wait_ge(silu_ok, g * 4 + (ei + 1))
                v.tensor_tensor(hT[:, :, :], sgate[:, :, :], bank[4][:, SEQ:512].rearrange("p (f n) -> p f n", f=FC),
                                ALU.mult).then_inc(hid_ok, 1)
                dve.wait_ge(moe_used, g * 96 + (24 * ei + 24))
                for cb in range(4):
                    v.tensor_tensor(yy[:, cb, :], bank[cb][:, :], m5[:, 512 * cb:512 * cb + 512], ALU.mult).then_inc(y_ok, 1)
                for cb in range(4):
                    for t in range(2):
                        i = 2 * cb + t
                        dve.wait_ge(comb, g * 32 + (8 * ei + i + 2))
                        hs = h[:, t, 512 * cb:512 * cb + 512]
                        v.tensor_tensor(hs, hs, bank[6 + i % 2][:, :], ALU.add).then_inc(comb_add, 1)
        dve.wait_ge(comb_add, E * 8 + 1)
        v.tensor_tensor_reduce(ring[:, 1, :], h[:, 1, :], h[:, 1, :], 1.0, 0.0, ALU.mult, ALU.add, ss[:, 1:2]).then_inc(f_sq_d, 1)
        dve.wait_ge(f_sq_d, 1)
        dve.wait_ge(f_sq_a, 1)
        v.tensor_scalar(rs[:, 4:6], ss[:, 0:2], 1.0 / D, EPS, ALU.mult, ALU.add).then_inc(f_mean, 1)
        dve.wait_ge(f_rstd, 1)
        dve.wait_ge(fw_in, 16)
        for t in range(2):
            for half in range(2):
                cs = slice(1024 * half, 1024 * half + 1024)
                v.scalar_tensor_tensor(out=h[:, t, cs], in0=h[:, t, cs], scalar=rs[:, t:t + 1], in1=fwb[:, cs],
                                       op0=ALU.mult, op1=ALU.mult).then_inc(f_out, 1)

    @block.gpsimd
    def _(pool):
        gp = nc.gpsimd
        links = [0]

        def link(ins):
            links[0] += 1
            ins.then_inc(pool_link, 1)
            pool.wait_ge(pool_link, links[0])

        gp.memset(pad[:, :], 0.0).then_inc(pool_init, 1)
        gp.memset(csT[:, :, :], 0.0).then_inc(pool_init, 1)
        gp.memset(ones[:, :], 1.0).then_inc(pool_init, 1)
        link(gp.memset(mhalf[:, :], -0.5))
        pool.wait_ge(mean_sq, 1)
        gp.tensor_tensor(rs[:, 0:4], rs[:, 4:8], mhalf[:, 0:4], ALU.pow).then_inc(rstd_ok, 1)

        def rope(b, t):
            wait_evacuated(pool, b, t)
            if n_rope[b] + t:
                pool.wait_ge(roped, n_rope[b] + t)
            tv = tmp[:, t, :].rearrange("p (h a f e) -> p h a f e", h=4, a=2, f=2)
            rv = ropet[:, :].rearrange("p (h a f e) -> p h a f e", h=4, a=2, f=2)
            sv = sinT[:, t, :].rearrange("p (a f e) -> p a f e", a=2, f=2)
            for f in range(2):
                swapped = gp.tensor_tensor(rv[:, :, :, f], tv[:, :, :, 1 - f],
                                           sv[:, :, f].unsqueeze(1).broadcast_to([P, 4, 2, 32]), ALU.mult)
            link(swapped)
            link(gp.tensor_tensor(tmp[:, t, :].rearrange("p (h d) -> p h d", h=4),
                                  tmp[:, t, :].rearrange("p (h d) -> p h d", h=4),
                                  cosT[:, t, :].unsqueeze(1).broadcast_to([P, 4, P]), ALU.mult))
            gp.tensor_tensor(tmp[:, t, :], tmp[:, t, :], ropet[:, :], ALU.add).then_inc(roped, 1)

        def mask(n):
            pool.wait_ge(powers, 2 * n + 2)
            if n:
                pool.wait_ge(masks, n)
            if n >= 2:
                pool.wait_ge(ret_masked, n - 1)
            if n == 0:
                pool.wait_ge(na_biased, 16)
            link(gp.tensor_tensor(wmask[:, n % 2, 1, :], gfb[:, 0, 256:640], gfb[:, 1, 0:384], ALU.add))
            gp.tensor_tensor(gfb[:, 0, 0:384], gfb[:, 0, 0:384], decay[:, 1280:1664], ALU.mult)
            link(gp.tensor_tensor(gfb[:, 1, 256:640], gfb[:, 1, 256:640], decay[:, 1664:2048], ALU.mult))
            gp.tensor_tensor(wmask[:, n % 2, 0, :], gfb[:, 0, 0:384], gfb[:, 1, 256:640], ALU.add).then_inc(masks, 1)

        for b in range(NB):
            if b in kq_blocks and BLOCKS[b][0][1] == "r":
                rope(b, 0)
                rope(b, 1)
            if b in RET_BLOCKS:
                for hh in range(4):
                    mask(4 * RET_BLOCKS[b] + hh)
                pool.wait_ge(ret_var, RET_BLOCKS[b] + 1)
                gp.tensor_tensor(rg[:, :], rg[:, :], mhalf[:, :], ALU.pow).then_inc(ret_rstd, 1)
        pool.wait_ge(mean_sq, 2)
        gp.tensor_tensor(rs[:, 0:2], rs[:, 4:6], mhalf[:, 0:2], ALU.pow).then_inc(rstd_ok, 1)
        pool.wait_ge(f_mean, 1)
        gp.tensor_tensor(rs[:, 0:2], rs[:, 4:6], mhalf[:, 0:2], ALU.pow).then_inc(f_rstd, 1)

    es.close()


def kernel(**inputs):
    import concourse.bacc as bacc
    from concourse.bass_utils import run_bass_kernel_spmd

    def cols(a):
        a = np.asarray(a)
        return np.ascontiguousarray(a.reshape(-1, P).T)

    consts = host_constants()
    b_mod = np.asarray(inputs["b_mod"]).reshape(6, D)
    arrays = {
        "x": inputs["x"], "c": cols(inputs["c"]), "ctx": inputs["ctx"], "c_ctx": cols(inputs["c_ctx"]),
        "w_mod": inputs["w_mod"],
        "b_col": np.ascontiguousarray(b_mod[[0, 1, 3, 4]].reshape(4, KC, P).transpose(2, 0, 1)),
        "b_row": np.ascontiguousarray(b_mod[[2, 5]].reshape(2, 4, 512)),
        "nm": cols(inputs["norm_mix_w"]), "nf": cols(inputs["norm_ffn_w"]), "w_in": inputs["w_in"],
        "rpb": inputs["na_rpb"], "dec_f": np.asarray(inputs["ret_decay_fwd"]).reshape(8),
        "dec_b": np.asarray(inputs["ret_decay_bwd"]).reshape(8), "gn": cols(inputs["ret_gn_w"]),
        "w_out": inputs["w_out"], "w_router": inputs["w_router"], "w_gate": inputs["w_gate"],
        "w_up": inputs["w_up"], "w_down": inputs["w_down"], "fw": inputs["final_norm_w"],
        "k_decay": consts["decay"], "k_small": consts["small"], "k_window": consts["window"], "k_late": consts["late"],
    }
    nc = bacc.Bacc("TRN2", target_bir_lowering=False, num_devices=1)
    feeds, args = {}, []
    for name, a in arrays.items():
        a = np.ascontiguousarray(a)
        feeds[f"in_{name}"] = a
        args.append(nc.dram_tensor(f"in_{name}", a.shape, mybir.dt.from_np(a.dtype), kind="ExternalInput").ap())
    args.append(nc.dram_tensor("out_0", (1, SEQ, D), F32, kind="ExternalOutput").ap())
    build(nc, *args)
    r = run_bass_kernel_spmd(nc, [feeds], core_ids=[0])
    return r.results[0]["out_0"]
```

```python
from contextlib import ExitStack

import concourse.bass as bass
import numpy as np
from concourse import mybir

F32 = mybir.dt.float32
F32R = mybir.dt.float32r
BF16 = mybir.dt.bfloat16
ALU = mybir.AluOpType
ACT = mybir.ActivationFunctionType
AX_X = mybir.AxisListType.X

P = 128
D = 2048
KC = D // P
SEQ = 256
GRID_W = 64
HD = 128
NEG = -1e30
EPS = 1e-6
SCALE = HD ** -0.5
E = 16
FF = 1024
CAP = 32
FC = FF // P

COL = {"kn": 0, "vn": 1024, "kr": 2048, "vr": 3072, "qn": 4096, "qr": 5120, "gr": 6144}
BLOCKS = [(kind, g) for fam in (("kn", "qn", "vn"), ("kr", "qr", "vr", "gr")) for g in range(2) for kind in fam]
NB = len(BLOCKS)
NO = D // 512
MOD_FIRST = [0, 2, 1, 3]
MOD_BEFORE = len(MOD_FIRST)
EARLY = KC // 2
MOD_DONE = {1: 4, 2: 5, 3: 6, 5: 7, 6: 8, 8: 9, 10: 10, 12: 11}
AHEAD = 2
CHUNKS = KC
NA_BLOCKS = {3: 0, 6: 1}
RET_BLOCKS = {9: 0, 13: 1}


def tiles_of(b):
    return 4 if b < NB and BLOCKS[b][0][0] in "kv" else 2


def bank_of(b, t):
    return t + (2 if b >= NB and (b - NB) % 2 == 0 else 0)


def mod_step(b, k):
    if b == 0:
        return (MOD_DONE[1], k - EARLY) if k >= EARLY else None
    if b == 1:
        return (MOD_DONE[1], EARLY + k // 2) if k % 2 else None
    return (MOD_DONE[b], k) if b in MOD_DONE else None


def stream_items():
    items = []
    for gi in MOD_FIRST:
        for q in range(8):
            items.append(("mod", gi, q))
            if gi == MOD_FIRST[2] and q in (1, 6):
                items.append(("w", 0, q // 4))
    for b in range(NB + NO):
        for q in range(4):
            if b > 1 or (b, q) in ((0, 2), (0, 3), (1, 1), (1, 2), (1, 3)):
                items.append(("w", b, q))
            if b == 0 and q == 2:
                continue
            for k in range(4 * (q - (b == 0)), 4 * q + 4):
                step = mod_step(b, k)
                if step and step[1] % 2 == 0:
                    if b == 0 and step[1] == 2:
                        items.append(("w", 1, 0))
                    items.append(("mod", step[0], step[1] // 2))
    return items


def host_constants():
    p = np.arange(P)[:, None].astype(np.float64)
    t = np.arange(-128, 512)[None, :]
    tb = np.arange(-384, 256)[None, :]
    tm = np.arange(-128, 256)[None, :]
    decay = np.concatenate([np.maximum(t - p, 0), np.maximum(p - tb, 0), t[:, :384] >= p, p >= tm], 1)
    ident = np.eye(P)
    freq = 10000.0 ** (-np.arange(0, 64, 2, dtype=np.float32) / np.float32(64))
    cos, sin = [], []
    for tile in range(2):
        tok = np.arange(P) + P * tile
        ar = (tok // GRID_W).astype(np.float32)[:, None] * freq.astype(np.float32)
        ac = (tok % GRID_W).astype(np.float32)[:, None] * freq.astype(np.float32)
        cos.append(np.concatenate([np.cos(ar), np.cos(ar), np.cos(ac), np.cos(ac)], 1))
        sin.append(np.concatenate([-np.sin(ar), np.sin(ar), -np.sin(ac), np.sin(ac)], 1))
    slots = np.tile(np.arange(1, CAP + 1), (P, 1))
    stack = np.tile(np.eye(CAP), (4, 1))
    sel = np.zeros((P, 2))
    sel[0::32, 0] = 1
    sel[1::32, 1] = 1
    small = np.concatenate([ident] + cos + sin + [slots, stack, sel], 1)
    cq = (np.arange(P) % GRID_W)[:, None]
    ck = np.arange(GRID_W)[None, :]
    start = np.clip(cq - 8, 0, GRID_W - 16)
    flip = np.zeros((P, P))
    flip[np.arange(P), (np.arange(P) // GRID_W) * GRID_W + GRID_W - 1 - np.arange(P) % GRID_W] = 1
    window = np.where((ck >= start) & (ck < start + 16), 0.0, NEG)
    spread = np.concatenate([np.tile(ident[:, 32 * e:32 * e + 32], (1, 4)) for e in range(4)], 1)
    late = np.concatenate([spread, np.triu(np.ones((P, P)))], 1)
    f = lambda a: np.ascontiguousarray(a.astype(np.float32))
    return {"decay": f(decay), "small": f(small), "window": f(np.concatenate([window, flip], 1)), "late": f(late)}


def build(nc, x, c, ctx, c_ctx, w_mod, b_col, b_row, nm, nf, w_in, rpb, dec_f, dec_b, gn, w_out, w_router,
          w_gate, w_up, w_down, fw, k_decay, k_small, k_window, k_late, out):
    es = ExitStack()
    base = [16512]

    def at(name, kib, shape, dt=F32):
        return nc.alloc_sbuf_tensor_at(name, [P, *shape], dt, offset=16512 + int(kib * 1024))

    ring = at("ring", 0, [8, 2048])
    ring_b = at("ring_b", 80, [2, 2048])
    ring_c = at("ring_c", 128, [2, 2048])
    xin = at("xin", 32, [4, D])
    kT = at("kT", 32, [4, 512])
    qT = at("qT", 40, [4, SEQ])
    vv = at("vv", 44, [4, 512])
    gg = at("gg", 52, [2, 512])
    pT = at("pT", 56, [2, 4, SEQ])
    junk = at("junk", 64, [D])
    uh = at("uh", 64, [KC, 512], F32R)
    mh = at("mh", 64, [KC, SEQ], F32R)
    ml = at("ml", 80, [KC, SEQ], F32R)
    xg = at("xg", 64, [KC, P])
    m5 = at("m5", 72, [D])
    xnT = at("xnT", 96, [KC, 512])
    ul = at("ul", 96, [KC, 512], F32R)
    h = at("h", 96, [2, D])
    h2n = at("h2n", 112, [2, D])
    mixT = at("mixT", 128, [KC, SEQ])
    hTT = at("hTT", 128, [KC, SEQ])
    whl = at("whl", 144, [3, 2, 512], F32R)
    gup = at("gup", 144, [4, 512])
    sgate = at("sgate", 152, [FC, CAP])
    hT = at("hT", 153, [FC, CAP])
    part = at("part", 156, [2, 512])
    affT = at("affT", 156, [4, SEQ])
    bias = at("bias", 160, [8, 6, GRID_W])
    wmask = at("wmask", 160, [2, 2, 384])
    gfb = at("gfb", 166, [2, 640])
    yy = at("yy", 160, [4, 512])
    oh = at("oh", 168, [2, 512])
    tmp = at("tmp", 172, [4, 512])
    oha = at("oha", 172, [2, 512])
    tg = at("tg", 176, [4, SEQ])
    pb = at("pb", 180, [2, 512])
    gcur = at("gcur", 180, [SEQ])
    spread = at("spread", 181, [4, P])
    tri = at("tri", 183, [P])
    ropet = at("ropet", 184, [512])
    window = at("window", 184, [GRID_W + P])
    pad = at("pad", 185, [P])
    bias_r = at("bias_r", 128, [8 * 6 * GRID_W])
    rt = at("rt", 184, [512])
    mrow = at("mrow", 186, [2, 512])
    decay = at("decay", 190, [2048])
    fwb = at("fwb", 190, [D])
    small = at("small", 198, [834])
    pos = [198 + 834 * 4 / 1024]

    def more(name, shape, dt=F32):
        n = int(np.prod(shape)) * (2 if dt == BF16 else 4)
        t_ = at(name, pos[0], shape, dt)
        pos[0] += -(-n // 32) * 32 / 1024
        return t_

    pos[0] = -(-int(pos[0] * 1024) // 32) * 32 / 1024
    csT = more("csT", [KC, 32])
    wr = more("wr", [KC, E])
    ones = more("ones", [P])
    tri_b = more("tri_b", [P], BF16)
    ones_b = more("ones_b", [P], BF16)
    modc = more("modc", [4, KC, 2])
    nmc = more("nmc", [KC])
    nfc = more("nfc", [KC])
    gnc = more("gnc", [8])
    bcol = more("bcol", [4, KC])
    cin = more("cin", [2, KC])
    dec = more("dec", [2, 8])
    lg = more("lg", [4, 16])
    acol = more("acol", [2, KC])
    a2 = more("a2", [KC])
    ss = more("ss", [8])
    rs = more("rs", [8])
    mhalf = more("mhalf", [8])
    nmax = more("nmax", [4])
    psumm = more("psumm", [4])
    prec = more("prec", [4])
    bst = more("bst", [8, 6])
    mv = more("mv", [8, 2])
    rg = more("rg", [8])
    assert pos[0] * 1024 + 16512 <= 229368
    ident = small[:, 0:128]
    cosT = small[:, 128:384].rearrange("p (t d) -> p t d", t=2)
    sinT = small[:, 384:640].rearrange("p (t d) -> p t d", t=2)
    slots = small[:, 640:672]
    stack = small[:, 672:704]
    sel = small[:, 704:706]
    wrb = rt[:, 256:512].rearrange("p (k e) -> p k e", k=KC)
    shift_sum, shift_lg = rt[:, 212:228], rt[:, 228:244]
    aff = rt[:, 0:32].rearrange("p (t e) -> p t e", t=2)
    rmax, rsum = rt[:, 32:34], rt[:, 34:36]
    gts = rt[:, 36:68].rearrange("p (t e) -> p t e", t=2)
    sels = rt[:, 68:100].rearrange("p (t e) -> p t e", t=2)
    slotm = rt[:, 100:132].rearrange("p (t e) -> p t e", t=2)
    top8 = rt[:, 132:164]
    eq_b = rt[:, 164:180].bitcast(BF16).rearrange("p (t e) -> p t e", t=2)
    gt_b = rt[:, 180:196].bitcast(BF16).rearrange("p (t e) -> p t e", t=2)
    sel_b = rt[:, 196:212].bitcast(BF16).rearrange("p (t e) -> p t e", t=2)

    bank = [es.enter_context(nc.psum_tensor(f"bank{i}", [P, 512], F32)) for i in range(8)]
    pad_dram = nc.dram_tensor("rpb_padded", (120, 128), F32, kind="Internal").ap()

    def sem(name):
        return es.enter_context(nc.semaphore(name))

    small_in = sem("small_in")
    cond_in = sem("cond_in")
    decay_in = sem("decay_in")
    late_in = sem("late_in")
    fw_in = sem("fw_in")
    pad_in = sem("pad_in")
    pad_out = sem("pad_out")
    bias_in = sem("bias_in")
    tok_in = [sem(f"tok_in{t}") for t in range(4)]
    ring_full = [sem(f"ring_full{i}") for i in range(12)]
    h_in = sem("h_in")
    out_done = sem("out_done")
    act_link, dve_link, pool_link = sem("act_link"), sem("dve_link"), sem("pool_link")
    squares, mean_sq, rstd_ok, normed = sem("squares"), sem("mean_sq"), sem("rstd_ok"), sem("normed")
    x_turned, xt_act, xt_dve = sem("x_turned"), sem("xt_act"), sem("xt_dve")
    pool_init, c_act = sem("pool_init"), sem("c_act")
    mod_item_used, part_act, part_dve = sem("mod_item_used"), sem("part_act"), sem("part_dve")
    mod_mac = sem("mod_mac")
    mod_small, mod_add, a_ready = sem("mod_small"), sem("mod_add"), sem("a_ready")
    lg_act, lg_dve = sem("lg_act"), sem("lg_dve")
    bias_pe, bias_ok = sem("bias_pe"), sem("bias_ok")
    u_aff, uh_ok, ul_ok = sem("u_aff"), sem("uh_ok"), sem("ul_ok")
    hi_split, lo_split, chunk_used, tile_done = sem("hi_split"), sem("lo_split"), sem("chunk_used"), sem("tile_done")
    ev_act, ev_dve, roped = sem("ev_act"), sem("ev_dve"), sem("roped")
    kq_turned, kq_act, kq_dve = sem("kq_turned"), sem("kq_act"), sem("kq_dve")
    na_score, na_biased, na_exp, na_norm = sem("na_score"), sem("na_biased"), sem("na_exp"), sem("na_norm")
    na_turned, na_pt, na_out, na_mix = sem("na_turned"), sem("na_pt"), sem("na_out"), sem("na_mix")
    powers, masks = sem("powers"), sem("masks")
    ret_score, ret_masked, ret_out, ret_kept = sem("ret_score"), sem("ret_masked"), sem("ret_out"), sem("ret_kept")
    gate_act, ret_var, ret_rstd, ret_gated = sem("gate_act"), sem("ret_var"), sem("ret_rstd"), sem("ret_gated")
    ret_stats = sem("ret_stats")
    ret_turned, ret_mix_a, ret_mix_d = sem("ret_turned"), sem("ret_mix_a"), sem("ret_mix_d")
    mh_ok, ml_ok = sem("mh_ok"), sem("ml_ok")
    row_bc, row_act, h_ready, h_sq = sem("row_bc"), sem("row_act"), sem("h_ready"), sem("h_sq")
    h2_act, h_turned, ht_act, ht_dve = sem("h2_act"), sem("h_turned"), sem("ht_act"), sem("ht_dve")
    shift_in, shift_pe = sem("shift_in"), sem("shift_pe")
    r_pe, r_dve, r_act = sem("r_pe"), sem("r_dve"), sem("r_act")
    moe_used, gathered, xg_act, xg_dve = sem("moe_used"), sem("gathered"), sem("xg_act"), sem("xg_dve")
    gu_act, gu_dve, summed, silu_ok, hid_ok = sem("gu_act"), sem("gu_dve"), sem("summed"), sem("silu_ok"), sem("hid_ok")
    g_pe, g_ok, y_ok, comb, comb_add = sem("g_pe"), sem("g_ok"), sem("y_ok"), sem("comb"), sem("comb_add")
    f_pre, f_out_a = sem("f_pre"), sem("f_out_a")
    f_sq_a, f_mean, f_rstd, f_out = sem("f_sq_a"), sem("f_mean"), sem("f_rstd"), sem("f_out")

    items = stream_items()
    n_items = len(items)
    item_at = {it: n for n, it in enumerate(items)}
    slot, fill, fills, free_at = [], [], [0] * 12, [-99] * 12
    multiplied_at = {mod_step(b, k): CHUNKS * b + k for b in range(NB) for k in range(KC) if mod_step(b, k)}
    for n, (kind, b, q) in enumerate(items):
        if kind == "w" and b == 0:
            s_ = 4 + q
        else:
            late = n > item_at["w", 0, 3]
            usable = [0, 1, 2, 3] + [6] * (late and n < item_at["w", 2, 2]) + [7] * (late and n < item_at["w", 3, 0])
            s_ = min(usable, key=lambda i: free_at[i])
        if kind == "w":
            free_at[s_] = CHUNKS * b + 4 * q + 3 - AHEAD
        elif b in MOD_FIRST:
            free_at[s_] = (8 * MOD_FIRST.index(b) + q) // 2 - 9
        else:
            free_at[s_] = multiplied_at[b, 2 * q + 1]
        fills[s_] += 16
        slot.append(s_)
        fill.append(fills[s_])
    mod_order = MOD_FIRST + [MOD_DONE[b] for b in sorted(MOD_DONE)]

    def wait_item(eng, item):
        n = item_at[item]
        eng.wait_ge(ring_full[slot[n]], fill[n])

    n_even = [sum((tiles_of(i) + 1) // 2 for i in range(b)) for b in range(NB + 1)]

    def wait_evacuated(eng, b, t):
        if b >= NB:
            eng.wait_ge(h_ready, 2 * (b - NB) + t + 1)
        else:
            eng.wait_ge(ev_dve if t % 2 else ev_act, n_even[b] + t // 2 + 1)

    last_user = {}
    before = {}
    for b in range(NB + NO):
        for t in range(tiles_of(b)):
            before[b, t] = last_user.get(bank_of(b, t))
            last_user[bank_of(b, t)] = (b, t)
    n_tile = [sum(tiles_of(i) - 1 for i in range(b)) for b in range(NB + NO + 1)]

    def wait_projected(eng, b, t):
        if t == tiles_of(b) - 1:
            eng.wait_ge(chunk_used, CHUNKS * (b + 1))
        else:
            eng.wait_ge(tile_done, n_tile[b] + t + 1)

    kq_blocks = [b for b in range(NB) if BLOCKS[b][0][0] in "kq"]
    n_kq = {b: sum(tiles_of(i) for i in kq_blocks if i < b) for b in kq_blocks}
    n_kk = {b: sum(tiles_of(i) for i in kq_blocks if i < b and BLOCKS[i][0][0] == "k") for b in kq_blocks}
    n_qq = {b: n_kq[b] - n_kk[b] for b in kq_blocks}
    n_rope = {b: 2 * sum(1 for i in kq_blocks if i < b and BLOCKS[i][0][1] == "r") for b in kq_blocks}

    def wait_turned_read(eng, m):
        for b in kq_blocks:
            if n_kq[b] <= m < n_kq[b] + tiles_of(b):
                if BLOCKS[b][0][0] == "k":
                    eng.wait_ge(kq_dve, n_kk[b] + m - n_kq[b] + 1)
                else:
                    eng.wait_ge(kq_act, n_qq[b] + m - n_kq[b] + 1)

    moe_slots = [4, 5, 6, 7] + sorted(range(4), key=lambda i: free_at[i]) + [8, 9, 10, 11]
    RING = len(moe_slots)

    def slot_buf(s):
        return ring[:, s, :] if s < 8 else (ring_b if s < 10 else ring_c)[:, s % 2, :]

    wg_v = w_gate[0].rearrange("e (j k p) f -> e j p k f", p=P, k=2)
    wu_v = w_up[0].rearrange("e (j k p) f -> e j p k f", p=P, k=2)
    wd_v = w_down[0].rearrange("e (r k p) (j n) -> e j r p k n", p=P, r=2, n=512)
    win_v = w_in[0].rearrange("(k p) n -> p k n", p=P)
    wout_v = w_out[0].rearrange("(k p) n -> p k n", p=P)
    wmod_v = w_mod[0].rearrange("(k p) n -> p k n", p=P)
    x_v = x[0].rearrange("(t p) d -> t p d", p=P)
    ctx_v = ctx[0].rearrange("(t p) d -> t p d", p=P)
    out_v = out[0].rearrange("(t p) d -> t p d", p=P)

    block = es.enter_context(nc.Block())

    @block.sync
    def _(sp):
        for n, (kind, b, q) in enumerate(items):
            if slot[n] >= 4 and fill[n] == 16:
                sp.wait_ge(x_turned, KC)
            elif fill[n] > 16:
                k0, b0, q0 = items[max(i for i in range(n) if slot[i] == slot[n])]
                if k0 == "mod" and b0 < MOD_BEFORE:
                    sp.wait_ge(mod_item_used, 8 * mod_order.index(b0) + q0 + 1)
                elif k0 == "mod":
                    sp.wait_ge(mod_mac, KC * (b0 - MOD_BEFORE) + 2 * q0 + 2)
                else:
                    sp.wait_ge(lo_split, CHUNKS * b0 + 4 * q0 + 4)
            if kind == "mod":
                dst = ring[:, slot[n], :].rearrange("p (k c) -> p k c", k=2)
                src = wmod_v[:, 2 * q:2 * q + 2, 1024 * b:1024 * b + 1024]
            else:
                dst = ring[:, slot[n], :].rearrange("p (k c) -> p k c", k=4)
                if b < NB:
                    c0 = COL[BLOCKS[b][0]] + 512 * BLOCKS[b][1]
                    src = win_v[:, 4 * q:4 * q + 4, c0:c0 + 512]
                else:
                    src = wout_v[:, 4 * q:4 * q + 4, 512 * (b - NB):512 * (b - NB) + 512]
            sp.dma_start(dst, src).then_inc(ring_full[slot[n]], 16)

        def expert_item(e, i):
            s = moe_slots[i % RING]
            what, j = i // 8, i % 8
            if what == 2:
                dst = slot_buf(s).rearrange("p (k c) -> p k c", k=4)
                src = wd_v[bass.ds(e, 1), j // 2, j % 2]
            else:
                dst = slot_buf(s).rearrange("p (k c) -> p k c", k=2)
                src = (wg_v, wu_v)[what][bass.ds(e, 1), j]
            sp.dma_start(dst, src.rearrange("a p k f -> (a p) k f")).then_inc(ring_full[s], 16)

        for i in range(RING):
            s = moe_slots[i]
            if i == 0:
                sp.wait_ge(ret_out, 8)
                sp.wait_ge(ret_gated, 2)
            if s < 4:
                _, b0, q0 = items[max(n for n in range(n_items) if slot[n] == s)]
                sp.wait_ge(lo_split, CHUNKS * b0 + 4 * q0 + 4)
            if s == 8:
                sp.wait_ge(chunk_used, CHUNKS * (NB + NO))
            if s == 10:
                sp.wait_ge(r_pe, 1)
            expert_item(0, i)
        with sp.Fori(0, E - 1) as e:
            for i in range(RING, RING + 24):
                if i == 15:
                    sp.wait_ge(moe_used, e * 24 + (i - RING + 2))
                elif i != 16:
                    sp.wait_ge(moe_used, e * 24 + (i - RING + 1))
                expert_item(e + 1 if i >= 24 else e, i % 24)
        for i in range(RING, 24):
            sp.wait_ge(moe_used, 24 * (E - 1) + i - RING + 1)
            expert_item(E - 1, i)
        for i, (t, half) in enumerate(((1, 0), (0, 0), (1, 1), (0, 1))):
            cs = slice(1024 * half, 1024 * half + 1024)
            if i == 1:
                sp.wait_ge(f_out_a, 1)
            else:
                sp.wait_ge(f_out, max(i, 1))
            sp.dma_start(out_v[t][:, cs], h2n[:, t, cs]).then_inc(out_done, 16)
        sp.wait_ge(out_done, 64)
        sp.wait_ge(pad_out, 16)

    @block.tensor
    def _(pe):
        mm = nc.tensor.matmul

        def mod_item(i, q):
            gi = mod_order[i]
            if i and q == 0:
                pe.wait_ge(part_act, i)
                pe.wait_ge(part_dve, i)
            wait_item(pe, ("mod", gi, q))
            w = ring[:, slot[item_at["mod", gi, q]], :].rearrange("p (k c) -> p k c", k=2)
            for half in range(2):
                for kk in range(2):
                    quad = 2 * ((q + half) % 2) + kk
                    last = mm(bank[4 + half][32 * quad:32 * quad + 32, :], csT[:, 2 * q + kk, :],
                              w[:, kk, 512 * half:512 * half + 512], start=q < 2, stop=q >= 6)
            last.then_inc(mod_item_used, 1)

        def mod_sums(i):
            gi = mod_order[i]
            if i < MOD_BEFORE:
                pe.wait_ge(part_act, i + 1)
                pe.wait_ge(part_dve, i + 1)
                col = sel
            else:
                pe.wait_ge(mod_mac, KC * (i - MOD_BEFORE + 1))
                col = ones[:, 0:2]
            if i:
                pe.wait_ge(mod_add, i)
            for half in range(2):
                if gi // 2 in (2, 5):
                    quad = 2 * (gi % 2) + half
                    last = mm(bank[7][32 * quad:32 * quad + 1, :], col[:, 0:1], part[:, half, :], start=True, stop=True)
                else:
                    for j in range(4):
                        i2 = 4 * half + j
                        last = mm(bank[7][:, 2 * i2:2 * i2 + 2], part[:, half, P * j:P * j + P], col,
                                  start=True, stop=True)
            last.then_inc(mod_small, 1)

        def project(b, k):
            cidx = CHUNKS * b + k
            if b == 0:
                pe.wait_ge(ul_ok, k + 1)
            if b == NB:
                pe.wait_ge(ml_ok, k + 1)
            pe.wait_ge(lo_split, cidx + 1)
            wh, wl = whl[:, cidx % (AHEAD + 1), 0, :], whl[:, cidx % (AHEAD + 1), 1, :]
            hi, lo = (uh, ul) if b < NB else (mh, ml)
            for t in range(tiles_of(b)):
                if k == 0 and before[b, t]:
                    wait_evacuated(pe, *before[b, t])
                ps = bank[bank_of(b, t)][:, :]
                cols = slice(P * t, P * t + P)
                mm(ps, hi[:, k, cols], wh, start=k == 0, stop=False)
                mm(ps, hi[:, k, cols], wl, start=False, stop=False)
                last = mm(ps, lo[:, k, cols], wh, start=False, stop=k == KC - 1)
                if t == tiles_of(b) - 1:
                    last.then_inc(chunk_used, 1)
                elif k == KC - 1:
                    last.then_inc(tile_done, 1)

        def turn_tile(b, t):
            m = n_kq[b] + t
            wait_evacuated(pe, b, t)
            if BLOCKS[b][0][1] == "r" and t < 2:
                pe.wait_ge(roped, n_rope[b] + t + 1)
            if m >= 2:
                wait_turned_read(pe, m - 2)
            if b in MOD_DONE or b == 0:
                pe.wait_ge(mod_add, mod_order.index(MOD_DONE[b]) + 1 if b else MOD_BEFORE)
            for hh in range(4):
                last = nc.tensor.transpose(bank[6 + m % 2][:, P * hh:P * hh + P], tmp[:, t, P * hh:P * hh + P], ident)
            last.then_inc(kq_turned, 1)

        def na_scores(g, u):
            n = 8 * g + u
            if u == 0:
                pe.wait_ge(kq_dve, n_kk[3 * g] + 4)
                pe.wait_ge(kq_act, n_qq[3 * g + 1] + 2)
            if n >= 2:
                pe.wait_ge(na_biased, n - 1)
            hh, qt = u // 2, u % 2
            mm(bank[4 + u % 2][:, :], qT[:, hh, P * qt:P * qt + P], kT[:, hh, :], start=True, stop=True).then_inc(na_score, 1)

        def na_turn(g, u):
            n = 8 * g + u
            pe.wait_ge(na_norm, n + 1)
            if n >= 1:
                pe.wait_ge(na_pt, n)
            for kt in range(4):
                last = nc.tensor.transpose(bank[6][:, P * kt:P * kt + P], pb[:, u % 2, P * kt:P * kt + P], ident)
            last.then_inc(na_turned, 1)

        def na_values(g, u):
            hn = 4 * g + u // 2
            pe.wait_ge(na_pt, 8 * g + u + 1)
            if u == 1:
                wait_evacuated(pe, 3 * g + 2, 2)
                wait_evacuated(pe, 3 * g + 2, 3)
            if hn:
                pe.wait_ge(na_mix, hn)
            for kt in range(4):
                last = mm(bank[7][:, 0:SEQ], vv[:, kt, P * (u // 2):P * (u // 2) + P], pT[:, (u // 2) % 2, kt, :],
                          start=kt == 0, stop=kt == 3)
            last.then_inc(na_out, 1)

        def ret_scores(g, hh):
            n = 4 * g + hh
            if hh == 0:
                pe.wait_ge(kq_dve, n_kk[6 + 4 * g] + 4)
                pe.wait_ge(kq_act, n_qq[7 + 4 * g] + 2)
            if n:
                pe.wait_ge(ret_masked, n)
            for kt in range(4):
                last = mm(bank[4 + kt // 2][:, SEQ * (kt % 2):SEQ * (kt % 2) + SEQ], kT[:, hh, P * kt:P * kt + P],
                          qT[:, hh, :], start=True, stop=True)
            last.then_inc(ret_score, 1)

        def ret_values(g, hh):
            n = 4 * g + hh
            pe.wait_ge(ret_masked, n + 1)
            if hh == 0:
                wait_evacuated(pe, 8 + 4 * g, 2)
                wait_evacuated(pe, 8 + 4 * g, 3)
            if n >= 2:
                pe.wait_ge(ret_kept, n - 1)
            for it in range(2):
                for kt in range(4):
                    last = mm(bank[6 + hh % 2][:, P * it:P * it + P], pT[:, hh % 2, kt, P * it:P * it + P],
                              vv[:, kt, P * hh:P * hh + P], start=kt == 0, stop=kt == 3)
            last.then_inc(ret_out, 1)

        def ret_turn(g):
            pe.wait_ge(ret_gated, g + 1)
            for hh in range(4):
                for it in range(2):
                    last = nc.tensor.transpose(bank[6 + hh // 2][:, SEQ * (hh % 2) + P * it:SEQ * (hh % 2) + P * it + P],
                                               pb[:, it, P * hh:P * hh + P], ident)
            last.then_inc(ret_turned, 1)

        def row_on_all(m, quad, dst):
            return mm(dst, ones[32 * quad:32 * quad + 1, :], mrow[32 * quad:32 * quad + 1, m, :], start=True, stop=True)

        def turn_tokens(k):
            if k == 0:
                pe.wait_ge(small_in, 16 * 11)
                pe.wait_ge(normed, 4)
            if k >= 4:
                pe.wait_ge(xt_dve if k % 2 else xt_act, k // 2 - 1)
            for t in range(4):
                last = nc.tensor.transpose(bank[k % 4][:, P * t:P * t + P], xin[:, t, P * k:P * k + P], ident)
            last.then_inc(x_turned, 1)

        def flip_bias(j):
            if j == 0:
                pe.wait_ge(bias_in, 16 * 16)
                pe.wait_ge(kq_dve, 4)
                pe.wait_ge(kq_act, 2)
            else:
                pe.wait_ge(bias_ok, j)
            mm(bank[6][:, :], window[:, GRID_W:], bias_r[:, 512 * j:512 * j + 512], start=True, stop=True).then_inc(bias_pe, 1)

        pe.wait_ge(c_act, 2)
        pe.wait_ge(pool_init, 3)
        for i in range(MOD_BEFORE):
            for q in range(8):
                mod_item(i, q)
                if i and q == 1:
                    mod_sums(i - 1)
                if i == 1 and q < 6:
                    for k in range(3 * q - max(q - 4, 0), 3 * q + 3 - max(q - 3, 0)):
                        turn_tokens(k)
                step = 8 * (i - 2) + q
                if step >= 3 and step % 2:
                    if step == 3:
                        pe.wait_ge(xt_act, 8)
                        pe.wait_ge(xt_dve, 8)
                    project(0, (step - 3) // 2)
        mod_sums(MOD_BEFORE - 1)

        def turn_stream(cb):
            pe.wait_ge(h_ready, 2 * cb + 2)
            if cb:
                pe.wait_ge(ht_act, cb)
                pe.wait_ge(ht_dve, cb)
            for i in range(4):
                k = 4 * cb + i
                bk = bank[(0 if cb == NO - 1 else 6) + i // 2]
                for t in range(2):
                    last = nc.tensor.transpose(bk[:, SEQ * (i % 2) + P * t:SEQ * (i % 2) + P * t + P],
                                               h[:, t, P * k:P * k + P], ident)
            last.then_inc(h_turned, 1)

        def router_chunk(k):
            if k == 0:
                pe.wait_ge(row_act, 4)
                pe.wait_ge(a_ready, 3)
            if k % 2 == 0:
                pe.wait_ge(ht_dve if k % 4 else ht_act, k // 4 + 1)
            for t in range(2):
                last = mm(bank[4 + t][:, 0:E], hTT[:, k, P * t:P * t + P], wr[:, k, :], start=k == 0, stop=k == KC - 1)
            return last

        for b in range(NB + NO):
            for k in range(EARLY - 1 if b == 0 else 0, KC):
                project(b, k)
                prev = b - 1
                if prev in MOD_DONE and k == 0:
                    if prev in NA_BLOCKS:
                        pe.wait_ge(na_mix, 4 * NA_BLOCKS[prev] + 4)
                    mod_sums(mod_order.index(MOD_DONE[prev]))
                if prev in kq_blocks and 4 <= k < 4 + tiles_of(prev):
                    turn_tile(prev, k - 4)
                if b == 2 and 8 <= k < 14:
                    flip_bias(k - 8)
                if b in NA_BLOCKS:
                    g = NA_BLOCKS[b]
                    if 4 <= k < 12:
                        na_scores(g, k - 4)
                    if 6 <= k < 14:
                        na_turn(g, k - 6)
                    if 7 <= k < 15 and k % 2 == 0:
                        na_values(g, k - 7)
                if b in RET_BLOCKS:
                    g = RET_BLOCKS[b]
                    if k in (4, 7, 10, 13):
                        ret_scores(g, (k - 4) // 3)
                    if k in (6, 9, 12, 15):
                        ret_values(g, (k - 6) // 3)
                if prev in RET_BLOCKS and k == 8:
                    ret_turn(RET_BLOCKS[prev])
                if b > NB and k == 4:
                    turn_stream(b - NB - 1)
                if b == NB + 1 and k == 9:
                    pe.wait_ge(shift_in, 1)
                    pe.wait_ge(ht_act, 1)
                    mm(bank[6][:, 0:E], ones[:, :], shift_sum, start=True, stop=True).then_inc(shift_pe, 1)
                if b >= NB and k == 8:
                    cb = b - NB
                    if cb >= 2:
                        pe.wait_ge(row_act, cb - 1)
                    row_on_all(0, cb, bank[4 + cb % 2][:, :]).then_inc(row_bc, 1)

        for k in range(8):
            router_chunk(k)
        turn_stream(NO - 1)
        for k in range(8, KC - 1):
            router_chunk(k)
        router_chunk(KC - 1).then_inc(r_pe, 1)
        pe.wait_ge(r_dve, 2)
        for t in range(2):
            last = nc.tensor.transpose(bank[0][0:E, P * t:P * t + P], aff[:, t, :], ident)
        last.then_inc(r_pe, 1)
        pe.wait_ge(ht_act, NO)
        pe.wait_ge(ht_dve, NO)
        for cb in range(2):
            row_on_all(1, cb, bank[6 + cb][:, :]).then_inc(row_bc, 1)
        pe.wait_ge(r_dve, 3)
        for i in range(2):
            for t in range(2):
                last = nc.tensor.transpose(bank[1][:, E * (2 * i + t):E * (2 * i + t) + E],
                                           affT[0:16, 1 + i, P * t:P * t + P], ident[0:16, 0:16])
        last.then_inc(r_pe, 1)
        pe.wait_ge(r_dve, 4)
        pe.wait_ge(late_in, 32)
        for t in range(2):
            srcs = [(ones_b, eq_b[:, 0, :])] * (t == 1) + [(tri_b, eq_b[:, t, :]), (ones_b, gt_b[:, 0, :]), (ones_b, gt_b[:, 1, :])]
            for i, (l, r) in enumerate(srcs):
                last = mm(bank[4][:, E * t:E * t + E], l[:, :], r, start=i == 0, stop=i == len(srcs) - 1)
        last.then_inc(r_pe, 1)
        pe.wait_ge(r_dve, 5)
        for t in range(2):
            srcs = [(ones_b, sel_b[:, 0, :])] * (t == 1) + [(tri_b, sel_b[:, t, :])]
            for i, (l, r) in enumerate(srcs):
                last = mm(bank[5][:, E * t:E * t + E], l[:, :], r, start=i == 0, stop=i == len(srcs) - 1)
        last.then_inc(r_pe, 1)
        for cb in range(2, 4):
            row_on_all(1, cb, bank[cb][:, :]).then_inc(row_bc, 1)
        pe.wait_ge(r_dve, 6)
        pe.wait_ge(row_act, 6)
        for g in range(4):
            for t in range(2):
                last = nc.tensor.transpose(bank[6 + g // 2][:, SEQ * (g % 2) + P * t:SEQ * (g % 2) + P * t + P],
                                           oha[:, t, P * g:P * g + P], ident)
        last.then_inc(r_pe, 1)

        def gather(g, j):
            for k in range(4 * j, 4 * j + 4):
                for t in range(2):
                    last = mm(bank[2 + j % 2][:, P * (k % 4):P * (k % 4) + P], h2n[:, t, P * k:P * k + P],
                              oh[:, t, bass.ds(g * P, P)], start=t == 0, stop=t == 1)
            last.then_inc(gathered, 1)

        def combine(g, ei, cb):
            pe.wait_ge(y_ok, g * 16 + (4 * ei + cb + 2))
            pe.wait_ge(comb_add, g * 32 + (8 * ei + max(2 * cb - 2, 1)))
            for t in range(2):
                mm((bank[cb] if t else bank[6 + cb % 2])[:, :], gcur[:, P * t:P * t + P], yy[:, cb, :],
                   start=True, stop=True).then_inc(comb, 1)

        pe.wait_ge(row_act, 8)
        pe.wait_ge(h2_act, 2)
        pe.sem_inc(summed, 1)
        pe.sem_inc(comb, 1)
        with pe.Fori(0, 4) as g:
            pe.wait_ge(comb_add, g * 32 + 1)
            for ei in range(4):
                if ei:
                    pe.wait_ge(comb_add, g * 32 + (8 * ei + 1))
                for m in range(2):
                    if ei == 0 and m == 1:
                        pe.wait_ge(xg_act, g * 8 + 8)
                        pe.wait_ge(xg_dve, g * 8 + 8)
                    for j in range(8):
                        if ei == 0 and m == 0 and j == 0:
                            gather(g, 0)
                            gather(g, 1)
                        if ei == 0 and m == 0:
                            pe.wait_ge(xg_act, g * 8 + (j + 1))
                            pe.wait_ge(xg_dve, g * 8 + (j + 1))
                        i = 8 * m + j
                        s = moe_slots[i % RING]
                        pe.wait_ge(ring_full[s], g * (16 * 8) + (fills[s] + 16 * (2 * ei + i // RING + 1)))
                        w = slot_buf(s).rearrange("p (k c) -> p k c", k=2)
                        for half in range(2):
                            for kk in range(2):
                                quad = 2 * ((j + half) % 2) + kk
                                last = mm(bank[2 * m + half][32 * quad:32 * quad + 32, :],
                                          xg[:, 2 * j + kk, CAP * ei:CAP * ei + CAP],
                                          w[:, kk, 512 * half:512 * half + 512], start=j < 2, stop=j >= 6)
                        last.then_inc(moe_used, 1)
                        if ei == 0 and m == 0 and j in (1, 3):
                            gather(g, (j + 3) // 2)
                pe.wait_ge(g_ok, g * 4 + (ei + 1))
                if ei == 0:
                    pe.wait_ge(r_act, 2)
                    pe.wait_ge(r_dve, 7)
                mm(bank[5][:, 0:SEQ], spread[:, ei, :], tg[:, bass.ds(g, 1), :].rearrange("p a n -> p (a n)"),
                   start=True, stop=True).then_inc(g_pe, 1)
                pe.wait_ge(gu_act, g * 8 + (2 * ei + 2))
                pe.wait_ge(gu_dve, g * 8 + (2 * ei + 2))
                pe.wait_ge(hid_ok, g * 4 + (ei + 1))
                for i in range(16):
                    last = mm(bank[4][:, CAP * i:CAP * i + CAP], gup[:, i // 4, P * (i % 4):P * (i % 4) + P], stack,
                              start=True, stop=True)
                last.then_inc(summed, 1)
                pe.wait_ge(hid_ok, g * 4 + (ei + 2))
                pe.wait_ge(g_ok, g * 4 + (ei + 2))
                for cb in range(5):
                    for j in range(2 * cb, 2 * cb + 2) if cb < 4 else ():
                        s = moe_slots[(16 + j) % RING]
                        pe.wait_ge(ring_full[s], g * (16 * 8) + (fills[s] + 16 * (2 * ei + 2)))
                        w = slot_buf(s).rearrange("p (k c) -> p k c", k=4)
                        for quad in range(4):
                            last = mm(bank[cb][32 * quad:32 * quad + 32, :], hT[:, 4 * (j % 2) + quad, :],
                                      w[:, quad, :], start=j % 2 == 0, stop=j % 2 == 1)
                        last.then_inc(moe_used, 1)
                    if cb:
                        combine(g, ei, cb - 1)

    @block.scalar
    def _(act):
        a = nc.scalar.activation
        links = [0]

        def link(ins):
            links[0] += 1
            ins.then_inc(act_link, 1)
            act.wait_ge(act_link, links[0])

        for i, src in enumerate((c, c_ctx)):
            act.dma_start(cin[:, i, :], src).then_inc(cond_in, 16)
        for t in range(4):
            act.dma_start(xin[:, t, :], (x_v if t < 2 else ctx_v)[t % 2]).then_inc(tok_in[t], 16)
        act.wait_ge(pool_init, 1)
        act.dma_start(pad[0:120, 48:79], rpb[0].rearrange("h r c -> (h r) c")).then_inc(pad_in, 16)
        loads = [(small[:, 0:706], k_small), (nmc[:, :], nm), (nfc[:, :], nf),
                 (gnc[:, :], gn), (bcol[:, :, :], b_col), (dec[:, 0, :], dec_f.partition_broadcast(P)),
                 (dec[:, 1, :], dec_b.partition_broadcast(P)), (window[:, :], k_window),
                 (wr[:, :, :], w_router[0].rearrange("(k p) e -> p k e", p=P))]
        for dst, src in loads:
            act.dma_start(dst, src).then_inc(small_in, 16)
        for m in range(2):
            act.dma_start(mrow[0:P:32, m, :], b_row[m]).then_inc(small_in, 16)
        act.wait_ge(pool_init, 2)
        act.wait_ge(cond_in, 32)
        for i in range(2):
            a(csT[:, :, i], cin[:, i, :], ACT.Silu).then_inc(c_act, 1)
        act.wait_ge(pad_in, 16)
        act.dma_start(pad_dram, pad[0:120, :]).then_inc(pad_out, 16)
        for t in range(4):
            act.wait_ge(tok_in[t], 16)
            a(junk[:, :], xin[:, t, :], ACT.Square, accum_out=ss[:, t:t + 1]).then_inc(squares, 1)
            act.wait_ge(squares, t + 1)
        act.wait_ge(lg_dve, 1)
        link(a(lg[:, 1, :], lg[:, 0, :], ACT.Exp, scale=-1.0))
        a(lg[:, 2, :], lg[:, 1, :], ACT.Ln, bias=1.0).then_inc(lg_act, 1)

        def keep_tokens():
            for k in range(0, KC, 2):
                act.wait_ge(x_turned, k + 1)
                a(xnT[:, k, :], bank[k % 4][:, :], ACT.Copy).then_inc(xt_act, 1)

        def mod_part(i):
            act.wait_ge(mod_item_used, 8 * i + 8)
            if i:
                act.wait_ge(mod_small, i)
            a(part[:, 0, :], bank[4][:, :], ACT.Copy).then_inc(part_act, 1)

        def split(b, k):
            cidx = CHUNKS * b + k
            if k % 4 == 0:
                wait_item(act, ("w", b, k // 4))
            if cidx > AHEAD:
                act.wait_ge(chunk_used, cidx - AHEAD)
            n = item_at["w", b, k // 4]
            a(whl[:, cidx % (AHEAD + 1), 0, :], ring[:, slot[n], 512 * (k % 4):512 * (k % 4) + 512], ACT.Copy).then_inc(hi_split, 1)

        def evacuate(b):
            kind = BLOCKS[b][0][0]
            for t in range(0, tiles_of(b), 2):
                wait_projected(act, b, t)
                if kind in "kq":
                    dst = tmp[:, t, :]
                    i = kq_blocks.index(b)
                    if i:
                        act.wait_ge(kq_turned, n_kq[b])
                else:
                    dst = (vv if kind == "v" else gg)[:, t, :]
                    if kind == "g" and BLOCKS[b][1]:
                        act.wait_ge(ret_gated, 1)
                    if kind == "v" and b == 5:
                        act.wait_ge(na_out, 4)
                    if kind == "v" and b == 8:
                        act.wait_ge(na_out, 8)
                    if kind == "v" and b == 12:
                        act.wait_ge(ret_out, 4)
                a(dst, bank[bank_of(b, t)][:, :], ACT.Copy).then_inc(ev_act, 1)

        def load_bias(half, hh):
            if half == 0 and hh == 0:
                act.wait_ge(pad_out, 16)
            src = bass.AP(pad_dram.tensor, pad_dram.offset + (15 * hh + 5 - half) * P,
                          [[1, GRID_W], [P, 6], [1, GRID_W]])
            dst = bias_r[64 * half:64 * half + 64, 384 * hh:384 * hh + 384].rearrange("p (s c) -> p s c", s=6)
            act.dma_start(dst, src).then_inc(bias_in, 16)

        def query_tile(b, t):
            act.wait_ge(kq_turned, n_kq[b] + t + 1)
            src = bank[6 + (n_kq[b] + t) % 2][:, :].rearrange("p (h n) -> p h n", h=4)
            a(qT[:, :, P * t:P * t + P], src, ACT.Copy, scale=SCALE).then_inc(kq_act, 1)

        def na_exponent(g, u):
            n = 8 * g + u
            act.wait_ge(na_biased, n + 1)
            a(pb[:, u % 2, :], pb[:, u % 2, :], ACT.Exp, bias=nmax[:, n % 4:n % 4 + 1],
              accum_out=psumm[:, n % 4:n % 4 + 1]).then_inc(na_exp, 1)

        def na_keep(g, u):
            act.wait_ge(na_turned, 8 * g + u + 1)
            src = bank[6][:, :].rearrange("p (k n) -> p k n", k=4)
            a(pT[:, (u // 2) % 2, :, P * (u % 2):P * (u % 2) + P], src, ACT.Copy).then_inc(na_pt, 1)

        def na_mixed(g, u):
            hn = 4 * g + u // 2
            act.wait_ge(na_out, hn + 1)
            a(mixT[:, hn, :], bank[7][:, 0:SEQ], ACT.Copy).then_inc(na_mix, 1)

        def gamma_powers(n):
            if n:
                act.wait_ge(masks, n)
            else:
                act.wait_ge(lg_dve, 2)
                act.wait_ge(decay_in, 16)
            for i in range(2):
                a(gfb[:, i, :], decay[:, 640 * i:640 * i + 640], ACT.Exp,
                  scale=lg[:, 3, 8 * i + n:8 * i + n + 1]).then_inc(powers, 1)

        def ret_keep(g, hh):
            n = 4 * g + hh
            act.wait_ge(ret_out, n + 1)
            if hh == 0 and g:
                act.wait_ge(ret_turned, 1)
            src = bank[6 + hh % 2][:, 0:SEQ].rearrange("p (t e) -> p t e", t=2)
            a(pb[:, :, P * hh:P * hh + P], src, ACT.Copy).then_inc(ret_kept, 1)

        def ret_mixed(g, half):
            act.wait_ge(ret_turned, g + 1)
            hn = 8 + 4 * g + 2 * half
            a(mixT[:, hn, :], bank[6 + half][:, 0:SEQ], ACT.Copy, scale=gnc[:, hn - 8:hn - 7]).then_inc(ret_mix_a, 1)

        def ahead(cidx):
            b, k = divmod(cidx, KC)
            split(b, k)
            if b == 0:
                if k % EARLY == 0:
                    act.wait_ge(a_ready, k // EARLY + 1)
                    act.wait_ge(xt_dve, 8)
                link(a(xnT[:, k, SEQ:512], xnT[:, k, SEQ:512], ACT.Identity, scale=acol[:, 1, k:k + 1],
                       bias=modc[:, 0, k, 1:2]))
                act.wait_ge(u_aff, k + 1)
                a(uh[:, k, :], xnT[:, k, :], ACT.Copy).then_inc(uh_ok, 1)
            if b == NB:
                if k == 0:
                    act.wait_ge(na_mix, 8)
                if k == 8:
                    act.wait_ge(ret_mix_a, 2)
                    act.wait_ge(ret_mix_d, 2)
                if k == 12:
                    act.wait_ge(ret_mix_a, 4)
                    act.wait_ge(ret_mix_d, 4)
                act.wait_ge(chunk_used, CHUNKS * (NB - 1) + k // 2 + 1)
                a(mh[:, k, :], mixT[:, k, :], ACT.Copy).then_inc(mh_ok, 1)

        def keep_stream(cb):
            act.wait_ge(h_turned, cb + 1)
            if cb == 0:
                act.wait_ge(ml_ok, KC)
            a(hTT[:, 4 * cb:4 * cb + 2, :], bank[0 if cb == NO - 1 else 6][:, :].rearrange("p (k n) -> p k n", k=2),
              ACT.Copy).then_inc(ht_act, 1)

        mod_part(0)
        keep_tokens()
        mod_part(1)
        for cidx in range(5):
            ahead(cidx)
        mod_part(2)
        for cidx in range(5, EARLY):
            ahead(cidx)
        mod_part(3)
        for b in range(NB + NO):
            prev = b - 1
            for k in range(EARLY - AHEAD if b == 0 else 0, KC):
                if k == 0 and 0 <= prev < NB:
                    evacuate(prev)
                if prev in RET_BLOCKS and k == 9:
                    ret_mixed(RET_BLOCKS[prev], 0)
                    ret_mixed(RET_BLOCKS[prev], 1)
                if CHUNKS * b + k + AHEAD < CHUNKS * (NB + NO):
                    ahead(CHUNKS * b + k + AHEAD)
                if b == 1:
                    load_bias(k // 8, k % 8)
                if b == 3 and k == 1:
                    act.dma_start(decay[:, :], k_decay).then_inc(decay_in, 16)
                if prev in kq_blocks and BLOCKS[prev][0][0] == "q" and 4 <= k < 6:
                    query_tile(prev, k - 4)
                if b in NA_BLOCKS:
                    g = NA_BLOCKS[b]
                    if 4 <= k < 12:
                        na_exponent(g, k - 4)
                    if 6 <= k < 14:
                        na_keep(g, k - 6)
                    if 7 <= k < 15 and k % 2 == 0:
                        na_mixed(g, k - 7)
                if b + 1 in RET_BLOCKS and k == 12:
                    gamma_powers(4 * RET_BLOCKS[b + 1])
                if b in RET_BLOCKS:
                    g = RET_BLOCKS[b]
                    if k in (2, 5, 8):
                        gamma_powers(4 * g + 1 + (k - 2) // 3)
                    if k in (6, 9, 12, 15):
                        ret_keep(g, (k - 6) // 3)
                if prev in RET_BLOCKS and k == 2:
                    act.wait_ge(ev_dve, n_even[prev] + 1)
                    act.wait_ge(ev_act, n_even[prev] + 1)
                    a(gg[:, :, :], gg[:, :, :], ACT.Silu).then_inc(gate_act, 1)
                if b == NB and k == 2:
                    act.wait_ge(chunk_used, CHUNKS * NB)
                    for t in range(2):
                        act.dma_start(h[:, t, :], x_v[t]).then_inc(h_in, 16)
                if b == NB + 1 and k == 5:
                    act.wait_ge(ret_turned, 2)
                    act.dma_start(spread[:, :, :], k_late[:, 0:512].rearrange("p (e m) -> p e m", e=4)).then_inc(late_in, 16)
                    act.dma_start(tri[:, :], k_late[:, 512:640]).then_inc(late_in, 16)
                if b >= NB and k == 9:
                    cb = b - NB
                    act.wait_ge(row_bc, cb + 1)
                    if cb >= 2:
                        act.wait_ge(h_ready, 2 * (cb - 1))
                    a(part[:, cb % 2, :], bank[4 + cb % 2][:, :], ACT.Copy).then_inc(row_act, 1)
                if b > NB and k == 5:
                    keep_stream(b - NB - 1)
                if b > NB and k in (3, 4):
                    cb, t = b - 1 - NB, k - 3
                    act.wait_ge(h_ready, 2 * cb + t + 1)
                    a(tmp[:, t, :], h[:, t, 512 * cb:512 * cb + 512], ACT.Square,
                      accum_out=ss[:, 4 * t + cb:4 * t + cb + 1]).then_inc(h_sq, 1)
        for t in range(2):
            act.wait_ge(h_ready, 2 * NO - 1 + t)
            a(tmp[:, t, :], h[:, t, 1536:2048], ACT.Square, accum_out=ss[:, 4 * t + 3:4 * t + 4]).then_inc(h_sq, 1)
        keep_stream(NO - 1)
        act.wait_ge(rstd_ok, 2)
        a(h2n[:, 0, :], h[:, 0, :], ACT.Copy, scale=rs[:, 0:1]).then_inc(h2_act, 1)
        act.wait_ge(r_dve, 1)
        a(aff[:, :, :], aff[:, :, :], ACT.Exp).then_inc(r_act, 1)
        a(h2n[:, 1, :], h[:, 1, :], ACT.Copy, scale=rs[:, 1:2]).then_inc(h2_act, 1)
        act.wait_ge(chunk_used, CHUNKS * (NB + NO))
        for cb in range(4):
            act.wait_ge(row_bc, NO + cb + 1)
            a(m5[:, 512 * cb:512 * cb + 512], bank[(6, 7, 2, 3)[cb]][:, :], ACT.Copy).then_inc(row_act, 1)
        act.dma_start(fwb[:, :], fw.partition_broadcast(P)).then_inc(fw_in, 16)
        act.wait_ge(r_pe, 6)
        a(tg[:, 0:2, :], bank[6][:, :].rearrange("p (g n) -> p g n", g=2), ACT.Copy).then_inc(r_act, 1)

        with act.Fori(0, 4) as g:
            for j in range(4):
                act.wait_ge(gathered, g * 4 + (j + 1))
                for k in (4 * j, 4 * j + 2):
                    a(xg[:, k, :], bank[2 + j % 2][:, P * (k % 4):P * (k % 4) + P], ACT.Identity, scale=a2[:, k:k + 1],
                      bias=modc[:, 2, k, 0:1]).then_inc(xg_act, 1)
            for ei in range(4):
                for m in range(2):
                    act.wait_ge(moe_used, g * 96 + (24 * ei + 8 * m + 8))
                    if m == 0:
                        act.wait_ge(summed, g * 4 + (ei + 1))
                    a(gup[:, 2 * m, :], bank[2 * m][:, :], ACT.Copy).then_inc(gu_act, 1)
                act.wait_ge(summed, g * 4 + (ei + 2))
                act.wait_ge(hid_ok, g * 4 + (ei + 1))
                a(sgate[:, :, :], bank[4][:, 0:SEQ].rearrange("p (f n) -> p f n", f=FC), ACT.Silu).then_inc(silu_ok, 1)
        for i in range(8):
            cb, t = i // 2, i % 2
            act.wait_ge(comb_add, E * 8 - 8 + i + 2)
            a(ring[:, 0, 512 * t:512 * t + 512], h[:, t, 512 * cb:512 * cb + 512], ACT.Square,
              accum_out=ss[:, 4 * t + cb:4 * t + cb + 1]).then_inc(f_sq_a, 1)
            if i >= 1:
                act.wait_ge(f_sq_a, i)
        act.wait_ge(f_pre, 6)
        act.wait_ge(f_rstd, 1)
        a(h2n[:, 0, 0:1024], h2n[:, 0, 0:1024], ACT.Copy, scale=rs[:, 0:1]).then_inc(f_out_a, 1)

    @block.vector
    def _(dve):
        v = nc.vector
        links = [0]

        def link(ins):
            links[0] += 1
            ins.then_inc(dve_link, 1)
            dve.wait_ge(dve_link, links[0])

        for t in range(4):
            dve.wait_ge(squares, t + 1)
        v.tensor_scalar(rs[:, 4:8], ss[:, 0:4], 1.0 / D, EPS, ALU.mult, ALU.add).then_inc(mean_sq, 1)
        dve.wait_ge(rstd_ok, 1)
        for t in range(4):
            v.tensor_scalar(xin[:, t, :], xin[:, t, :], rs[:, t:t + 1], None, ALU.mult).then_inc(normed, 1)
        dve.wait_ge(small_in, 16 * 11)
        decs = dec[:, :, :].rearrange("p a b -> p (a b)")
        link(v.tensor_scalar(lg[:, 3, :], decs, -1.0, None, ALU.mult))
        v.tensor_tensor(lg[:, 0, :], lg[:, 3, :], decs, ALU.max).then_inc(lg_dve, 1)
        dve.wait_ge(lg_act, 1)
        link(v.tensor_scalar(lg[:, 0, :], decs, 0.0, None, ALU.min))
        v.tensor_tensor(lg[:, 3, :], lg[:, 0, :], lg[:, 2, :], ALU.subtract).then_inc(lg_dve, 1)

        def keep_tokens(k):
            dve.wait_ge(x_turned, k + 1)
            v.tensor_copy(xnT[:, k, :], bank[k % 4][:, :]).then_inc(xt_dve, 1)

        def mask_bias(j):
            dve.wait_ge(bias_pe, j + 1)
            bv = bias[:, :, :, :].rearrange("p h s c -> p (h s) c")
            v.tensor_tensor(bv[:, 8 * j:8 * j + 8, :], bank[6][:, :].rearrange("p (s c) -> p s c", s=8),
                            window[:, 0:GRID_W].unsqueeze(1).broadcast_to([P, 8, GRID_W]), ALU.add).then_inc(bias_ok, 1)

        def mod_part(i):
            dve.wait_ge(mod_item_used, 8 * i + 8)
            if i:
                dve.wait_ge(mod_small, i)
            v.tensor_copy(part[:, 1, :], bank[5][:, :]).then_inc(part_dve, 1)

        def mod_finish(i):
            gi = mod_order[i]
            dve.wait_ge(mod_small, i + 1)
            m = gi // 2
            if m in (2, 5):
                for half in range(2):
                    r = 32 * (2 * (gi % 2) + half)
                    last = v.tensor_tensor(mrow[r:r + 1, m // 3, :], mrow[r:r + 1, m // 3, :], bank[7][r:r + 1, :], ALU.add)
                last.then_inc(mod_add, 1)
            else:
                mi = {0: 0, 1: 1, 3: 2, 4: 3}[m]
                k0 = 8 * (gi % 2)
                v.tensor_tensor(modc[:, mi, k0:k0 + 8, :], bank[7][:, 0:16].rearrange("p (k c) -> p k c", c=2),
                                bcol[:, mi, k0:k0 + 8].unsqueeze(2).broadcast_to([P, 8, 2]), ALU.add).then_inc(mod_add, 1)

        def mod_multiply(i, k):
            gi = mod_order[i]
            if k == 0:
                dve.wait_ge(mod_small, i)
            if k % 2 == 0:
                wait_item(dve, ("mod", gi, k // 2))
            n = item_at["mod", gi, k // 2]
            w = ring[:, slot[n], 1024 * (k % 2):1024 * (k % 2) + 1024]
            acc = part[:, :, :].rearrange("p a n -> p (a n)")
            if k == 0:
                ins = v.tensor_scalar(acc, w, csT[:, k, 0:1], None, ALU.mult)
            else:
                dve.wait_ge(mod_mac, KC * (i - MOD_BEFORE) + k)
                ins = v.scalar_tensor_tensor(out=acc, in0=w, scalar=csT[:, k, 0:1], in1=acc, op0=ALU.mult, op1=ALU.add)
            ins.then_inc(mod_mac, 1)

        def norm_scale(h0):
            dve.wait_ge(mod_add, 2 if h0 == 0 else 4)
            for i in range(2):
                last = v.scalar_tensor_tensor(out=acol[:, i, h0:h0 + 8], in0=modc[:, 1, h0:h0 + 8, i], scalar=1.0,
                                              in1=nmc[:, h0:h0 + 8], op0=ALU.add, op1=ALU.mult)
            last.then_inc(a_ready, 1)
            dve.wait_ge(a_ready, h0 // 8 + 1)

        def split(b, k):
            cidx = CHUNKS * b + k
            n = item_at["w", b, k // 4]
            dve.wait_ge(hi_split, cidx + 1)
            v.tensor_tensor(whl[:, cidx % (AHEAD + 1), 1, :], ring[:, slot[n], 512 * (k % 4):512 * (k % 4) + 512],
                            whl[:, cidx % (AHEAD + 1), 0, :].bitcast(F32), ALU.subtract).then_inc(lo_split, 1)

        def evacuate(b):
            kind = BLOCKS[b][0][0]
            for t in range(1, tiles_of(b), 2):
                wait_projected(dve, b, t)
                if kind in "kq":
                    dst = tmp[:, t, :]
                    if kq_blocks.index(b):
                        dve.wait_ge(kq_turned, n_kq[b])
                else:
                    dst = (vv if kind == "v" else gg)[:, t, :]
                    if kind == "v" and b == 5:
                        dve.wait_ge(na_out, 4)
                    if kind == "v" and b == 8:
                        dve.wait_ge(na_out, 8)
                    if kind == "v" and b == 12:
                        dve.wait_ge(ret_out, 4)
                v.tensor_copy(dst, bank[bank_of(b, t)][:, :]).then_inc(ev_dve, 1)

        def key_tile(b, t):
            dve.wait_ge(kq_turned, n_kq[b] + t + 1)
            src = bank[6 + (n_kq[b] + t) % 2][:, :].rearrange("p (h n) -> p h n", h=4)
            v.tensor_copy(kT[:, :, P * t:P * t + P], src).then_inc(kq_dve, 1)

        def na_bias(g, u):
            n = 8 * g + u
            hn, qt = 4 * g + u // 2, u % 2
            if n == 0:
                dve.wait_ge(bias_ok, 6)
            dve.wait_ge(na_score, n + 1)
            if n >= 2:
                dve.wait_ge(na_turned, n - 1)
            s = 2 * (1 - qt)
            v.tensor_tensor(pb[:, u % 2, 0:SEQ], bank[4 + u % 2][:, 0:SEQ],
                            bias[:, hn, s:s + 4, :].rearrange("p a b -> p (a b)"), ALU.add)
            link(v.tensor_copy(pb[:, u % 2, SEQ:512], bank[4 + u % 2][:, SEQ:512]))
            link(v.tensor_reduce(prec[:, n % 4:n % 4 + 1], pb[:, u % 2, :], AX_X, ALU.max))
            v.tensor_scalar(nmax[:, n % 4:n % 4 + 1], prec[:, n % 4:n % 4 + 1], -1.0, None, ALU.mult).then_inc(na_biased, 1)

        def na_normal(g, u):
            n = 8 * g + u
            dve.wait_ge(na_exp, n + 1)
            link(v.reciprocal(prec[:, n % 4:n % 4 + 1], psumm[:, n % 4:n % 4 + 1]))
            v.tensor_scalar(pb[:, u % 2, :], pb[:, u % 2, :], prec[:, n % 4:n % 4 + 1], None, ALU.mult).then_inc(na_norm, 1)

        def ret_mask(g, hh):
            n = 4 * g + hh
            dve.wait_ge(ret_score, n + 1)
            dve.wait_ge(masks, n + 1)
            if n >= 2:
                dve.wait_ge(ret_out, n - 1)
            for kt in range(4):
                o = P * (1 - kt % 2)
                last = v.tensor_tensor(pT[:, hh % 2, kt, :], bank[4 + kt // 2][:, SEQ * (kt % 2):SEQ * (kt % 2) + SEQ],
                                       wmask[:, hh % 2, kt // 2, o:o + SEQ], ALU.mult)
            last.then_inc(ret_masked, 1)

        def head_moments(g, hh):
            dve.wait_ge(ret_kept, 4 * g + hh + 1)
            for it in range(2):
                last = v.bn_stats(bst[:, 2 * hh + it, :], pb[:, it, P * hh:P * hh + P])
            last.then_inc(ret_stats, 1)

        def ret_moments(g):
            head_moments(g, 3)
            dve.wait_ge(ret_stats, 4 * g + 4)
            for i in range(8):
                last = v.bn_aggr(mv[:, i, :], bst[:, i, :])
            link(last)
            v.tensor_scalar(rg[:, :], mv[:, :, 1], EPS, None, ALU.add).then_inc(ret_var, 1)

        def ret_normal(g):
            dve.wait_ge(ret_rstd, g + 1)
            for hh in range(4):
                for it in range(2):
                    i = 2 * hh + it
                    last = v.tensor_scalar(pb[:, it, P * hh:P * hh + P], pb[:, it, P * hh:P * hh + P], mv[:, i, 0:1],
                                           rg[:, i:i + 1], ALU.subtract, ALU.mult)
            link(last)

        def ret_gate(g):
            dve.wait_ge(gate_act, g + 1)
            v.tensor_tensor(pb[:, :, :], pb[:, :, :], gg[:, :, :], ALU.mult).then_inc(ret_gated, 1)

        def ret_mixed(g, half):
            dve.wait_ge(ret_turned, g + 1)
            dve.wait_ge(ret_mix_a, 2 * g + half + 1)
            hn = 9 + 4 * g + 2 * half
            v.tensor_scalar(mixT[:, hn, :], bank[6 + half][:, SEQ:512], gnc[:, hn - 8:hn - 7], None, ALU.mult).then_inc(ret_mix_d, 1)

        def router_weights():
            link(v.scalar_tensor_tensor(out=a2[:, :], in0=modc[:, 3, :, 0], scalar=1.0, in1=nfc[:, :], op0=ALU.add, op1=ALU.mult))
            link(v.tensor_tensor(wrb, wr[:, :, :], modc[:, 2, :, 0:1].broadcast_to([P, KC, E]), ALU.mult))
            v.tensor_reduce(shift_sum, wrb.rearrange("p k e -> p e k"), AX_X, ALU.add).then_inc(shift_in, 1)
            link(v.tensor_tensor(wr[:, :, :], wr[:, :, :], a2[:, :].unsqueeze(2).broadcast_to([P, KC, E]), ALU.mult))
            dve.wait_ge(shift_pe, 1)
            v.tensor_copy(shift_lg, bank[6][:, 0:E])
            v.memset(ones_b[:, :], 1.0).then_inc(a_ready, 1)

        def keep_stream(cb):
            dve.wait_ge(h_turned, cb + 1)
            src = bank[1 if cb == NO - 1 else 7][:, :].rearrange("p (k n) -> p k n", k=2)
            v.tensor_copy(hTT[:, 4 * cb + 2:4 * cb + 4, :], src).then_inc(ht_dve, 1)

        def residual(cb):
            b = NB + cb
            dve.wait_ge(row_act, cb + 1)
            if cb == 0:
                dve.wait_ge(h_in, 32)
            for t in range(2):
                wait_projected(dve, b, t)
                link(v.tensor_tensor(tmp[:, 2 + t, :], bank[bank_of(b, t)][:, :], part[:, cb % 2, :], ALU.mult))
                v.tensor_tensor(h[:, t, 512 * cb:512 * cb + 512], h[:, t, 512 * cb:512 * cb + 512], tmp[:, 2 + t, :],
                                ALU.add).then_inc(h_ready, 1)

        def ahead(cidx):
            b, k = divmod(cidx, KC)
            if b == 0:
                v.tensor_scalar(xnT[:, k, 0:SEQ], xnT[:, k, 0:SEQ], acol[:, 0, k:k + 1], modc[:, 0, k, 0:1],
                                ALU.mult, ALU.add).then_inc(u_aff, 1)
            split(b, k)
            if b == 0:
                dve.wait_ge(uh_ok, k + 1)
                v.tensor_tensor(ul[:, k, :], xnT[:, k, :], uh[:, k, :].bitcast(F32), ALU.subtract).then_inc(ul_ok, 1)
            if b == NB:
                dve.wait_ge(mh_ok, k + 1)
                dve.wait_ge(chunk_used, CHUNKS * (NB - 1) + KC // 2 + k // 2 + 1)
                v.tensor_tensor(ml[:, k, :], mixT[:, k, :], mh[:, k, :].bitcast(F32), ALU.subtract).then_inc(ml_ok, 1)

        mod_part(0)
        keep_tokens(1)
        mod_finish(0)
        for k in range(3, KC, 2):
            keep_tokens(k)
        mod_part(1)
        mod_finish(1)
        norm_scale(0)
        dve.wait_ge(xt_act, 8)
        dve.wait_ge(xt_dve, 8)
        for cidx in range(5):
            ahead(cidx)
        mod_part(2)
        mod_finish(2)
        for cidx in range(5, EARLY):
            ahead(cidx)
        mod_part(3)
        mod_finish(3)
        norm_scale(8)
        for b in range(NB + NO):
            prev = b - 1
            for k in range(EARLY - AHEAD if b == 0 else 0, KC):
                if k == 0 and 0 <= prev < NB:
                    evacuate(prev)
                if prev in RET_BLOCKS and k == 9:
                    ret_mixed(RET_BLOCKS[prev], 0)
                    ret_mixed(RET_BLOCKS[prev], 1)
                if b in NA_BLOCKS:
                    g = NA_BLOCKS[b]
                    if 4 <= k < 12:
                        na_bias(g, k - 4)
                    if 5 <= k < 13:
                        na_normal(g, k - 5)
                if CHUNKS * b + k + AHEAD < CHUNKS * (NB + NO):
                    ahead(CHUNKS * b + k + AHEAD)
                if k == 2 and prev >= NB:
                    residual(prev - NB)
                if b == NB + 1 and k == 8:
                    router_weights()
                if b > NB and k == 5:
                    keep_stream(b - NB - 1)
                if k == 1 and prev in MOD_DONE:
                    mod_finish(mod_order.index(MOD_DONE[prev]))
                if mod_step(b, k):
                    mod_multiply(mod_order.index(mod_step(b, k)[0]), mod_step(b, k)[1])
                if b == 2 and 8 <= k < 14:
                    mask_bias(k - 8)
                if prev in kq_blocks and BLOCKS[prev][0][0] == "k" and 4 <= k < 8:
                    key_tile(prev, k - 4)
                if b in RET_BLOCKS:
                    g = RET_BLOCKS[b]
                    if k in (5, 8, 11, 14):
                        ret_mask(g, (k - 5) // 3)
                    if k in (9, 12, 15):
                        head_moments(g, (k - 9) // 3)
                if prev in RET_BLOCKS and k == 3:
                    ret_moments(RET_BLOCKS[prev])
                if prev in RET_BLOCKS and k == 5:
                    ret_normal(RET_BLOCKS[prev])
                if prev in RET_BLOCKS and k == 7:
                    ret_gate(RET_BLOCKS[prev])
        residual(NO - 1)
        dve.wait_ge(h_sq, 2 * NO)
        link(v.tensor_reduce(rs[:, 2:4], ss[:, :].rearrange("p (t c) -> p t c", t=2), AX_X, ALU.add))
        v.tensor_scalar(rs[:, 4:6], rs[:, 2:4], 1.0 / D, EPS, ALU.mult, ALU.add).then_inc(mean_sq, 1)
        keep_stream(NO - 1)
        dve.wait_ge(late_in, 32)
        v.tensor_copy(tri_b[:, :], tri[:, :])
        dve.wait_ge(rstd_ok, 2)
        dve.wait_ge(r_pe, 1)
        for t in range(2):
            last = v.scalar_tensor_tensor(out=aff[:, t, :], in0=bank[4 + t][:, 0:E], scalar=rs[:, t:t + 1],
                                          in1=shift_lg, op0=ALU.mult, op1=ALU.add)
        link(last)
        link(v.tensor_reduce(rmax, aff[:, :, :], AX_X, ALU.max))
        v.tensor_tensor(aff[:, :, :], aff[:, :, :], rmax.unsqueeze(2).broadcast_to([P, 2, E]),
                        ALU.subtract).then_inc(r_dve, 1)
        dve.wait_ge(r_act, 1)
        link(v.tensor_reduce(rsum, aff[:, :, :], AX_X, ALU.add))
        link(v.reciprocal(rmax, rsum))
        v.tensor_tensor(aff[:, :, :], aff[:, :, :], rmax.unsqueeze(2).broadcast_to([P, 2, E]), ALU.mult).then_inc(r_dve, 1)
        dve.wait_ge(r_pe, 2)
        v.tensor_copy(affT[0:E, 0, :], bank[0][0:E, 0:SEQ])
        link(v.tensor_copy(affT[0:E, 3, :], bank[0][0:E, 0:SEQ]))
        for i in range(4):
            link(v.max(top8[0:E, 8 * i:8 * i + 8], affT[0:E, 3, :]))
            if i < 3:
                link(v.match_replace(affT[0:E, 3, :], top8[0:E, 8 * i:8 * i + 8], affT[0:E, 3, :], -1.0))
        v.tensor_scalar(affT[0:E, 1, :], affT[0:E, 0, :], top8[0:E, 31:32], None, ALU.is_gt)
        v.tensor_scalar(affT[0:E, 2, :], affT[0:E, 0, :], top8[0:E, 31:32], None, ALU.is_equal).then_inc(r_dve, 1)
        dve.wait_ge(r_pe, 3)
        gts_ps = bank[1][:, 0:4 * E].rearrange("p (i t e) -> p i t e", i=2, t=2)
        v.tensor_copy(gt_b, gts_ps[:, 0])
        v.tensor_copy(gts, gts_ps[:, 0])
        v.tensor_copy(slotm, gts_ps[:, 1])
        v.tensor_copy(eq_b, gts_ps[:, 1]).then_inc(r_dve, 1)
        dve.wait_ge(r_dve, 4)
        dve.wait_ge(r_pe, 4)
        ps_t = bank[4][:, 0:2 * E].rearrange("p (t e) -> p t e", t=2)
        link(v.tensor_scalar(sels, ps_t, float(CAP), None, ALU.is_le))
        link(v.tensor_tensor(sels, sels, slotm, ALU.mult))
        link(v.tensor_tensor(sels, sels, gts, ALU.add))
        v.tensor_copy(sel_b, sels).then_inc(r_dve, 1)
        dve.wait_ge(r_pe, 5)
        ps_s = bank[5][:, 0:2 * E].rearrange("p (t e) -> p t e", t=2)
        link(v.tensor_tensor(slotm, ps_s, sels, ALU.mult))
        for t in range(2):
            last = v.tensor_tensor(oh[:, t, :].rearrange("p (e s) -> p e s", e=E),
                                   slotm[:, t, :].unsqueeze(2).broadcast_to([P, E, CAP]),
                                   slots.unsqueeze(1).broadcast_to([P, E, CAP]), ALU.is_equal)
        link(last)
        for t in range(2):
            last = v.tensor_tensor(oha[:, t, :].rearrange("p (e s) -> p e s", e=E),
                                   oh[:, t, :].rearrange("p (e s) -> p e s", e=E),
                                   aff[:, t, :].unsqueeze(2).broadcast_to([P, E, CAP]), ALU.mult)
        last.then_inc(r_dve, 1)
        dve.wait_ge(r_pe, 6)
        v.tensor_copy(tg[:, 2:4, :], bank[7][:, :].rearrange("p (g n) -> p g n", g=2)).then_inc(r_dve, 1)

        for credit in (y_ok, g_ok, hid_ok, comb_add):
            dve.sem_inc(credit, 1)
        with dve.Fori(0, 4) as g:
            for j in range(4):
                dve.wait_ge(gathered, g * 4 + (j + 1))
                dve.wait_ge(xg_act, g * 8 + (2 * j + 2))
                for k in (4 * j + 1, 4 * j + 3):
                    v.tensor_scalar(xg[:, k, :], bank[2 + j % 2][:, P * (k % 4):P * (k % 4) + P], a2[:, k:k + 1],
                                    modc[:, 2, k, 0:1], ALU.mult, ALU.add).then_inc(xg_dve, 1)
            for ei in range(4):
                for m in range(2):
                    dve.wait_ge(moe_used, g * 96 + (24 * ei + 8 * m + 8))
                    if m == 0:
                        dve.wait_ge(summed, g * 4 + (ei + 1))
                    v.tensor_copy(gup[:, 2 * m + 1, :], bank[2 * m + 1][:, :]).then_inc(gu_dve, 1)
                dve.wait_ge(g_pe, g * 4 + (ei + 1))
                dve.wait_ge(comb, g * 32 + (8 * ei + 1))
                v.tensor_copy(gcur[:, :], bank[5][:, 0:SEQ]).then_inc(g_ok, 1)
                dve.wait_ge(silu_ok, g * 4 + (ei + 1))
                v.tensor_tensor(hT[:, :, :], sgate[:, :, :], bank[4][:, SEQ:512].rearrange("p (f n) -> p f n", f=FC),
                                ALU.mult).then_inc(hid_ok, 1)
                for cb in range(5):
                    if cb < 4:
                        dve.wait_ge(moe_used, g * 96 + (24 * ei + 2 * cb + 18))
                        v.tensor_tensor(yy[:, cb, :], bank[cb][:, :], m5[:, 512 * cb:512 * cb + 512], ALU.mult).then_inc(y_ok, 1)
                    for t in range(2) if cb else ():
                        i = 2 * (cb - 1) + t
                        dve.wait_ge(comb, g * 32 + (8 * ei + i + 2))
                        hs = h[:, t, 512 * (cb - 1):512 * cb]
                        ps = bank[cb - 1] if t else bank[6 + (cb - 1) % 2]
                        v.tensor_tensor(hs, hs, ps[:, :], ALU.add).then_inc(comb_add, 1)
        dve.wait_ge(comb_add, E * 8 + 1)
        dve.wait_ge(fw_in, 16)
        dve.wait_ge(gathered, 16)
        for t in range(2):
            link(v.tensor_tensor(h2n[:, t, 1536:2048], h[:, t, 1536:2048], fwb[:, 1536:2048], ALU.mult))
        dve.wait_ge(f_sq_a, 8)
        link(v.tensor_reduce(rs[:, 2:4], ss[:, :].rearrange("p (t c) -> p t c", t=2), AX_X, ALU.add))
        v.tensor_scalar(rs[:, 4:6], rs[:, 2:4], 1.0 / D, EPS, ALU.mult, ALU.add).then_inc(f_mean, 1)
        dve.wait_ge(f_pre, 6)
        dve.wait_ge(f_rstd, 1)
        for t, half in ((1, 0), (1, 1), (0, 1)):
            cs = slice(1024 * half, 1024 * half + 1024)
            v.tensor_scalar(h2n[:, t, cs], h2n[:, t, cs], rs[:, t:t + 1], None, ALU.mult).then_inc(f_out, 1)

    @block.gpsimd
    def _(pool):
        gp = nc.gpsimd
        links = [0]

        def link(ins):
            links[0] += 1
            ins.then_inc(pool_link, 1)
            pool.wait_ge(pool_link, links[0])

        gp.memset(pad[:, :], 0.0).then_inc(pool_init, 1)
        gp.memset(csT[:, :, :], 0.0).then_inc(pool_init, 1)
        gp.memset(ones[:, :], 1.0).then_inc(pool_init, 1)
        link(gp.memset(mhalf[:, :], -0.5))
        pool.wait_ge(mean_sq, 1)
        gp.tensor_tensor(rs[:, 0:4], rs[:, 4:8], mhalf[:, 0:4], ALU.pow).then_inc(rstd_ok, 1)

        def rope(b, t):
            wait_evacuated(pool, b, t)
            if n_rope[b] + t:
                pool.wait_ge(roped, n_rope[b] + t)
            tv = tmp[:, t, :].rearrange("p (h a f e) -> p h a f e", h=4, a=2, f=2)
            rv = ropet[:, :].rearrange("p (h a f e) -> p h a f e", h=4, a=2, f=2)
            sv = sinT[:, t, :].rearrange("p (a f e) -> p a f e", a=2, f=2)
            for f in range(2):
                swapped = gp.tensor_tensor(rv[:, :, :, f], tv[:, :, :, 1 - f],
                                           sv[:, :, f].unsqueeze(1).broadcast_to([P, 4, 2, 32]), ALU.mult)
            link(swapped)
            link(gp.tensor_tensor(tmp[:, t, :].rearrange("p (h d) -> p h d", h=4),
                                  tmp[:, t, :].rearrange("p (h d) -> p h d", h=4),
                                  cosT[:, t, :].unsqueeze(1).broadcast_to([P, 4, P]), ALU.mult))
            gp.tensor_tensor(tmp[:, t, :], tmp[:, t, :], ropet[:, :], ALU.add).then_inc(roped, 1)

        def mask(n):
            pool.wait_ge(powers, 2 * n + 2)
            if n:
                pool.wait_ge(masks, n)
            if n >= 2:
                pool.wait_ge(ret_masked, n - 1)
            if n == 0:
                pool.wait_ge(na_biased, 16)
                pool.wait_ge(decay_in, 16)
            link(gp.tensor_tensor(wmask[:, n % 2, 1, :], gfb[:, 0, 256:640], gfb[:, 1, 0:384], ALU.add))
            gp.tensor_tensor(gfb[:, 0, 0:384], gfb[:, 0, 0:384], decay[:, 1280:1664], ALU.mult)
            link(gp.tensor_tensor(gfb[:, 1, 256:640], gfb[:, 1, 256:640], decay[:, 1664:2048], ALU.mult))
            gp.tensor_tensor(wmask[:, n % 2, 0, :], gfb[:, 0, 0:384], gfb[:, 1, 256:640], ALU.add).then_inc(masks, 1)

        for b in range(NB):
            if b in kq_blocks and BLOCKS[b][0][1] == "r":
                rope(b, 0)
                rope(b, 1)
            if b + 1 in RET_BLOCKS:
                mask(4 * RET_BLOCKS[b + 1])
            if b in RET_BLOCKS:
                for hh in range(1, 4):
                    mask(4 * RET_BLOCKS[b] + hh)
                pool.wait_ge(ret_var, RET_BLOCKS[b] + 1)
                gp.tensor_tensor(rg[:, :], rg[:, :], mhalf[:, :], ALU.pow).then_inc(ret_rstd, 1)
        pool.wait_ge(mean_sq, 2)
        gp.tensor_tensor(rs[:, 0:2], rs[:, 4:6], mhalf[:, 0:2], ALU.pow).then_inc(rstd_ok, 1)
        pool.wait_ge(fw_in, 16)
        pool.wait_ge(gathered, 16)
        for i in range(6):
            cb, t = i // 2, i % 2
            pool.wait_ge(comb_add, E * 8 - 8 + i + 2)
            cs = slice(512 * cb, 512 * cb + 512)
            gp.tensor_tensor(h2n[:, t, cs], h[:, t, cs], fwb[:, cs], ALU.mult).then_inc(f_pre, 1)
        pool.wait_ge(f_mean, 1)
        gp.tensor_tensor(rs[:, 0:2], rs[:, 4:6], mhalf[:, 0:2], ALU.pow).then_inc(f_rstd, 1)

    es.close()


def kernel(**inputs):
    import concourse.bacc as bacc
    from concourse.bass_utils import run_bass_kernel_spmd

    def cols(a):
        a = np.asarray(a)
        return np.ascontiguousarray(a.reshape(-1, P).T)

    consts = host_constants()
    b_mod = np.asarray(inputs["b_mod"]).reshape(6, D)
    arrays = {
        "x": inputs["x"], "c": cols(inputs["c"]), "ctx": inputs["ctx"], "c_ctx": cols(inputs["c_ctx"]),
        "w_mod": inputs["w_mod"],
        "b_col": np.ascontiguousarray(b_mod[[0, 1, 3, 4]].reshape(4, KC, P).transpose(2, 0, 1)),
        "b_row": np.ascontiguousarray(b_mod[[2, 5]].reshape(2, 4, 512)),
        "nm": cols(inputs["norm_mix_w"]), "nf": cols(inputs["norm_ffn_w"]), "w_in": inputs["w_in"],
        "rpb": inputs["na_rpb"], "dec_f": np.asarray(inputs["ret_decay_fwd"]).reshape(8),
        "dec_b": np.asarray(inputs["ret_decay_bwd"]).reshape(8), "gn": cols(inputs["ret_gn_w"]),
        "w_out": inputs["w_out"], "w_router": inputs["w_router"], "w_gate": inputs["w_gate"],
        "w_up": inputs["w_up"], "w_down": inputs["w_down"], "fw": inputs["final_norm_w"],
        "k_decay": consts["decay"], "k_small": consts["small"], "k_window": consts["window"], "k_late": consts["late"],
    }
    nc = bacc.Bacc("TRN2", target_bir_lowering=False, num_devices=1)
    feeds, args = {}, []
    for name, a in arrays.items():
        a = np.ascontiguousarray(a)
        feeds[f"in_{name}"] = a
        args.append(nc.dram_tensor(f"in_{name}", a.shape, mybir.dt.from_np(a.dtype), kind="ExternalInput").ap())
    args.append(nc.dram_tensor("out_0", (1, SEQ, D), F32, kind="ExternalOutput").ap())
    build(nc, *args)
    r = run_bass_kernel_spmd(nc, [feeds], core_ids=[0])
    return r.results[0]["out_0"]
```

```python
from contextlib import ExitStack

import concourse.bass as bass
import numpy as np
from concourse import mybir

F32 = mybir.dt.float32
F32R = mybir.dt.float32r
BF16 = mybir.dt.bfloat16
ALU = mybir.AluOpType
ACT = mybir.ActivationFunctionType
AX_X = mybir.AxisListType.X

P = 128
D = 2048
KC = D // P
SEQ = 256
GRID_W = 64
HD = 128
NEG = -1e30
EPS = 1e-6
SCALE = HD ** -0.5
E = 16
FF = 1024
CAP = 32
FC = FF // P

COL = {"kn": 0, "vn": 1024, "kr": 2048, "vr": 3072, "qn": 4096, "qr": 5120, "gr": 6144}
BLOCKS = [(kind, g) for fam in (("kn", "qn", "vn"), ("kr", "qr", "vr", "gr")) for g in range(2) for kind in fam]
NB = len(BLOCKS)
NO = D // 512
MOD_BEFORE = 4
PROJECT_AT = [-1, 0, 1, 2, 5, 6, 7, 8, 12, 13, 14, 15]
EARLY = len(PROJECT_AT)
W_AT = [-5, 1, 6]
MOD_STEPS = [(0, k) for k in range(EARLY, KC)] + [(1, k) for k in range(1, KC, 2)] + \
            [(b, k) for b in (2, 3) for k in range(KC)] + [(4, k) for k in range(8, KC, 2)] + \
            [(b, k) for b in (5, 6, 8, 10, 12) for k in range(KC)]
MOD_AT = {step: (MOD_BEFORE + n // KC, n % KC) for n, step in enumerate(MOD_STEPS)}
MOD_SUMS = {((b, k + 1) if k + 1 < KC else (b + 1, 0)): i for (b, k), (i, c) in MOD_AT.items() if c == KC - 1}
MOD_FINISH = {((b, k + 1) if k + 1 < KC else (b + 1, 0)): i for (b, k), i in MOD_SUMS.items()}
AHEAD = 2
CHUNKS = KC
NA_BLOCKS = {3: 0, 6: 1}
RET_BLOCKS = {9: 0, 13: 1}


def is_direct(b):
    return b < NB and BLOCKS[b][0] in ("kn", "qn")


def tiles_of(b):
    return 4 if b < NB and (BLOCKS[b][0][0] in "kv" or is_direct(b)) else 2


def bank_of(b, t):
    return t + (2 if b >= NB and (b - NB) % 2 == 0 else 0)


def sums_by(b, k):
    return MOD_BEFORE + sum(1 for step in MOD_SUMS if step <= (b, k))


def stream_items():
    items = []
    for i in range(MOD_BEFORE):
        for q in range(8):
            items.append(("mod", i, q))
            if 8 * (i - 2) + q in W_AT:
                items.append(("w", 0, W_AT.index(8 * (i - 2) + q)))
    for b in range(NB + NO):
        for q in range(4):
            if ("w", b, q) not in items:
                items.append(("w", b, q))
            for k in range(4 * q, 4 * q + 4):
                if (b, k) in MOD_AT and MOD_AT[b, k][1] % 2 == 0:
                    i, c = MOD_AT[b, k]
                    if b == 0 and c == 2:
                        items.append(("w", 1, 0))
                    items.append(("mod", i, c // 2))
    return items


def host_constants():
    p = np.arange(P)[:, None].astype(np.float64)
    t = np.arange(-128, 512)[None, :]
    tb = np.arange(-384, 256)[None, :]
    tm = np.arange(-128, 256)[None, :]
    decay = np.concatenate([np.maximum(t - p, 0), np.maximum(p - tb, 0), t[:, :384] >= p, p >= tm], 1)
    ident = np.eye(P)
    freq = 10000.0 ** (-np.arange(0, 64, 2, dtype=np.float32) / np.float32(64))
    cos, sin = [], []
    for tile in range(2):
        tok = np.arange(P) + P * tile
        ar = (tok // GRID_W).astype(np.float32)[:, None] * freq.astype(np.float32)
        ac = (tok % GRID_W).astype(np.float32)[:, None] * freq.astype(np.float32)
        cos.append(np.concatenate([np.cos(ar), np.cos(ar), np.cos(ac), np.cos(ac)], 1))
        sin.append(np.concatenate([-np.sin(ar), np.sin(ar), -np.sin(ac), np.sin(ac)], 1))
    slots = np.tile(np.arange(1, CAP + 1), (P, 1))
    stack = np.tile(np.eye(CAP), (4, 1))
    sel = np.zeros((P, 2))
    sel[0::32, 0] = 1
    sel[1::32, 1] = 1
    small = np.concatenate([ident] + cos + sin + [slots, stack, sel], 1)
    cq = (np.arange(P) % GRID_W)[:, None]
    ck = np.arange(GRID_W)[None, :]
    start = np.clip(cq - 8, 0, GRID_W - 16)
    flip = np.zeros((P, P))
    flip[np.arange(P), (np.arange(P) // GRID_W) * GRID_W + GRID_W - 1 - np.arange(P) % GRID_W] = 1
    window = np.where((ck >= start) & (ck < start + 16), 0.0, NEG)
    spread = np.concatenate([np.tile(ident[:, 32 * e:32 * e + 32], (1, 4)) for e in range(4)], 1)
    late = np.concatenate([spread, np.triu(np.ones((P, P)))], 1)
    f = lambda a: np.ascontiguousarray(a.astype(np.float32))
    return {"decay": f(decay), "small": f(small), "window": f(np.concatenate([window, flip], 1)), "late": f(late)}


def build(nc, x, c, ctx, c_ctx, w_mod, b_col, b_row, nm, nf, w_in, rpb, dec_f, dec_b, gn, w_out, w_router,
          w_gate, w_up, w_down, fw, k_decay, k_small, k_window, k_late, out):
    es = ExitStack()

    def at(name, kib, shape, dt=F32):
        return nc.alloc_sbuf_tensor_at(name, [P, *shape], dt, offset=16512 + int(kib * 1024))

    ring = at("ring", 0, [8, 2048])
    ring_b = at("ring_b", 80, [2, 2048])
    ring_c = at("ring_c", 128, [2, 2048])
    xin = at("xin", 32, [4, D])
    kT = at("kT", 32, [4, 512])
    qT = at("qT", 40, [4, SEQ])
    vv = at("vv", 44, [4, 512])
    gg = at("gg", 52, [2, 512])
    pT = at("pT", 56, [2, 4, SEQ])
    junk = at("junk", 64, [D])
    uh = at("uh", 64, [KC, 512], F32R)
    mh = at("mh", 64, [KC, SEQ], F32R)
    ml = at("ml", 80, [KC, SEQ], F32R)
    xg = at("xg", 64, [KC, P])
    m5 = at("m5", 72, [D])
    xnT = at("xnT", 96, [KC, 512])
    ul = at("ul", 96, [KC, 512], F32R)
    h = at("h", 96, [2, D])
    h2n = at("h2n", 112, [2, D])
    mixT = at("mixT", 128, [KC, SEQ])
    hTT = at("hTT", 128, [KC, SEQ])
    whl = at("whl", 144, [3, 2, 512], F32R)
    gup = at("gup", 144, [4, 512])
    sgate = at("sgate", 152, [FC, CAP])
    hT = at("hT", 153, [FC, CAP])
    part = at("part", 156, [2, 512])
    affT = at("affT", 156, [4, SEQ])
    bias = at("bias", 160, [8, 6, GRID_W])
    wmask = at("wmask", 160, [2, 2, 384])
    gfb = at("gfb", 166, [2, 640])
    yy = at("yy", 160, [4, 512])
    oh = at("oh", 168, [2, 512])
    tmp = at("tmp", 172, [4, 512])
    oha = at("oha", 172, [2, P])
    tg = at("tg", 176, [SEQ])
    pb = at("pb", 180, [2, 512])
    gcur = at("gcur", 180, [SEQ])
    spread = at("spread", 181, [4, P])
    tri = at("tri", 183, [P])
    ropet = at("ropet", 184, [512])
    window = at("window", 184, [GRID_W + P])
    pad = at("pad", 185, [P])
    bias_r = at("bias_r", 128, [8 * 6 * GRID_W])
    rt = at("rt", 184, [512])
    mrow = at("mrow", 186, [2, 512])
    decay = at("decay", 190, [2048])
    wr_pad = at("wr_pad", 190, [KC, 32])
    lpart = at("lpart", 192, [SEQ])
    fwb = at("fwb", 190, [D])
    small = at("small", 198, [834])
    pos = [198 + 834 * 4 / 1024]

    def more(name, shape, dt=F32):
        n = int(np.prod(shape)) * (2 if dt == BF16 else 4)
        t_ = at(name, pos[0], shape, dt)
        pos[0] += -(-n // 32) * 32 / 1024
        return t_

    pos[0] = -(-int(pos[0] * 1024) // 32) * 32 / 1024
    csT = more("csT", [KC, 32])
    wr = more("wr", [KC, E])
    ones = more("ones", [P])
    tri_b = more("tri_b", [P], BF16)
    ones_b = more("ones_b", [P], BF16)
    modc = more("modc", [4, KC, 2])
    nmc = more("nmc", [KC])
    nfc = more("nfc", [KC])
    gnc = more("gnc", [8])
    bcol = more("bcol", [4, KC])
    cin = more("cin", [2, KC])
    dec = more("dec", [2, 8])
    lg = more("lg", [4, 16])
    acol = more("acol", [2, KC])
    a2 = more("a2", [KC])
    ss = more("ss", [8])
    rs = more("rs", [8])
    mhalf = more("mhalf", [8])
    nmax = more("nmax", [4])
    psumm = more("psumm", [4])
    prec = more("prec", [4])
    bst = more("bst", [8, 6])
    mv = more("mv", [8, 2])
    rg = more("rg", [8])
    assert pos[0] * 1024 + 16512 <= 229368
    ident = small[:, 0:128]
    cosT = small[:, 128:384].rearrange("p (t d) -> p t d", t=2)
    sinT = small[:, 384:640].rearrange("p (t d) -> p t d", t=2)
    slots = small[:, 640:672]
    stack = small[:, 672:704]
    sel = small[:, 704:706]
    wrb = rt[:, 256:512].rearrange("p (k e) -> p k e", k=KC)
    shift_sum, shift_lg = rt[:, 212:228], rt[:, 228:244]
    aff = rt[:, 0:32].rearrange("p (t e) -> p t e", t=2)
    rmax, rsum = rt[:, 32:34], rt[:, 34:36]
    gts = rt[:, 36:68].rearrange("p (t e) -> p t e", t=2)
    sels = rt[:, 68:100].rearrange("p (t e) -> p t e", t=2)
    slotm = rt[:, 100:132].rearrange("p (t e) -> p t e", t=2)
    top8 = rt[:, 132:164]
    eq_b = rt[:, 164:180].bitcast(BF16).rearrange("p (t e) -> p t e", t=2)
    gt_b = rt[:, 180:196].bitcast(BF16).rearrange("p (t e) -> p t e", t=2)
    sel_b = rt[:, 196:212].bitcast(BF16).rearrange("p (t e) -> p t e", t=2)

    bank = [es.enter_context(nc.psum_tensor(f"bank{i}", [P, 512], F32)) for i in range(8)]
    pad_dram = nc.dram_tensor("rpb_padded", (120, 128), F32, kind="Internal").ap()

    def sem(name):
        return es.enter_context(nc.semaphore(name))

    small_in = sem("small_in")
    cond_in = sem("cond_in")
    decay_in = sem("decay_in")
    late_in = sem("late_in")
    fw_in = sem("fw_in")
    pad_in = sem("pad_in")
    pad_out = sem("pad_out")
    bias_in = sem("bias_in")
    tok_in = [sem(f"tok_in{t}") for t in range(4)]
    ring_full = [sem(f"ring_full{i}") for i in range(12)]
    h_in = sem("h_in")
    out_done = sem("out_done")
    act_link, dve_link, pool_link = sem("act_link"), sem("dve_link"), sem("pool_link")
    squares, mean_sq, rstd_ok, normed = sem("squares"), sem("mean_sq"), sem("rstd_ok"), sem("normed")
    x_turned, xt_act, xt_dve = sem("x_turned"), sem("xt_act"), sem("xt_dve")
    pool_init, c_act = sem("pool_init"), sem("c_act")
    mod_item_used, part_act, part_dve = sem("mod_item_used"), sem("part_act"), sem("part_dve")
    mod_mac = sem("mod_mac")
    mod_small, mod_add, a_ready = sem("mod_small"), sem("mod_add"), sem("a_ready")
    lg_act, lg_dve = sem("lg_act"), sem("lg_dve")
    bias_pe, bias_ok = sem("bias_pe"), sem("bias_ok")
    u_aff, uh_ok, ul_ok = sem("u_aff"), sem("uh_ok"), sem("ul_ok")
    hi_split, lo_split, chunk_used, tile_done = sem("hi_split"), sem("lo_split"), sem("chunk_used"), sem("tile_done")
    ev_act, ev_dve, roped = sem("ev_act"), sem("ev_dve"), sem("roped")
    kq_turned, kq_act, kq_dve = sem("kq_turned"), sem("kq_act"), sem("kq_dve")
    na_score, na_biased, na_exp, na_norm = sem("na_score"), sem("na_biased"), sem("na_exp"), sem("na_norm")
    na_turned, na_pt, na_out, na_mix = sem("na_turned"), sem("na_pt"), sem("na_out"), sem("na_mix")
    powers, masks = sem("powers"), sem("masks")
    ret_score, ret_masked, ret_out, ret_kept = sem("ret_score"), sem("ret_masked"), sem("ret_out"), sem("ret_kept")
    gate_act, ret_var, ret_rstd, ret_gated = sem("gate_act"), sem("ret_var"), sem("ret_rstd"), sem("ret_gated")
    ret_stats = sem("ret_stats")
    ret_turned, ret_mix_a, ret_mix_d = sem("ret_turned"), sem("ret_mix_a"), sem("ret_mix_d")
    mh_ok, ml_ok = sem("mh_ok"), sem("ml_ok")
    row_bc, row_act, h_ready, h_sq = sem("row_bc"), sem("row_act"), sem("h_ready"), sem("h_sq")
    h2_act, h_turned, ht_act, ht_dve = sem("h2_act"), sem("h_turned"), sem("ht_act"), sem("ht_dve")
    shift_in, shift_pe = sem("shift_in"), sem("shift_pe")
    r_pe, r_dve, r_act = sem("r_pe"), sem("r_dve"), sem("r_act")
    lg_pe, lg_copied = sem("lg_pe"), sem("lg_copied")
    og_ok, og_pe, tg_ok = sem("og_ok"), sem("og_pe"), sem("tg_ok")
    moe_used, gathered, xg_act, xg_dve = sem("moe_used"), sem("gathered"), sem("xg_act"), sem("xg_dve")
    gu_act, gu_dve, summed, silu_ok, hid_ok = sem("gu_act"), sem("gu_dve"), sem("summed"), sem("silu_ok"), sem("hid_ok")
    g_pe, g_ok, y_ok, comb, comb_add = sem("g_pe"), sem("g_ok"), sem("y_ok"), sem("comb"), sem("comb_add")
    f_pre, f_out_a = sem("f_pre"), sem("f_out_a")
    f_sq_a, f_mean, f_rstd, f_out = sem("f_sq_a"), sem("f_mean"), sem("f_rstd"), sem("f_out")

    items = stream_items()
    n_items = len(items)
    item_at = {it: n for n, it in enumerate(items)}
    slot, fill, fills, free_at = [], [], [0] * 12, [-99] * 12
    multiplied_at = {MOD_AT[b, k]: CHUNKS * b + k for b, k in MOD_STEPS}
    for n, (kind, b, q) in enumerate(items):
        if kind == "w" and b == 0:
            s_ = (10, 11, 6, 7)[q]
        else:
            late = n > item_at["w", 0, 3]
            usable = [0, 1, 2, 3] + [6] * (late and n < item_at["w", 2, 2]) + [7] * (late and n < item_at["w", 3, 0])
            s_ = min(usable, key=lambda i: free_at[i])
        if kind == "w":
            free_at[s_] = CHUNKS * b + 4 * q + 3 - AHEAD
        elif b < MOD_BEFORE:
            free_at[s_] = 8 * (b - 2) + q - 4
        else:
            free_at[s_] = multiplied_at[b, 2 * q + 1]
        fills[s_] += 16
        slot.append(s_)
        fill.append(fills[s_])

    def wait_item(eng, item):
        n = item_at[item]
        eng.wait_ge(ring_full[slot[n]], fill[n])

    n_even = [sum((tiles_of(i) + 1) // 2 for i in range(b)) for b in range(NB + 1)]

    def wait_evacuated(eng, b, t):
        if b >= NB:
            eng.wait_ge(h_ready, 2 * (b - NB) + t + 1)
        else:
            eng.wait_ge(ev_dve if t % 2 else ev_act, n_even[b] + t // 2 + 1)

    last_user = {}
    before = {}
    for b in range(NB + NO):
        for t in range(tiles_of(b)):
            before[b, t] = last_user.get(bank_of(b, t))
            last_user[bank_of(b, t)] = (b, t)
    n_tile = [sum(tiles_of(i) - 1 for i in range(b)) for b in range(NB + NO + 1)]

    def wait_projected(eng, b, t):
        if t == tiles_of(b) - 1:
            eng.wait_ge(chunk_used, CHUNKS * (b + 1))
        else:
            eng.wait_ge(tile_done, n_tile[b] + t + 1)

    kq_blocks = [b for b in range(NB) if BLOCKS[b][0] in ("kr", "qr")]
    n_kq = {b: sum(tiles_of(i) for i in kq_blocks if i < b) for b in kq_blocks}
    n_kk = {b: sum(tiles_of(i) for i in kq_blocks if i < b and BLOCKS[i][0][0] == "k") for b in kq_blocks}
    n_qq = {b: n_kq[b] - n_kk[b] for b in kq_blocks}
    n_rope = {b: 2 * sum(1 for i in kq_blocks if i < b and BLOCKS[i][0][1] == "r") for b in kq_blocks}

    def wait_turned_read(eng, m):
        for b in kq_blocks:
            if n_kq[b] <= m < n_kq[b] + tiles_of(b):
                if BLOCKS[b][0][0] == "k":
                    eng.wait_ge(kq_dve, n_kk[b] + m - n_kq[b] + 1)
                else:
                    eng.wait_ge(kq_act, n_qq[b] + m - n_kq[b] + 1)

    moe_slots = [4, 5, 6, 7] + sorted(range(4), key=lambda i: free_at[i]) + [8, 9, 10, 11]
    RING = len(moe_slots)

    m5_bank = (6, 7, 2, 6)

    def slot_buf(s):
        return ring[:, s, :] if s < 8 else (ring_b if s < 10 else ring_c)[:, s % 2, :]

    wg_v = w_gate[0].rearrange("e (j k p) f -> e j p k f", p=P, k=2)
    wu_v = w_up[0].rearrange("e (j k p) f -> e j p k f", p=P, k=2)
    wd_v = w_down[0].rearrange("e (r k p) (j n) -> e j r p k n", p=P, r=2, n=512)
    win_v = w_in[0].rearrange("(k p) n -> p k n", p=P)
    wout_v = w_out[0].rearrange("(k p) n -> p k n", p=P)
    wmod_v = w_mod[0].rearrange("(k p) n -> p k n", p=P)
    x_v = x[0].rearrange("(t p) d -> t p d", p=P)
    ctx_v = ctx[0].rearrange("(t p) d -> t p d", p=P)
    out_v = out[0].rearrange("(t p) d -> t p d", p=P)

    block = es.enter_context(nc.Block())

    @block.sync
    def _(sp):
        for n, (kind, b, q) in enumerate(items):
            if fill[n] == 16 and slot[n] in (6, 7):
                sp.wait_ge(x_turned, KC)
            elif fill[n] > 16:
                k0, b0, q0 = items[max(i for i in range(n) if slot[i] == slot[n])]
                if k0 == "mod" and b0 < MOD_BEFORE:
                    sp.wait_ge(mod_item_used, 8 * b0 + q0 + 1)
                elif k0 == "mod":
                    sp.wait_ge(mod_mac, KC * (b0 - MOD_BEFORE) + 2 * q0 + 2)
                else:
                    sp.wait_ge(lo_split, CHUNKS * b0 + 4 * q0 + 4)
            if kind == "mod" and b < MOD_BEFORE:
                dst = slot_buf(slot[n]).rearrange("p (k c) -> p k c", k=4)
                c0 = D * (q // 4) + 512 * b
                src = wmod_v[:, 4 * (q % 4):4 * (q % 4) + 4, c0:c0 + 512]
            elif kind == "mod":
                dst = slot_buf(slot[n]).rearrange("p (k c) -> p k c", k=2)
                src = wmod_v[:, 2 * q:2 * q + 2, 1024 * b:1024 * b + 1024]
            else:
                dst = slot_buf(slot[n]).rearrange("p (k c) -> p k c", k=4)
                if b < NB:
                    c0 = COL[BLOCKS[b][0]] + 512 * BLOCKS[b][1]
                    src = win_v[:, 4 * q:4 * q + 4, c0:c0 + 512]
                else:
                    src = wout_v[:, 4 * q:4 * q + 4, 512 * (b - NB):512 * (b - NB) + 512]
            sp.dma_start(dst, src).then_inc(ring_full[slot[n]], 16)

        def expert_item(e, i):
            s = moe_slots[i % RING]
            what, j = i // 8, i % 8
            if what == 2:
                dst = slot_buf(s).rearrange("p (k c) -> p k c", k=4)
                src = wd_v[bass.ds(e, 1), j // 2, j % 2]
            else:
                dst = slot_buf(s).rearrange("p (k c) -> p k c", k=2)
                src = (wg_v, wu_v)[what][bass.ds(e, 1), j]
            sp.dma_start(dst, src.rearrange("a p k f -> (a p) k f")).then_inc(ring_full[s], 16)

        for i in range(RING):
            s = moe_slots[i]
            if i == 0:
                sp.wait_ge(ret_out, 8)
                sp.wait_ge(ret_gated, 2)
            if s < 4:
                _, b0, q0 = items[max(n for n in range(n_items) if slot[n] == s)]
                sp.wait_ge(lo_split, CHUNKS * b0 + 4 * q0 + 4)
            if s == 8:
                sp.wait_ge(chunk_used, CHUNKS * (NB + NO))
            if s == 10:
                sp.wait_ge(r_pe, 1)
            expert_item(0, i)
        with sp.Fori(0, E - 1) as e:
            for i in range(RING, RING + 24):
                if i == 15:
                    sp.wait_ge(moe_used, e * 24 + (i - RING + 2))
                elif i != 16:
                    sp.wait_ge(moe_used, e * 24 + (i - RING + 1))
                expert_item(e + 1 if i >= 24 else e, i % 24)
        for i in range(RING, 24):
            sp.wait_ge(moe_used, 24 * (E - 1) + i - RING + 1)
            expert_item(E - 1, i)
        for i, (t, half) in enumerate(((1, 0), (0, 0), (1, 1), (0, 1))):
            cs = slice(1024 * half, 1024 * half + 1024)
            if i == 1:
                sp.wait_ge(f_out_a, 1)
            else:
                sp.wait_ge(f_out, max(i, 1))
            sp.dma_start(out_v[t][:, cs], h2n[:, t, cs]).then_inc(out_done, 16)
        sp.wait_ge(out_done, 64)
        sp.wait_ge(pad_out, 16)

    @block.tensor
    def _(pe):
        mm = nc.tensor.matmul

        def mod_item(i, q):
            if i and q % 4 == 0:
                pe.wait_ge(part_dve if q else part_act, i)
            wait_item(pe, ("mod", i, q))
            w = slot_buf(slot[item_at["mod", i, q]]).rearrange("p (k c) -> p k c", k=4)
            for quad in range(4):
                last = mm(bank[4 + q // 4][32 * quad:32 * quad + 32, :], csT[:, 4 * (q % 4) + quad, :],
                          w[:, quad, :], start=q % 4 == 0, stop=q % 4 == 3)
            last.then_inc(mod_item_used, 1)

        def mod_sums(i):
            if i < MOD_BEFORE:
                pe.wait_ge(part_act, i + 1)
                pe.wait_ge(part_dve, i + 1)
                col = sel
            else:
                pe.wait_ge(mod_mac, KC * (i - MOD_BEFORE + 1))
                col = ones[:, 0:2]
            if i:
                pe.wait_ge(mod_add, i)
            for half in range(2):
                if i // 2 in (2, 5):
                    quad = 2 * (i % 2) + half
                    last = mm(bank[7][32 * quad:32 * quad + 1, :], col[:, 0:1], part[:, half, :], start=True, stop=True)
                else:
                    for j in range(4):
                        i2 = 4 * half + j
                        last = mm(bank[7][:, 2 * i2:2 * i2 + 2], part[:, half, P * j:P * j + P], col,
                                  start=True, stop=True)
            last.then_inc(mod_small, 1)

        def project(b, k):
            cidx = CHUNKS * b + k
            if b == 0:
                pe.wait_ge(ul_ok, k + 1)
            if b == NB:
                pe.wait_ge(ml_ok, k + 1)
            pe.wait_ge(lo_split, cidx + 1)
            wh, wl = whl[:, cidx % (AHEAD + 1), 0, :], whl[:, cidx % (AHEAD + 1), 1, :]
            hi, lo = (uh, ul) if b < NB else (mh, ml)
            for t in range(tiles_of(b)):
                if k == 0 and before[b, t]:
                    wait_evacuated(pe, *before[b, t])
                ps = bank[bank_of(b, t)][:, :]
                cols = slice(P * t, P * t + P)
                if is_direct(b):
                    n = SEQ if BLOCKS[b][0] == "qn" else 2 * SEQ
                    mm(ps[:, 0:n], wh[:, cols], hi[:, k, 0:n], start=k == 0, stop=False)
                    mm(ps[:, 0:n], wl[:, cols], hi[:, k, 0:n], start=False, stop=False)
                    last = mm(ps[:, 0:n], wh[:, cols], lo[:, k, 0:n], start=False, stop=k == KC - 1)
                else:
                    mm(ps, hi[:, k, cols], wh, start=k == 0, stop=False)
                    mm(ps, hi[:, k, cols], wl, start=False, stop=False)
                    last = mm(ps, lo[:, k, cols], wh, start=False, stop=k == KC - 1)
                if t == tiles_of(b) - 1:
                    last.then_inc(chunk_used, 1)
                elif k == KC - 1:
                    last.then_inc(tile_done, 1)

        def turn_tile(b, t):
            m = n_kq[b] + t
            wait_evacuated(pe, b, t)
            if BLOCKS[b][0][1] == "r" and t < 2:
                pe.wait_ge(roped, n_rope[b] + t + 1)
            if m >= 2:
                wait_turned_read(pe, m - 2)
            pe.wait_ge(mod_add, sums_by(b + 1, 4 + t))
            for hh in range(4):
                last = nc.tensor.transpose(bank[6 + m % 2][:, P * hh:P * hh + P], tmp[:, t, P * hh:P * hh + P], ident)
            last.then_inc(kq_turned, 1)

        def na_scores(g, u):
            n = 8 * g + u
            if u == 0:
                wait_evacuated(pe, 3 * g + 1, 2)
                wait_evacuated(pe, 3 * g + 1, 3)
            if n >= 2:
                pe.wait_ge(na_biased, n - 1)
            hh, qt = u // 2, u % 2
            mm(bank[4 + u % 2][:, :], qT[:, hh, P * qt:P * qt + P], kT[:, hh, :], start=True, stop=True).then_inc(na_score, 1)

        def na_turn(g, u):
            n = 8 * g + u
            pe.wait_ge(na_norm, n + 1)
            if n >= 1:
                pe.wait_ge(na_pt, n)
            for kt in range(4):
                last = nc.tensor.transpose(bank[6][:, P * kt:P * kt + P], pb[:, u % 2, P * kt:P * kt + P], ident)
            last.then_inc(na_turned, 1)

        def na_values(g, u):
            hn = 4 * g + u // 2
            pe.wait_ge(na_pt, 8 * g + u + 1)
            if u == 1:
                wait_evacuated(pe, 3 * g + 2, 2)
                wait_evacuated(pe, 3 * g + 2, 3)
                pe.wait_ge(mod_add, sums_by(3 * g + 3, 8))
            if hn:
                pe.wait_ge(na_mix, hn)
            for kt in range(4):
                last = mm(bank[7][:, 0:SEQ], vv[:, kt, P * (u // 2):P * (u // 2) + P], pT[:, (u // 2) % 2, kt, :],
                          start=kt == 0, stop=kt == 3)
            last.then_inc(na_out, 1)

        def ret_scores(g, hh):
            n = 4 * g + hh
            if hh == 0:
                pe.wait_ge(kq_dve, n_kk[6 + 4 * g] + 4)
                pe.wait_ge(kq_act, n_qq[7 + 4 * g] + 2)
            if n:
                pe.wait_ge(ret_masked, n)
            for kt in range(4):
                last = mm(bank[4 + kt // 2][:, SEQ * (kt % 2):SEQ * (kt % 2) + SEQ], kT[:, hh, P * kt:P * kt + P],
                          qT[:, hh, :], start=True, stop=True)
            last.then_inc(ret_score, 1)

        def ret_values(g, hh):
            n = 4 * g + hh
            pe.wait_ge(ret_masked, n + 1)
            if hh == 0:
                wait_evacuated(pe, 8 + 4 * g, 2)
                wait_evacuated(pe, 8 + 4 * g, 3)
            if n >= 2:
                pe.wait_ge(ret_kept, n - 1)
            for it in range(2):
                for kt in range(4):
                    last = mm(bank[6 + hh % 2][:, P * it:P * it + P], pT[:, hh % 2, kt, P * it:P * it + P],
                              vv[:, kt, P * hh:P * hh + P], start=kt == 0, stop=kt == 3)
            last.then_inc(ret_out, 1)

        def ret_turn(g):
            pe.wait_ge(ret_gated, g + 1)
            for hh in range(4):
                for it in range(2):
                    last = nc.tensor.transpose(bank[6 + hh // 2][:, SEQ * (hh % 2) + P * it:SEQ * (hh % 2) + P * it + P],
                                               pb[:, it, P * hh:P * hh + P], ident)
            last.then_inc(ret_turned, 1)

        def row_on_all(m, quad, dst):
            return mm(dst, ones[32 * quad:32 * quad + 1, :], mrow[32 * quad:32 * quad + 1, m, :], start=True, stop=True)

        def turn_tokens(k):
            if k == 0:
                pe.wait_ge(small_in, 16 * 11)
                pe.wait_ge(normed, 4)
            if k >= 4:
                pe.wait_ge(xt_dve if k % 2 else xt_act, k // 2 - 1)
            for t in range(4):
                last = nc.tensor.transpose(bank[k % 4][:, P * t:P * t + P], xin[:, t, P * k:P * k + P], ident)
            last.then_inc(x_turned, 1)

        def flip_bias(j):
            if j == 0:
                pe.wait_ge(bias_in, 16 * 16)
            else:
                pe.wait_ge(bias_ok, j)
            mm(bank[6][:, :], window[:, GRID_W:], bias_r[:, 512 * j:512 * j + 512], start=True, stop=True).then_inc(bias_pe, 1)

        pe.wait_ge(c_act, 2)
        pe.wait_ge(pool_init, 3)
        for i in range(MOD_BEFORE):
            for q in range(8):
                mod_item(i, q)
                if i and q == 1:
                    mod_sums(i - 1)
                if i == 1 and q < 6:
                    for k in range(3 * q - max(q - 4, 0), 3 * q + 3 - max(q - 3, 0)):
                        turn_tokens(k)
                if 8 * (i - 2) + q in PROJECT_AT:
                    k = PROJECT_AT.index(8 * (i - 2) + q)
                    if k == 0:
                        pe.wait_ge(xt_act, 8)
                        pe.wait_ge(xt_dve, 8)
                    project(0, k)
        mod_sums(MOD_BEFORE - 1)

        def turn_stream(cb):
            if cb:
                pe.wait_ge(ht_act, cb)
                pe.wait_ge(ht_dve, cb)
            for t in range(2):
                pe.wait_ge(h_ready, 2 * cb + (2 if cb == NO - 1 else t + 1))
                for i in range(4):
                    k = 4 * cb + i
                    bk = bank[(0 if cb == NO - 1 else 6) + i // 2]
                    last = nc.tensor.transpose(bk[:, SEQ * (i % 2) + P * t:SEQ * (i % 2) + P * t + P],
                                               h[:, t, P * k:P * k + P], ident)
            last.then_inc(h_turned, 1)

        def router_chunks(j):
            if j == 0:
                pe.wait_ge(row_act, 4)
                pe.wait_ge(a_ready, 5)
            pe.wait_ge(ht_act, j + 1)
            pe.wait_ge(ht_dve, j + 1)
            for quad in range(4):
                last = mm(bank[4][32 * quad:32 * quad + 32, 0:SEQ], wr_pad[:, 4 * j + quad, :], hTT[:, 4 * j + quad, :],
                          start=j == 0, stop=j == NO - 1)
            return last

        for b in range(NB + NO):
            for k in range(EARLY if b == 0 else 0, KC):
                project(b, k)
                prev = b - 1
                if (b, k) in MOD_SUMS:
                    n_mixed = 4 * sum(1 for nb in NA_BLOCKS if nb < b)
                    if n_mixed:
                        pe.wait_ge(na_mix, n_mixed)
                    mod_sums(MOD_SUMS[b, k])
                if prev in kq_blocks and 4 <= k < 4 + tiles_of(prev):
                    turn_tile(prev, k - 4)
                if b == 2 and 8 <= k < 14:
                    flip_bias(k - 8)
                if b in NA_BLOCKS:
                    g = NA_BLOCKS[b]
                    if 4 <= k < 12:
                        na_scores(g, k - 4)
                    if 6 <= k < 14:
                        na_turn(g, k - 6)
                    if 7 <= k < 15 and k % 2 == 0:
                        na_values(g, k - 7)
                if b in RET_BLOCKS:
                    g = RET_BLOCKS[b]
                    if k in (4, 7, 10, 13):
                        ret_scores(g, (k - 4) // 3)
                    if k in (6, 9, 12, 15):
                        ret_values(g, (k - 6) // 3)
                if prev in RET_BLOCKS and k == 8:
                    ret_turn(RET_BLOCKS[prev])
                if b > NB and k == 4:
                    turn_stream(b - NB - 1)
                if b == NB + 1 and k == 9:
                    pe.wait_ge(shift_in, 1)
                    pe.wait_ge(ht_act, 1)
                    mm(bank[6][:, 0:E], ones[:, :], shift_sum, start=True, stop=True).then_inc(shift_pe, 1)
                if b >= NB and k == 8:
                    cb = b - NB
                    if cb >= 2:
                        pe.wait_ge(row_act, cb - 1)
                    row_on_all(0, cb, bank[4 + cb % 2][:, :]).then_inc(row_bc, 1)

        for j in range(NO - 1):
            router_chunks(j)
        turn_stream(NO - 1)
        router_chunks(NO - 1).then_inc(lg_pe, 1)
        pe.wait_ge(lg_copied, 1)
        for t in range(2):
            last = mm(bank[5][:, E * t:E * t + E], lpart[:, P * t:P * t + P], stack[:, 0:E], start=True, stop=True)
        last.then_inc(r_pe, 1)
        pe.wait_ge(r_dve, 2)
        for t in range(2):
            last = nc.tensor.transpose(bank[0][0:E, P * t:P * t + P], aff[:, t, :], ident)
        last.then_inc(r_pe, 1)
        pe.wait_ge(ht_act, NO)
        pe.wait_ge(ht_dve, NO)
        for cb in range(3):
            row_on_all(1, cb, bank[m5_bank[cb]][:, :]).then_inc(row_bc, 1)
        pe.wait_ge(r_dve, 3)
        for i in range(2):
            for t in range(2):
                last = nc.tensor.transpose(bank[1][:, E * (2 * i + t):E * (2 * i + t) + E],
                                           affT[0:16, 1 + i, P * t:P * t + P], ident[0:16, 0:16])
        last.then_inc(r_pe, 1)
        pe.wait_ge(r_dve, 4)
        pe.wait_ge(late_in, 32)
        for t in range(2):
            srcs = [(ones_b, eq_b[:, 0, :])] * (t == 1) + [(tri_b, eq_b[:, t, :]), (ones_b, gt_b[:, 0, :]), (ones_b, gt_b[:, 1, :])]
            for i, (l, r) in enumerate(srcs):
                last = mm(bank[4][:, E * t:E * t + E], l[:, :], r, start=i == 0, stop=i == len(srcs) - 1)
        last.then_inc(r_pe, 1)
        pe.wait_ge(r_dve, 5)
        for t in range(2):
            srcs = [(ones_b, sel_b[:, 0, :])] * (t == 1) + [(tri_b, sel_b[:, t, :])]
            for i, (l, r) in enumerate(srcs):
                last = mm(bank[5][:, E * t:E * t + E], l[:, :], r, start=i == 0, stop=i == len(srcs) - 1)
        last.then_inc(r_pe, 1)
        pe.wait_ge(row_act, NO + 1)
        row_on_all(1, 3, bank[m5_bank[3]][:, :]).then_inc(row_bc, 1)
        def gather(g, j):
            for k in range(2 * j, 2 * j + 2):
                for t in range(2):
                    last = mm(bank[2 + j % 2][:, P * (k % 2):P * (k % 2) + P], h2n[:, t, P * k:P * k + P],
                              oh[:, t, bass.ds(g * P, P)], start=t == 0, stop=t == 1)
            last.then_inc(gathered, 1)

        def combine(g, ei, cb):
            pe.wait_ge(y_ok, g * 16 + (4 * ei + cb + 2))
            pe.wait_ge(comb_add, g * 32 + (8 * ei + max(2 * cb - 2, 1)))
            for t in range(2):
                mm((bank[cb] if t else bank[6 + cb % 2])[:, :], gcur[:, P * t:P * t + P], yy[:, cb, :],
                   start=True, stop=True).then_inc(comb, 1)

        pe.wait_ge(r_dve, 6)
        pe.wait_ge(row_act, NO + 3)
        pe.wait_ge(h2_act, 2)
        pe.sem_inc(summed, 1)
        pe.sem_inc(comb, 1)
        with pe.Fori(0, 4) as g:
            pe.wait_ge(comb_add, g * 32 + 1)
            for ei in range(4):
                if ei:
                    pe.wait_ge(comb_add, g * 32 + (8 * ei + 1))
                for m in range(2):
                    for j in range(8):
                        if ei == 0 and m == 0 and j == 0:
                            gather(g, 0)
                            gather(g, 1)
                        if ei == 0 and m == 0:
                            pe.wait_ge(xg_dve if j % 2 else xg_act, g * 4 + (j // 2 + 1))
                        i = 8 * m + j
                        s = moe_slots[i % RING]
                        pe.wait_ge(ring_full[s], g * (16 * 8) + (fills[s] + 16 * (2 * ei + i // RING + 1)))
                        w = slot_buf(s).rearrange("p (k c) -> p k c", k=2)
                        for half in range(2):
                            for kk in range(2):
                                quad = 2 * ((j + half) % 2) + kk
                                last = mm(bank[2 * m + half][32 * quad:32 * quad + 32, :],
                                          xg[:, 2 * j + kk, CAP * ei:CAP * ei + CAP],
                                          w[:, kk, 512 * half:512 * half + 512], start=j < 2, stop=j >= 6)
                        last.then_inc(moe_used, 1)
                        if ei == 0 and m == 0 and j < 6:
                            gather(g, j + 2)
                pe.wait_ge(g_ok, g * 4 + (ei + 1))
                if ei == 0:
                    pe.wait_ge(og_ok, g + 1)
                    for t in range(2):
                        last = nc.tensor.transpose(bank[5][:, SEQ + P * t:SEQ + P * t + P], oha[:, t, :], ident)
                    last.then_inc(og_pe, 1)
                    pe.wait_ge(tg_ok, g + 1)
                mm(bank[5][:, 0:SEQ], spread[:, ei, :], tg[:, :], start=True, stop=True).then_inc(g_pe, 1)
                pe.wait_ge(gu_act, g * 8 + (2 * ei + 2))
                pe.wait_ge(gu_dve, g * 8 + (2 * ei + 2))
                pe.wait_ge(hid_ok, g * 4 + (ei + 1))
                for i in range(16):
                    last = mm(bank[4][:, CAP * i:CAP * i + CAP], gup[:, i // 4, P * (i % 4):P * (i % 4) + P], stack,
                              start=True, stop=True)
                last.then_inc(summed, 1)
                pe.wait_ge(hid_ok, g * 4 + (ei + 2))
                pe.wait_ge(g_ok, g * 4 + (ei + 2))
                for cb in range(5):
                    for j in range(2 * cb, 2 * cb + 2) if cb < 4 else ():
                        s = moe_slots[(16 + j) % RING]
                        pe.wait_ge(ring_full[s], g * (16 * 8) + (fills[s] + 16 * (2 * ei + 2)))
                        w = slot_buf(s).rearrange("p (k c) -> p k c", k=4)
                        for quad in range(4):
                            last = mm(bank[cb][32 * quad:32 * quad + 32, :], hT[:, 4 * (j % 2) + quad, :],
                                      w[:, quad, :], start=j % 2 == 0, stop=j % 2 == 1)
                        last.then_inc(moe_used, 1)
                    if cb:
                        combine(g, ei, cb - 1)

    @block.scalar
    def _(act):
        a = nc.scalar.activation
        links = [0]

        def link(ins):
            links[0] += 1
            ins.then_inc(act_link, 1)
            act.wait_ge(act_link, links[0])

        for i, src in enumerate((c, c_ctx)):
            act.dma_start(cin[:, i, :], src).then_inc(cond_in, 16)
        for t in range(4):
            act.dma_start(xin[:, t, :], (x_v if t < 2 else ctx_v)[t % 2]).then_inc(tok_in[t], 16)
        act.wait_ge(pool_init, 1)
        act.dma_start(pad[0:120, 48:79], rpb[0].rearrange("h r c -> (h r) c")).then_inc(pad_in, 16)
        loads = [(small[:, 0:706], k_small), (nmc[:, :], nm), (nfc[:, :], nf),
                 (gnc[:, :], gn), (bcol[:, :, :], b_col), (dec[:, 0, :], dec_f.partition_broadcast(P)),
                 (dec[:, 1, :], dec_b.partition_broadcast(P)), (window[:, :], k_window),
                 (wr[:, :, :], w_router[0].rearrange("(k p) e -> p k e", p=P))]
        for dst, src in loads:
            act.dma_start(dst, src).then_inc(small_in, 16)
        for m in range(2):
            act.dma_start(mrow[0:P:32, m, :], b_row[m]).then_inc(small_in, 16)
        act.wait_ge(pool_init, 2)
        act.wait_ge(cond_in, 32)
        for i in range(2):
            a(csT[:, :, i], cin[:, i, :], ACT.Silu).then_inc(c_act, 1)
        act.wait_ge(pad_in, 16)
        act.dma_start(pad_dram, pad[0:120, :]).then_inc(pad_out, 16)
        for t in range(4):
            act.wait_ge(tok_in[t], 16)
            a(junk[:, :], xin[:, t, :], ACT.Square, accum_out=ss[:, t:t + 1]).then_inc(squares, 1)
            act.wait_ge(squares, t + 1)
        act.wait_ge(lg_dve, 1)
        link(a(lg[:, 1, :], lg[:, 0, :], ACT.Exp, scale=-1.0))
        a(lg[:, 2, :], lg[:, 1, :], ACT.Ln, bias=1.0).then_inc(lg_act, 1)

        def keep_tokens():
            for k in range(0, KC, 2):
                act.wait_ge(x_turned, k + 1)
                a(xnT[:, k, :], bank[k % 4][:, :], ACT.Copy).then_inc(xt_act, 1)

        def mod_part(i):
            act.wait_ge(mod_item_used, 8 * i + 4)
            if i:
                act.wait_ge(mod_small, i)
            a(part[:, 0, :], bank[4][:, :], ACT.Copy).then_inc(part_act, 1)

        def split(b, k):
            cidx = CHUNKS * b + k
            if k % 4 == 0:
                wait_item(act, ("w", b, k // 4))
            if cidx > AHEAD:
                act.wait_ge(chunk_used, cidx - AHEAD)
            n = item_at["w", b, k // 4]
            a(whl[:, cidx % (AHEAD + 1), 0, :], slot_buf(slot[n])[:, 512 * (k % 4):512 * (k % 4) + 512], ACT.Copy).then_inc(hi_split, 1)

        def evacuate(b):
            kind = BLOCKS[b][0][0]
            for t in range(0, tiles_of(b), 2):
                wait_projected(act, b, t)
                if is_direct(b):
                    if b >= 3:
                        act.wait_ge(na_score, 8)
                    if kind == "k":
                        a(kT[:, t, :], bank[bank_of(b, t)][:, :], ACT.Copy).then_inc(ev_act, 1)
                    else:
                        a(qT[:, t, :], bank[bank_of(b, t)][:, 0:SEQ], ACT.Copy, scale=SCALE).then_inc(ev_act, 1)
                    continue
                if kind in "kq":
                    dst = tmp[:, t, :]
                    i = kq_blocks.index(b)
                    if i:
                        act.wait_ge(kq_turned, n_kq[b])
                else:
                    dst = (vv if kind == "v" else gg)[:, t, :]
                    if kind == "g" and BLOCKS[b][1]:
                        act.wait_ge(ret_gated, 1)
                    if kind == "v" and b == 5:
                        act.wait_ge(na_out, 4)
                    if kind == "v" and b == 8:
                        act.wait_ge(na_out, 8)
                    if kind == "v" and b == 12:
                        act.wait_ge(ret_out, 4)
                a(dst, bank[bank_of(b, t)][:, :], ACT.Copy).then_inc(ev_act, 1)

        def load_bias(half, hh):
            if half == 0 and hh == 0:
                act.wait_ge(pad_out, 16)
            src = bass.AP(pad_dram.tensor, pad_dram.offset + (15 * hh + 5 - half) * P,
                          [[1, GRID_W], [P, 6], [1, GRID_W]])
            dst = bias_r[64 * half:64 * half + 64, 384 * hh:384 * hh + 384].rearrange("p (s c) -> p s c", s=6)
            act.dma_start(dst, src).then_inc(bias_in, 16)

        def query_tile(b, t):
            act.wait_ge(kq_turned, n_kq[b] + t + 1)
            src = bank[6 + (n_kq[b] + t) % 2][:, :].rearrange("p (h n) -> p h n", h=4)
            a(qT[:, :, P * t:P * t + P], src, ACT.Copy, scale=SCALE).then_inc(kq_act, 1)

        def na_exponent(g, u):
            n = 8 * g + u
            act.wait_ge(na_biased, n + 1)
            a(pb[:, u % 2, :], pb[:, u % 2, :], ACT.Exp, bias=nmax[:, n % 4:n % 4 + 1],
              accum_out=psumm[:, n % 4:n % 4 + 1]).then_inc(na_exp, 1)

        def na_keep(g, u):
            act.wait_ge(na_turned, 8 * g + u + 1)
            src = bank[6][:, :].rearrange("p (k n) -> p k n", k=4)
            a(pT[:, (u // 2) % 2, :, P * (u % 2):P * (u % 2) + P], src, ACT.Copy).then_inc(na_pt, 1)

        def na_mixed(g, u):
            hn = 4 * g + u // 2
            act.wait_ge(na_out, hn + 1)
            a(mixT[:, hn, :], bank[7][:, 0:SEQ], ACT.Copy).then_inc(na_mix, 1)

        def gamma_powers(n):
            if n:
                act.wait_ge(masks, n)
            else:
                act.wait_ge(lg_dve, 2)
                act.wait_ge(decay_in, 16)
            for i in range(2):
                a(gfb[:, i, :], decay[:, 640 * i:640 * i + 640], ACT.Exp,
                  scale=lg[:, 3, 8 * i + n:8 * i + n + 1]).then_inc(powers, 1)

        def ret_keep(g, hh):
            n = 4 * g + hh
            act.wait_ge(ret_out, n + 1)
            if hh == 0 and g:
                act.wait_ge(ret_turned, 1)
            src = bank[6 + hh % 2][:, 0:SEQ].rearrange("p (t e) -> p t e", t=2)
            a(pb[:, :, P * hh:P * hh + P], src, ACT.Copy).then_inc(ret_kept, 1)

        def ret_mixed(g, half):
            act.wait_ge(ret_turned, g + 1)
            hn = 8 + 4 * g + 2 * half
            a(mixT[:, hn, :], bank[6 + half][:, 0:SEQ], ACT.Copy, scale=gnc[:, hn - 8:hn - 7]).then_inc(ret_mix_a, 1)

        def ahead(cidx):
            b, k = divmod(cidx, KC)
            split(b, k)
            if b == 0:
                if k % 4 == 0:
                    act.wait_ge(a_ready, k // 4 + 1)
                    act.wait_ge(xt_dve, 8)
                link(a(xnT[:, k, SEQ:512], xnT[:, k, SEQ:512], ACT.Identity, scale=acol[:, 1, k:k + 1],
                       bias=modc[:, 0, k, 1:2]))
                act.wait_ge(u_aff, k + 1)
                a(uh[:, k, :], xnT[:, k, :], ACT.Copy).then_inc(uh_ok, 1)
            if b == NB:
                if k == 0:
                    act.wait_ge(na_mix, 8)
                if k == 8:
                    act.wait_ge(ret_mix_a, 2)
                    act.wait_ge(ret_mix_d, 2)
                if k == 12:
                    act.wait_ge(ret_mix_a, 4)
                    act.wait_ge(ret_mix_d, 4)
                act.wait_ge(chunk_used, CHUNKS * (NB - 1) + k // 2 + 1)
                a(mh[:, k, :], mixT[:, k, :], ACT.Copy).then_inc(mh_ok, 1)

        def keep_stream(cb):
            act.wait_ge(h_turned, cb + 1)
            if cb == 0:
                act.wait_ge(ml_ok, KC)
            a(hTT[:, 4 * cb:4 * cb + 2, :], bank[0 if cb == NO - 1 else 6][:, :].rearrange("p (k n) -> p k n", k=2),
              ACT.Copy).then_inc(ht_act, 1)

        mod_part(0)
        keep_tokens()
        mod_part(1)
        for cidx in range(7):
            ahead(cidx)
        mod_part(2)
        for cidx in range(7, 11):
            ahead(cidx)
        mod_part(3)
        ahead(11)
        for b in range(NB + NO):
            prev = b - 1
            for k in range(EARLY - AHEAD if b == 0 else 0, KC):
                if k == 0 and 0 <= prev < NB:
                    evacuate(prev)
                if prev in RET_BLOCKS and k == 9:
                    ret_mixed(RET_BLOCKS[prev], 0)
                    ret_mixed(RET_BLOCKS[prev], 1)
                if CHUNKS * b + k + AHEAD < CHUNKS * (NB + NO):
                    ahead(CHUNKS * b + k + AHEAD)
                if b == 1:
                    load_bias(k // 8, k % 8)
                if b == 3 and k == 1:
                    act.dma_start(decay[:, :], k_decay).then_inc(decay_in, 16)
                if prev in kq_blocks and BLOCKS[prev][0][0] == "q" and 4 <= k < 6:
                    query_tile(prev, k - 4)
                if b in NA_BLOCKS:
                    g = NA_BLOCKS[b]
                    if 4 <= k < 12:
                        na_exponent(g, k - 4)
                    if 6 <= k < 14:
                        na_keep(g, k - 6)
                    if 7 <= k < 15 and k % 2 == 0:
                        na_mixed(g, k - 7)
                if b + 1 in RET_BLOCKS and k == 12:
                    gamma_powers(4 * RET_BLOCKS[b + 1])
                if b in RET_BLOCKS:
                    g = RET_BLOCKS[b]
                    if k in (2, 5, 8):
                        gamma_powers(4 * g + 1 + (k - 2) // 3)
                    if k in (6, 9, 12, 15):
                        ret_keep(g, (k - 6) // 3)
                if prev in RET_BLOCKS and k == 2:
                    act.wait_ge(ev_dve, n_even[prev] + 1)
                    act.wait_ge(ev_act, n_even[prev] + 1)
                    a(gg[:, :, :], gg[:, :, :], ACT.Silu).then_inc(gate_act, 1)
                if b == NB and k == 2:
                    act.wait_ge(chunk_used, CHUNKS * NB)
                    for t in range(2):
                        act.dma_start(h[:, t, :], x_v[t]).then_inc(h_in, 16)
                if b == NB + 1 and k == 5:
                    act.wait_ge(ret_turned, 2)
                    act.dma_start(spread[:, :, :], k_late[:, 0:512].rearrange("p (e m) -> p e m", e=4)).then_inc(late_in, 16)
                    act.dma_start(tri[:, :], k_late[:, 512:640]).then_inc(late_in, 16)
                if b >= NB and k == 9:
                    cb = b - NB
                    act.wait_ge(row_bc, cb + 1)
                    if cb >= 2:
                        act.wait_ge(h_ready, 2 * (cb - 1))
                    a(part[:, cb % 2, :], bank[4 + cb % 2][:, :], ACT.Copy).then_inc(row_act, 1)
                if b > NB and k == 5:
                    keep_stream(b - NB - 1)
                if b > NB and k in (3, 4):
                    cb, t = b - 1 - NB, k - 3
                    act.wait_ge(h_ready, 2 * cb + t + 1)
                    a(tmp[:, t, :], h[:, t, 512 * cb:512 * cb + 512], ACT.Square,
                      accum_out=ss[:, 4 * t + cb:4 * t + cb + 1]).then_inc(h_sq, 1)
        for t in range(2):
            act.wait_ge(h_ready, 2 * NO - 1 + t)
            a(tmp[:, t, :], h[:, t, 1536:2048], ACT.Square, accum_out=ss[:, 4 * t + 3:4 * t + 4]).then_inc(h_sq, 1)
        keep_stream(NO - 1)
        act.wait_ge(rstd_ok, 2)
        a(h2n[:, 0, :], h[:, 0, :], ACT.Copy, scale=rs[:, 0:1]).then_inc(h2_act, 1)
        act.wait_ge(r_dve, 1)
        a(aff[:, :, :], aff[:, :, :], ACT.Exp).then_inc(r_act, 1)
        a(h2n[:, 1, :], h[:, 1, :], ACT.Copy, scale=rs[:, 1:2]).then_inc(h2_act, 1)
        act.wait_ge(chunk_used, CHUNKS * (NB + NO))
        for cb in range(4):
            act.wait_ge(row_bc, NO + cb + 1)
            a(m5[:, 512 * cb:512 * cb + 512], bank[m5_bank[cb]][:, :], ACT.Copy).then_inc(row_act, 1)
        act.wait_ge(r_pe, 1)
        act.dma_start(fwb[:, :], fw.partition_broadcast(P)).then_inc(fw_in, 16)

        with act.Fori(0, 4) as g:
            for j in range(0, 8, 2):
                act.wait_ge(gathered, g * 8 + (j + 1))
                for k in (2 * j, 2 * j + 1):
                    last = a(xg[:, k, :], bank[2][:, P * (k % 2):P * (k % 2) + P], ACT.Identity, scale=a2[:, k:k + 1],
                             bias=modc[:, 2, k, 0:1])
                last.then_inc(xg_act, 1)
            act.wait_ge(og_pe, g + 1)
            a(tg[:, :], bank[5][:, SEQ:2 * SEQ], ACT.Copy).then_inc(tg_ok, 1)
            for ei in range(4):
                for m in range(2):
                    act.wait_ge(moe_used, g * 96 + (24 * ei + 8 * m + 8))
                    if m == 0:
                        act.wait_ge(summed, g * 4 + (ei + 1))
                    a(gup[:, 2 * m, :], bank[2 * m][:, :], ACT.Copy).then_inc(gu_act, 1)
                act.wait_ge(summed, g * 4 + (ei + 2))
                act.wait_ge(hid_ok, g * 4 + (ei + 1))
                a(sgate[:, :, :], bank[4][:, 0:SEQ].rearrange("p (f n) -> p f n", f=FC), ACT.Silu).then_inc(silu_ok, 1)
        for i in range(8):
            cb, t = i // 2, i % 2
            act.wait_ge(comb_add, E * 8 - 8 + i + 2)
            a(ring[:, 0, 512 * t:512 * t + 512], h[:, t, 512 * cb:512 * cb + 512], ACT.Square,
              accum_out=ss[:, 4 * t + cb:4 * t + cb + 1]).then_inc(f_sq_a, 1)
            if i >= 1:
                act.wait_ge(f_sq_a, i)
        act.wait_ge(f_pre, 6)
        act.wait_ge(f_rstd, 1)
        a(h2n[:, 0, 0:1024], h2n[:, 0, 0:1024], ACT.Copy, scale=rs[:, 0:1]).then_inc(f_out_a, 1)

    @block.vector
    def _(dve):
        v = nc.vector
        links = [0]

        def link(ins):
            links[0] += 1
            ins.then_inc(dve_link, 1)
            dve.wait_ge(dve_link, links[0])

        for t in range(4):
            dve.wait_ge(squares, t + 1)
        v.tensor_scalar(rs[:, 4:8], ss[:, 0:4], 1.0 / D, EPS, ALU.mult, ALU.add).then_inc(mean_sq, 1)
        dve.wait_ge(rstd_ok, 1)
        for t in range(4):
            v.tensor_scalar(xin[:, t, :], xin[:, t, :], rs[:, t:t + 1], None, ALU.mult).then_inc(normed, 1)
        dve.wait_ge(small_in, 16 * 11)
        decs = dec[:, :, :].rearrange("p a b -> p (a b)")
        link(v.tensor_scalar(lg[:, 3, :], decs, -1.0, None, ALU.mult))
        v.tensor_tensor(lg[:, 0, :], lg[:, 3, :], decs, ALU.max).then_inc(lg_dve, 1)
        dve.wait_ge(lg_act, 1)
        link(v.tensor_scalar(lg[:, 0, :], decs, 0.0, None, ALU.min))
        v.tensor_tensor(lg[:, 3, :], lg[:, 0, :], lg[:, 2, :], ALU.subtract).then_inc(lg_dve, 1)

        def keep_tokens(k):
            dve.wait_ge(x_turned, k + 1)
            v.tensor_copy(xnT[:, k, :], bank[k % 4][:, :]).then_inc(xt_dve, 1)

        def mask_bias(j):
            dve.wait_ge(bias_pe, j + 1)
            bv = bias[:, :, :, :].rearrange("p h s c -> p (h s) c")
            v.tensor_tensor(bv[:, 8 * j:8 * j + 8, :], bank[6][:, :].rearrange("p (s c) -> p s c", s=8),
                            window[:, 0:GRID_W].unsqueeze(1).broadcast_to([P, 8, GRID_W]), ALU.add).then_inc(bias_ok, 1)

        def mod_part(i):
            dve.wait_ge(mod_item_used, 8 * i + 8)
            if i:
                dve.wait_ge(mod_small, i)
            v.tensor_copy(part[:, 1, :], bank[5][:, :]).then_inc(part_dve, 1)

        def mod_finish(i):
            dve.wait_ge(mod_small, i + 1)
            m = i // 2
            if i < MOD_BEFORE:
                for mi in range(2):
                    last = v.tensor_tensor(modc[:, mi, 4 * i:4 * i + 4, :],
                                           bank[7][:, 8 * mi:8 * mi + 8].rearrange("p (k c) -> p k c", c=2),
                                           bcol[:, mi, 4 * i:4 * i + 4].unsqueeze(2).broadcast_to([P, 4, 2]), ALU.add)
                last.then_inc(mod_add, 1)
            elif m in (2, 5):
                for half in range(2):
                    r = 32 * (2 * (i % 2) + half)
                    last = v.tensor_tensor(mrow[r:r + 1, m // 3, :], mrow[r:r + 1, m // 3, :], bank[7][r:r + 1, :], ALU.add)
                last.then_inc(mod_add, 1)
            else:
                mi = m - 1
                k0 = 8 * (i % 2)
                v.tensor_tensor(modc[:, mi, k0:k0 + 8, :], bank[7][:, 0:16].rearrange("p (k c) -> p k c", c=2),
                                bcol[:, mi, k0:k0 + 8].unsqueeze(2).broadcast_to([P, 8, 2]), ALU.add).then_inc(mod_add, 1)

        def mod_multiply(i, k):
            if k == 0:
                dve.wait_ge(mod_small, i)
            if k % 2 == 0:
                wait_item(dve, ("mod", i, k // 2))
            n = item_at["mod", i, k // 2]
            w = slot_buf(slot[n])[:, 1024 * (k % 2):1024 * (k % 2) + 1024]
            acc = part[:, :, :].rearrange("p a n -> p (a n)")
            if k == 0:
                ins = v.tensor_scalar(acc, w, csT[:, k, 0:1], None, ALU.mult)
            else:
                dve.wait_ge(mod_mac, KC * (i - MOD_BEFORE) + k)
                ins = v.scalar_tensor_tensor(out=acc, in0=w, scalar=csT[:, k, 0:1], in1=acc, op0=ALU.mult, op1=ALU.add)
            ins.then_inc(mod_mac, 1)

        def norm_scale(i):
            dve.wait_ge(mod_add, i + 1)
            ks = slice(4 * i, 4 * i + 4)
            for c in range(2):
                last = v.scalar_tensor_tensor(out=acol[:, c, ks], in0=modc[:, 1, ks, c], scalar=1.0,
                                              in1=nmc[:, ks], op0=ALU.add, op1=ALU.mult)
            last.then_inc(a_ready, 1)
            dve.wait_ge(a_ready, i + 1)

        def split(b, k):
            cidx = CHUNKS * b + k
            n = item_at["w", b, k // 4]
            dve.wait_ge(hi_split, cidx + 1)
            v.tensor_tensor(whl[:, cidx % (AHEAD + 1), 1, :], slot_buf(slot[n])[:, 512 * (k % 4):512 * (k % 4) + 512],
                            whl[:, cidx % (AHEAD + 1), 0, :].bitcast(F32), ALU.subtract).then_inc(lo_split, 1)

        def evacuate(b):
            kind = BLOCKS[b][0][0]
            for t in range(1, tiles_of(b), 2):
                wait_projected(dve, b, t)
                if is_direct(b):
                    if b >= 3:
                        dve.wait_ge(na_score, 8)
                    if kind == "k":
                        v.tensor_copy(kT[:, t, :], bank[bank_of(b, t)][:, :]).then_inc(ev_dve, 1)
                    else:
                        v.tensor_scalar(qT[:, t, :], bank[bank_of(b, t)][:, 0:SEQ], SCALE, None, ALU.mult).then_inc(ev_dve, 1)
                    continue
                if kind in "kq":
                    dst = tmp[:, t, :]
                    if kq_blocks.index(b):
                        dve.wait_ge(kq_turned, n_kq[b])
                else:
                    dst = (vv if kind == "v" else gg)[:, t, :]
                    if kind == "v" and b == 5:
                        dve.wait_ge(na_out, 4)
                    if kind == "v" and b == 8:
                        dve.wait_ge(na_out, 8)
                    if kind == "v" and b == 12:
                        dve.wait_ge(ret_out, 4)
                v.tensor_copy(dst, bank[bank_of(b, t)][:, :]).then_inc(ev_dve, 1)

        def key_tile(b, t):
            dve.wait_ge(kq_turned, n_kq[b] + t + 1)
            src = bank[6 + (n_kq[b] + t) % 2][:, :].rearrange("p (h n) -> p h n", h=4)
            v.tensor_copy(kT[:, :, P * t:P * t + P], src).then_inc(kq_dve, 1)

        def na_bias(g, u):
            n = 8 * g + u
            hn, qt = 4 * g + u // 2, u % 2
            if n == 0:
                dve.wait_ge(bias_ok, 6)
            dve.wait_ge(na_score, n + 1)
            if n >= 2:
                dve.wait_ge(na_turned, n - 1)
            s = 2 * (1 - qt)
            v.tensor_tensor(pb[:, u % 2, 0:SEQ], bank[4 + u % 2][:, 0:SEQ],
                            bias[:, hn, s:s + 4, :].rearrange("p a b -> p (a b)"), ALU.add)
            link(v.tensor_copy(pb[:, u % 2, SEQ:512], bank[4 + u % 2][:, SEQ:512]))
            link(v.tensor_reduce(prec[:, n % 4:n % 4 + 1], pb[:, u % 2, :], AX_X, ALU.max))
            v.tensor_scalar(nmax[:, n % 4:n % 4 + 1], prec[:, n % 4:n % 4 + 1], -1.0, None, ALU.mult).then_inc(na_biased, 1)

        def na_normal(g, u):
            n = 8 * g + u
            dve.wait_ge(na_exp, n + 1)
            link(v.reciprocal(prec[:, n % 4:n % 4 + 1], psumm[:, n % 4:n % 4 + 1]))
            v.tensor_scalar(pb[:, u % 2, :], pb[:, u % 2, :], prec[:, n % 4:n % 4 + 1], None, ALU.mult).then_inc(na_norm, 1)

        def ret_mask(g, hh):
            n = 4 * g + hh
            dve.wait_ge(ret_score, n + 1)
            dve.wait_ge(masks, n + 1)
            if n >= 2:
                dve.wait_ge(ret_out, n - 1)
            for kt in range(4):
                o = P * (1 - kt % 2)
                last = v.tensor_tensor(pT[:, hh % 2, kt, :], bank[4 + kt // 2][:, SEQ * (kt % 2):SEQ * (kt % 2) + SEQ],
                                       wmask[:, hh % 2, kt // 2, o:o + SEQ], ALU.mult)
            last.then_inc(ret_masked, 1)

        def head_moments(g, hh):
            dve.wait_ge(ret_kept, 4 * g + hh + 1)
            for it in range(2):
                last = v.bn_stats(bst[:, 2 * hh + it, :], pb[:, it, P * hh:P * hh + P])
            last.then_inc(ret_stats, 1)

        def ret_moments(g):
            head_moments(g, 3)
            dve.wait_ge(ret_stats, 4 * g + 4)
            for i in range(8):
                last = v.bn_aggr(mv[:, i, :], bst[:, i, :])
            link(last)
            v.tensor_scalar(rg[:, :], mv[:, :, 1], EPS, None, ALU.add).then_inc(ret_var, 1)

        def ret_normal(g):
            dve.wait_ge(ret_rstd, g + 1)
            for hh in range(4):
                for it in range(2):
                    i = 2 * hh + it
                    last = v.tensor_scalar(pb[:, it, P * hh:P * hh + P], pb[:, it, P * hh:P * hh + P], mv[:, i, 0:1],
                                           rg[:, i:i + 1], ALU.subtract, ALU.mult)
            link(last)

        def ret_gate(g):
            dve.wait_ge(gate_act, g + 1)
            v.tensor_tensor(pb[:, :, :], pb[:, :, :], gg[:, :, :], ALU.mult).then_inc(ret_gated, 1)

        def ret_mixed(g, half):
            dve.wait_ge(ret_turned, g + 1)
            dve.wait_ge(ret_mix_a, 2 * g + half + 1)
            hn = 9 + 4 * g + 2 * half
            v.tensor_scalar(mixT[:, hn, :], bank[6 + half][:, SEQ:512], gnc[:, hn - 8:hn - 7], None, ALU.mult).then_inc(ret_mix_d, 1)

        def router_weights():
            link(v.scalar_tensor_tensor(out=a2[:, :], in0=modc[:, 3, :, 0], scalar=1.0, in1=nfc[:, :], op0=ALU.add, op1=ALU.mult))
            link(v.tensor_tensor(wrb, wr[:, :, :], modc[:, 2, :, 0:1].broadcast_to([P, KC, E]), ALU.mult))
            v.tensor_reduce(shift_sum, wrb.rearrange("p k e -> p e k"), AX_X, ALU.add).then_inc(shift_in, 1)
            dve.wait_ge(masks, 8)
            link(v.memset(wr_pad[:, :, :], 0.0))
            link(v.tensor_tensor(wr_pad[:, :, 0:E], wr[:, :, :], a2[:, :].unsqueeze(2).broadcast_to([P, KC, E]), ALU.mult))
            dve.wait_ge(shift_pe, 1)
            v.tensor_copy(shift_lg, bank[6][:, 0:E])
            v.memset(ones_b[:, :], 1.0).then_inc(a_ready, 1)

        def keep_stream(cb):
            dve.wait_ge(h_turned, cb + 1)
            src = bank[1 if cb == NO - 1 else 7][:, :].rearrange("p (k n) -> p k n", k=2)
            v.tensor_copy(hTT[:, 4 * cb + 2:4 * cb + 4, :], src).then_inc(ht_dve, 1)

        def residual(cb):
            b = NB + cb
            dve.wait_ge(row_act, cb + 1)
            if cb == 0:
                dve.wait_ge(h_in, 32)
            for t in range(2):
                wait_projected(dve, b, t)
                link(v.tensor_tensor(tmp[:, 2 + t, :], bank[bank_of(b, t)][:, :], part[:, cb % 2, :], ALU.mult))
                v.tensor_tensor(h[:, t, 512 * cb:512 * cb + 512], h[:, t, 512 * cb:512 * cb + 512], tmp[:, 2 + t, :],
                                ALU.add).then_inc(h_ready, 1)

        def ahead(cidx):
            b, k = divmod(cidx, KC)
            if b == 0:
                v.tensor_scalar(xnT[:, k, 0:SEQ], xnT[:, k, 0:SEQ], acol[:, 0, k:k + 1], modc[:, 0, k, 0:1],
                                ALU.mult, ALU.add).then_inc(u_aff, 1)
            split(b, k)
            if b == 0:
                dve.wait_ge(uh_ok, k + 1)
                v.tensor_tensor(ul[:, k, :], xnT[:, k, :], uh[:, k, :].bitcast(F32), ALU.subtract).then_inc(ul_ok, 1)
            if b == NB:
                dve.wait_ge(mh_ok, k + 1)
                dve.wait_ge(chunk_used, CHUNKS * (NB - 1) + KC // 2 + k // 2 + 1)
                v.tensor_tensor(ml[:, k, :], mixT[:, k, :], mh[:, k, :].bitcast(F32), ALU.subtract).then_inc(ml_ok, 1)

        mod_part(0)
        keep_tokens(1)
        mod_finish(0)
        norm_scale(0)
        for k in range(3, KC, 2):
            keep_tokens(k)
        dve.wait_ge(xt_act, 8)
        dve.wait_ge(xt_dve, 8)
        for cidx in range(3):
            ahead(cidx)
        mod_part(1)
        ahead(3)
        mod_finish(1)
        norm_scale(1)
        for cidx in range(4, 8):
            ahead(cidx)
        mod_part(2)
        mod_finish(2)
        norm_scale(2)
        for cidx in range(8, EARLY):
            ahead(cidx)
        mod_part(3)
        mod_finish(3)
        norm_scale(3)
        for b in range(NB + NO):
            prev = b - 1
            for k in range(EARLY - AHEAD if b == 0 else 0, KC):
                if k == 0 and 0 <= prev < NB:
                    evacuate(prev)
                if prev in RET_BLOCKS and k == 9:
                    ret_mixed(RET_BLOCKS[prev], 0)
                    ret_mixed(RET_BLOCKS[prev], 1)
                if b in NA_BLOCKS:
                    g = NA_BLOCKS[b]
                    if 4 <= k < 12:
                        na_bias(g, k - 4)
                    if 5 <= k < 13:
                        na_normal(g, k - 5)
                if CHUNKS * b + k + AHEAD < CHUNKS * (NB + NO):
                    ahead(CHUNKS * b + k + AHEAD)
                if k == 2 and prev >= NB:
                    residual(prev - NB)
                if b == NB + 1 and k == 8:
                    router_weights()
                if b > NB and k == 5:
                    keep_stream(b - NB - 1)
                if (b, k) in MOD_FINISH:
                    mod_finish(MOD_FINISH[b, k])
                if (b, k) in MOD_AT:
                    mod_multiply(*MOD_AT[b, k])
                if b == 2 and 8 <= k < 14:
                    mask_bias(k - 8)
                if prev in kq_blocks and BLOCKS[prev][0][0] == "k" and 4 <= k < 8:
                    key_tile(prev, k - 4)
                if b in RET_BLOCKS:
                    g = RET_BLOCKS[b]
                    if k in (5, 8, 11, 14):
                        ret_mask(g, (k - 5) // 3)
                    if k in (9, 12, 15):
                        head_moments(g, (k - 9) // 3)
                if prev in RET_BLOCKS and k == 3:
                    ret_moments(RET_BLOCKS[prev])
                if prev in RET_BLOCKS and k == 5:
                    ret_normal(RET_BLOCKS[prev])
                if prev in RET_BLOCKS and k == 7:
                    ret_gate(RET_BLOCKS[prev])
        residual(NO - 1)
        dve.wait_ge(h_sq, 2 * NO)
        link(v.tensor_reduce(rs[:, 2:4], ss[:, :].rearrange("p (t c) -> p t c", t=2), AX_X, ALU.add))
        v.tensor_scalar(rs[:, 4:6], rs[:, 2:4], 1.0 / D, EPS, ALU.mult, ALU.add).then_inc(mean_sq, 1)
        keep_stream(NO - 1)
        dve.wait_ge(lg_pe, 1)
        v.tensor_copy(lpart[:, :], bank[4][:, 0:SEQ]).then_inc(lg_copied, 1)
        dve.wait_ge(late_in, 32)
        v.tensor_copy(tri_b[:, :], tri[:, :])
        dve.wait_ge(rstd_ok, 2)
        dve.wait_ge(r_pe, 1)
        for t in range(2):
            last = v.scalar_tensor_tensor(out=aff[:, t, :], in0=bank[5][:, E * t:E * t + E], scalar=rs[:, t:t + 1],
                                          in1=shift_lg, op0=ALU.mult, op1=ALU.add)
        link(last)
        link(v.tensor_reduce(rmax, aff[:, :, :], AX_X, ALU.max))
        v.tensor_tensor(aff[:, :, :], aff[:, :, :], rmax.unsqueeze(2).broadcast_to([P, 2, E]),
                        ALU.subtract).then_inc(r_dve, 1)
        dve.wait_ge(r_act, 1)
        link(v.tensor_reduce(rsum, aff[:, :, :], AX_X, ALU.add))
        link(v.reciprocal(rmax, rsum))
        v.tensor_tensor(aff[:, :, :], aff[:, :, :], rmax.unsqueeze(2).broadcast_to([P, 2, E]), ALU.mult).then_inc(r_dve, 1)
        dve.wait_ge(r_pe, 2)
        link(v.tensor_copy(affT[0:E, 0, :], bank[0][0:E, 0:SEQ]))
        for i in range(4):
            left = affT[0:E, 3 if i else 0, :]
            link(v.max(top8[0:E, 8 * i:8 * i + 8], left))
            if i < 3:
                link(v.match_replace(affT[0:E, 3, :], top8[0:E, 8 * i:8 * i + 8], left, -1.0))
        v.tensor_scalar(affT[0:E, 1, :], affT[0:E, 0, :], top8[0:E, 31:32], None, ALU.is_gt)
        v.tensor_scalar(affT[0:E, 2, :], affT[0:E, 0, :], top8[0:E, 31:32], None, ALU.is_equal).then_inc(r_dve, 1)
        dve.wait_ge(r_pe, 3)
        gts_ps = bank[1][:, 0:4 * E].rearrange("p (i t e) -> p i t e", i=2, t=2)
        v.tensor_copy(gt_b, gts_ps[:, 0])
        v.tensor_copy(gts, gts_ps[:, 0])
        v.tensor_copy(slotm, gts_ps[:, 1])
        v.tensor_copy(eq_b, gts_ps[:, 1]).then_inc(r_dve, 1)
        dve.wait_ge(r_dve, 4)
        dve.wait_ge(r_pe, 4)
        ps_t = bank[4][:, 0:2 * E].rearrange("p (t e) -> p t e", t=2)
        link(v.tensor_scalar(sels, ps_t, float(CAP), None, ALU.is_le))
        link(v.tensor_tensor(sels, sels, slotm, ALU.mult))
        link(v.tensor_tensor(sels, sels, gts, ALU.add))
        v.tensor_copy(sel_b, sels).then_inc(r_dve, 1)
        dve.wait_ge(r_pe, 5)
        ps_s = bank[5][:, 0:2 * E].rearrange("p (t e) -> p t e", t=2)
        link(v.tensor_tensor(slotm, ps_s, sels, ALU.mult))
        for t in range(2):
            last = v.tensor_tensor(oh[:, t, :].rearrange("p (e s) -> p e s", e=E),
                                   slotm[:, t, :].unsqueeze(2).broadcast_to([P, E, CAP]),
                                   slots.unsqueeze(1).broadcast_to([P, E, CAP]), ALU.is_equal)
        last.then_inc(r_dve, 1)

        for credit in (y_ok, g_ok, hid_ok, comb_add):
            dve.sem_inc(credit, 1)
        with dve.Fori(0, 4) as g:
            for j in range(1, 8, 2):
                dve.wait_ge(gathered, g * 8 + (j + 1))
                for k in (2 * j, 2 * j + 1):
                    last = v.tensor_scalar(xg[:, k, :], bank[3][:, P * (k % 2):P * (k % 2) + P], a2[:, k:k + 1],
                                           modc[:, 2, k, 0:1], ALU.mult, ALU.add)
                last.then_inc(xg_dve, 1)
            for t in range(2):
                last = v.tensor_tensor(oha[:, t, :].rearrange("p (e s) -> p e s", e=4),
                                       oh[:, t, bass.ds(g * P, P)].rearrange("p (e s) -> p e s", e=4),
                                       aff[:, t, bass.ds(g * 4, 4)].unsqueeze(2).broadcast_to([P, 4, CAP]), ALU.mult)
            last.then_inc(og_ok, 1)
            for ei in range(4):
                for m in range(2):
                    dve.wait_ge(moe_used, g * 96 + (24 * ei + 8 * m + 8))
                    if m == 0:
                        dve.wait_ge(summed, g * 4 + (ei + 1))
                    v.tensor_copy(gup[:, 2 * m + 1, :], bank[2 * m + 1][:, :]).then_inc(gu_dve, 1)
                dve.wait_ge(g_pe, g * 4 + (ei + 1))
                dve.wait_ge(comb, g * 32 + (8 * ei + 1))
                v.tensor_copy(gcur[:, :], bank[5][:, 0:SEQ]).then_inc(g_ok, 1)
                dve.wait_ge(silu_ok, g * 4 + (ei + 1))
                v.tensor_tensor(hT[:, :, :], sgate[:, :, :], bank[4][:, SEQ:512].rearrange("p (f n) -> p f n", f=FC),
                                ALU.mult).then_inc(hid_ok, 1)
                for cb in range(5):
                    if cb < 4:
                        dve.wait_ge(moe_used, g * 96 + (24 * ei + 2 * cb + 18))
                        v.tensor_tensor(yy[:, cb, :], bank[cb][:, :], m5[:, 512 * cb:512 * cb + 512], ALU.mult).then_inc(y_ok, 1)
                    for t in range(2) if cb else ():
                        i = 2 * (cb - 1) + t
                        dve.wait_ge(comb, g * 32 + (8 * ei + i + 2))
                        hs = h[:, t, 512 * (cb - 1):512 * cb]
                        ps = bank[cb - 1] if t else bank[6 + (cb - 1) % 2]
                        v.tensor_tensor(hs, hs, ps[:, :], ALU.add).then_inc(comb_add, 1)
        dve.wait_ge(comb_add, E * 8 + 1)
        dve.wait_ge(fw_in, 16)
        dve.wait_ge(gathered, 32)
        for t in range(2):
            link(v.tensor_tensor(h2n[:, t, 1536:2048], h[:, t, 1536:2048], fwb[:, 1536:2048], ALU.mult))
        dve.wait_ge(f_sq_a, 8)
        link(v.tensor_reduce(rs[:, 2:4], ss[:, :].rearrange("p (t c) -> p t c", t=2), AX_X, ALU.add))
        v.tensor_scalar(rs[:, 4:6], rs[:, 2:4], 1.0 / D, EPS, ALU.mult, ALU.add).then_inc(f_mean, 1)
        dve.wait_ge(f_pre, 6)
        dve.wait_ge(f_rstd, 1)
        for t, half in ((1, 0), (1, 1), (0, 1)):
            cs = slice(1024 * half, 1024 * half + 1024)
            v.tensor_scalar(h2n[:, t, cs], h2n[:, t, cs], rs[:, t:t + 1], None, ALU.mult).then_inc(f_out, 1)

    @block.gpsimd
    def _(pool):
        gp = nc.gpsimd
        links = [0]

        def link(ins):
            links[0] += 1
            ins.then_inc(pool_link, 1)
            pool.wait_ge(pool_link, links[0])

        gp.memset(pad[:, :], 0.0).then_inc(pool_init, 1)
        gp.memset(csT[:, :, :], 0.0).then_inc(pool_init, 1)
        gp.memset(ones[:, :], 1.0).then_inc(pool_init, 1)
        link(gp.memset(mhalf[:, :], -0.5))
        pool.wait_ge(mean_sq, 1)
        gp.tensor_tensor(rs[:, 0:4], rs[:, 4:8], mhalf[:, 0:4], ALU.pow).then_inc(rstd_ok, 1)

        def rope(b, t):
            wait_evacuated(pool, b, t)
            if n_rope[b] + t:
                pool.wait_ge(roped, n_rope[b] + t)
            tv = tmp[:, t, :].rearrange("p (h a f e) -> p h a f e", h=4, a=2, f=2)
            rv = ropet[:, :].rearrange("p (h a f e) -> p h a f e", h=4, a=2, f=2)
            sv = sinT[:, t, :].rearrange("p (a f e) -> p a f e", a=2, f=2)
            for f in range(2):
                swapped = gp.tensor_tensor(rv[:, :, :, f], tv[:, :, :, 1 - f],
                                           sv[:, :, f].unsqueeze(1).broadcast_to([P, 4, 2, 32]), ALU.mult)
            link(swapped)
            link(gp.tensor_tensor(tmp[:, t, :].rearrange("p (h d) -> p h d", h=4),
                                  tmp[:, t, :].rearrange("p (h d) -> p h d", h=4),
                                  cosT[:, t, :].unsqueeze(1).broadcast_to([P, 4, P]), ALU.mult))
            gp.tensor_tensor(tmp[:, t, :], tmp[:, t, :], ropet[:, :], ALU.add).then_inc(roped, 1)

        def mask(n):
            pool.wait_ge(powers, 2 * n + 2)
            if n:
                pool.wait_ge(masks, n)
            if n >= 2:
                pool.wait_ge(ret_masked, n - 1)
            if n == 0:
                pool.wait_ge(na_biased, 16)
                pool.wait_ge(decay_in, 16)
            link(gp.tensor_tensor(wmask[:, n % 2, 1, :], gfb[:, 0, 256:640], gfb[:, 1, 0:384], ALU.add))
            gp.tensor_tensor(gfb[:, 0, 0:384], gfb[:, 0, 0:384], decay[:, 1280:1664], ALU.mult)
            link(gp.tensor_tensor(gfb[:, 1, 256:640], gfb[:, 1, 256:640], decay[:, 1664:2048], ALU.mult))
            gp.tensor_tensor(wmask[:, n % 2, 0, :], gfb[:, 0, 0:384], gfb[:, 1, 256:640], ALU.add).then_inc(masks, 1)

        for b in range(NB):
            if b in kq_blocks and BLOCKS[b][0][1] == "r":
                rope(b, 0)
                rope(b, 1)
            if b + 1 in RET_BLOCKS:
                mask(4 * RET_BLOCKS[b + 1])
            if b in RET_BLOCKS:
                for hh in range(1, 4):
                    mask(4 * RET_BLOCKS[b] + hh)
                pool.wait_ge(ret_var, RET_BLOCKS[b] + 1)
                gp.tensor_tensor(rg[:, :], rg[:, :], mhalf[:, :], ALU.pow).then_inc(ret_rstd, 1)
        pool.wait_ge(mean_sq, 2)
        gp.tensor_tensor(rs[:, 0:2], rs[:, 4:6], mhalf[:, 0:2], ALU.pow).then_inc(rstd_ok, 1)
        pool.wait_ge(fw_in, 16)
        pool.wait_ge(gathered, 32)
        for i in range(6):
            cb, t = i // 2, i % 2
            pool.wait_ge(comb_add, E * 8 - 8 + i + 2)
            cs = slice(512 * cb, 512 * cb + 512)
            gp.tensor_tensor(h2n[:, t, cs], h[:, t, cs], fwb[:, cs], ALU.mult).then_inc(f_pre, 1)
        pool.wait_ge(f_mean, 1)
        gp.tensor_tensor(rs[:, 0:2], rs[:, 4:6], mhalf[:, 0:2], ALU.pow).then_inc(f_rstd, 1)

    es.close()


def kernel(**inputs):
    import concourse.bacc as bacc
    from concourse.bass_utils import run_bass_kernel_spmd

    def cols(a):
        a = np.asarray(a)
        return np.ascontiguousarray(a.reshape(-1, P).T)

    consts = host_constants()
    b_mod = np.asarray(inputs["b_mod"]).reshape(6, D)
    arrays = {
        "x": inputs["x"], "c": cols(inputs["c"]), "ctx": inputs["ctx"], "c_ctx": cols(inputs["c_ctx"]),
        "w_mod": inputs["w_mod"],
        "b_col": np.ascontiguousarray(b_mod[[0, 1, 3, 4]].reshape(4, KC, P).transpose(2, 0, 1)),
        "b_row": np.ascontiguousarray(b_mod[[2, 5]].reshape(2, 4, 512)),
        "nm": cols(inputs["norm_mix_w"]), "nf": cols(inputs["norm_ffn_w"]), "w_in": inputs["w_in"],
        "rpb": inputs["na_rpb"], "dec_f": np.asarray(inputs["ret_decay_fwd"]).reshape(8),
        "dec_b": np.asarray(inputs["ret_decay_bwd"]).reshape(8), "gn": cols(inputs["ret_gn_w"]),
        "w_out": inputs["w_out"], "w_router": inputs["w_router"], "w_gate": inputs["w_gate"],
        "w_up": inputs["w_up"], "w_down": inputs["w_down"], "fw": inputs["final_norm_w"],
        "k_decay": consts["decay"], "k_small": consts["small"], "k_window": consts["window"], "k_late": consts["late"],
    }
    nc = bacc.Bacc("TRN2", target_bir_lowering=False, num_devices=1)
    feeds, args = {}, []
    for name, a in arrays.items():
        a = np.ascontiguousarray(a)
        feeds[f"in_{name}"] = a
        args.append(nc.dram_tensor(f"in_{name}", a.shape, mybir.dt.from_np(a.dtype), kind="ExternalInput").ap())
    args.append(nc.dram_tensor("out_0", (1, SEQ, D), F32, kind="ExternalOutput").ap())
    build(nc, *args)
    r = run_bass_kernel_spmd(nc, [feeds], core_ids=[0])
    return r.results[0]["out_0"]
```
